# Optimizing a Trainium2 kernel written in Bass

```python
import math
import jax, jax.numpy as jnp
from jax import lax
import numpy as np

D_MODEL = 1024
BATCH = 1
SEQ = 2048
DEPTH = 1
DEC_BATCH = 8
DEC_SEQ = 16
PAST_LEN = 128

CHUNK = 64
D_MIX = D_MODEL
D_POOL = D_MIX // 2
D_SSM = D_MIX - D_POOL
POOL_WINDOWS = (2, 4, 8, 16)
N_POOL_GROUPS = len(POOL_WINDOWS)
POOL_GW = D_POOL // N_POOL_GROUPS
POOL_HIST = max(POOL_WINDOWS) - 1
SSM_GROUP = 16
N_SSM_GROUPS = D_SSM // SSM_GROUP
SSM_STATE = 64
DT_MIN = 1e-3
DT_MAX = 1e-1
N_MEM = 256
MEM_HEADS = 4
MEM_HEAD_DIM = D_MODEL // MEM_HEADS
D_FF = 4 * D_MODEL
EPS = 1e-6

kernel_name = "hybrid_pool_s5_stream_encoder_step"

def rmsnorm(x, g):
    xf = x.astype(jnp.float32)
    y = xf * lax.rsqrt(jnp.mean(xf * xf, axis=-1, keepdims=True) + EPS)
    return (y * g.astype(jnp.float32)).astype(x.dtype)

def pool_mixer(u, hist, pos0, w_pool, pool_scale):
    S = u.shape[1]
    u_ext = jnp.concatenate([hist.astype(u.dtype), u], axis=1)
    uf = u_ext.astype(jnp.float32)
    c = jnp.pad(jnp.cumsum(uf, axis=1), ((0, 0), (1, 0), (0, 0)))
    cnt_pos = pos0 + jnp.arange(S) + 1
    cur = uf[:, POOL_HIST:]
    outs = []
    for g, w in enumerate(POOL_WINDOWS):
        sl = slice(g * POOL_GW, (g + 1) * POOL_GW)
        cg = c[..., sl]
        hi = POOL_HIST + 1
        win_sum = cg[:, hi:hi + S] - cg[:, hi - w:hi - w + S]
        cnt = jnp.minimum(cnt_pos, w).astype(jnp.float32)[None, :, None]
        pooled = win_sum / cnt - cur[..., sl]
        outs.append(jnp.einsum('bsc,cd->bsd', pooled, w_pool[g].astype(jnp.float32)))
    y = jnp.concatenate(outs, axis=-1) * pool_scale.astype(jnp.float32)
    return y.astype(u.dtype), u_ext[:, -POOL_HIST:]

def s5_mixer(u, h0_re, h0_im, a_re, a_im, b_re, b_im, c_re, c_im, d_skip, log_dt, w_glu, b_glu):
    B, S, _ = u.shape
    f32 = jnp.float32
    uf = u.astype(f32).reshape(B, S, N_SSM_GROUPS, SSM_GROUP)
    A = lax.complex(a_re.astype(f32), a_im.astype(f32))
    dt = jnp.exp(log_dt.astype(f32))[:, None]
    a_bar = jnp.exp(A * dt)
    b_bar = ((a_bar - 1.0) / A)[..., None] * lax.complex(b_re.astype(f32), b_im.astype(f32))
    bu = jnp.einsum('gph,bsgh->bsgp', b_bar, uf.astype(jnp.complex64))
    h0 = lax.complex(h0_re.astype(f32), h0_im.astype(f32))
    bu = bu.at[:, 0].add(a_bar * h0)
    a_seq = jnp.broadcast_to(a_bar, bu.shape)

    def combine(left, right):
        al, bl = left
        ar, br = right
        return ar * al, ar * bl + br

    _, h = lax.associative_scan(combine, (a_seq, bu), axis=1)
    cm = lax.complex(c_re.astype(f32), c_im.astype(f32))
    y = jnp.einsum('ghp,bsgp->bsgh', cm, h).real + d_skip.astype(f32) * uf
    y = jax.nn.gelu(y.reshape(B, S, D_SSM))
    y = y * jax.nn.sigmoid(y @ w_glu.astype(f32) + b_glu.astype(f32))
    h_last = h[:, -1]
    return y.astype(u.dtype), h_last.real.astype(h0_re.dtype), h_last.imag.astype(h0_im.dtype)

def mem_kv(mem, g_mem, w_k, w_v):
    B = mem.shape[0]
    m = rmsnorm(mem, g_mem)
    k = (m @ w_k).reshape(B, N_MEM, MEM_HEADS, MEM_HEAD_DIM)
    v = (m @ w_v).reshape(B, N_MEM, MEM_HEADS, MEM_HEAD_DIM)
    return k, v

def cross_attn(h, k, v, w_q, w_o):
    B, S, _ = h.shape
    q = (h @ w_q).reshape(B, S, MEM_HEADS, MEM_HEAD_DIM)
    s = jnp.einsum('bshd,bnhd->bhsn', q, k).astype(jnp.float32) * (MEM_HEAD_DIM ** -0.5)
    p = jax.nn.softmax(s, axis=-1).astype(v.dtype)
    o = jnp.einsum('bhsn,bnhd->bshd', p, v).reshape(B, S, MEM_HEADS * MEM_HEAD_DIM)
    return o @ w_o

def layer(x, pool_hist, pos0, h0_re, h0_im, mk, mv,
          g_mix, w_in, w_pool, pool_scale, a_re, a_im, b_re, b_im, c_re, c_im, d_skip, log_dt,
          w_glu, b_glu, w_out, g_xattn, w_q, w_o, g_mlp, w_up, w_down):
    h = rmsnorm(x, g_mix)
    z = h @ w_in
    y_pool, new_hist = pool_mixer(z[..., :D_POOL], pool_hist, pos0, w_pool, pool_scale)
    y_ssm, hr, hi = s5_mixer(z[..., D_POOL:], h0_re, h0_im, a_re, a_im, b_re, b_im,
                             c_re, c_im, d_skip, log_dt, w_glu, b_glu)
    x = x + jnp.concatenate([y_pool, y_ssm], axis=-1) @ w_out
    x = x + cross_attn(rmsnorm(x, g_xattn), mk, mv, w_q, w_o)
    hm = rmsnorm(x, g_mlp)
    x = x + jnp.square(jax.nn.relu(hm @ w_up)) @ w_down
    return x, new_hist, hr, hi

def setup_inputs(seed: int = 0) -> dict:
    key = jax.random.key(seed)
    ks = iter(jax.random.split(key, 48))
    f32 = jnp.float32

    def nrm(shape, scale):
        return jax.random.normal(next(ks), shape, f32) * scale

    L, G, P, H = DEPTH, N_SSM_GROUPS, SSM_STATE, SSM_GROUP
    n = jnp.arange(P, dtype=f32)
    inp = {
        "x_prompt": nrm((BATCH, SEQ, D_MODEL), 1.0),
        "x_sample": nrm((DEC_BATCH, DEC_SEQ, D_MODEL), 1.0),
        "cache_mem_k": nrm((L, DEC_BATCH, N_MEM, MEM_HEADS, MEM_HEAD_DIM), 1.0),
        "cache_mem_v": nrm((L, DEC_BATCH, N_MEM, MEM_HEADS, MEM_HEAD_DIM), 1.0),
        "state_pool": nrm((L, DEC_BATCH, POOL_HIST, D_POOL), 1.0),
        "state_ssm_re": nrm((L, DEC_BATCH, G, P), 0.1),
        "state_ssm_im": nrm((L, DEC_BATCH, G, P), 0.1),
        "mem_prompt": nrm((BATCH, N_MEM, D_MODEL), 1.0),
        "g_mix": 1.0 + nrm((L, D_MODEL), 0.02),
        "w_in": nrm((L, D_MODEL, D_MIX), D_MODEL ** -0.5),
        "w_pool": nrm((L, N_POOL_GROUPS, POOL_GW, POOL_GW), POOL_GW ** -0.5),
        "pool_scale": 1.0 + nrm((L, D_POOL), 0.1),
        "ssm_a_re": -0.5 + nrm((L, G, P), 0.01),
        "ssm_a_im": math.pi * n + nrm((L, G, P), 0.01),
        "ssm_b_re": nrm((L, G, P, H), (2.0 * H) ** -0.5),
        "ssm_b_im": nrm((L, G, P, H), (2.0 * H) ** -0.5),
        "ssm_c_re": nrm((L, G, H, P), (2.0 * P) ** -0.5 * 4.0),
        "ssm_c_im": nrm((L, G, H, P), (2.0 * P) ** -0.5 * 4.0),
        "ssm_d": nrm((L, G, H), 1.0),
        "ssm_log_dt": jax.random.uniform(next(ks), (L, G), f32, math.log(DT_MIN), math.log(DT_MAX)),
        "w_glu": nrm((L, D_SSM, D_SSM), D_SSM ** -0.5),
        "b_glu": nrm((L, D_SSM), 0.02),
        "w_out": nrm((L, D_MIX, D_MODEL), D_MIX ** -0.5),
        "g_xattn": 1.0 + nrm((L, D_MODEL), 0.02),
        "g_mem": 1.0 + nrm((L, D_MODEL), 0.02),
        "w_q": nrm((L, D_MODEL, MEM_HEADS * MEM_HEAD_DIM), D_MODEL ** -0.5),
        "w_k": nrm((L, D_MODEL, MEM_HEADS * MEM_HEAD_DIM), D_MODEL ** -0.5),
        "w_v": nrm((L, D_MODEL, MEM_HEADS * MEM_HEAD_DIM), D_MODEL ** -0.5),
        "w_o": nrm((L, MEM_HEADS * MEM_HEAD_DIM, D_MODEL), D_MODEL ** -0.5),
        "g_mlp": 1.0 + nrm((L, D_MODEL), 0.02),
        "w_up": nrm((L, D_MODEL, D_FF), D_MODEL ** -0.5),
        "w_down": nrm((L, D_FF, D_MODEL), D_FF ** -0.5),
        "g_final": 1.0 + nrm((D_MODEL,), 0.02),
    }
    return inp

def reference(x_prompt, x_sample, cache_mem_k, cache_mem_v, state_pool, state_ssm_re, state_ssm_im,
              mem_prompt, g_mix, w_in, w_pool, pool_scale, ssm_a_re, ssm_a_im, ssm_b_re, ssm_b_im,
              ssm_c_re, ssm_c_im, ssm_d, ssm_log_dt, w_glu, b_glu, w_out, g_xattn, g_mem,
              w_q, w_k, w_v, w_o, g_mlp, w_up, w_down, g_final):
    xp, xs = x_prompt, x_sample
    Bp = x_prompt.shape[0]
    mk_p, mv_p, pool_p, sre_p, sim_p = [], [], [], [], []
    pool_s, sre_s, sim_s = [], [], []
    for l in range(DEPTH):
        wts = (g_mix[l], w_in[l], w_pool[l], pool_scale[l], ssm_a_re[l], ssm_a_im[l],
               ssm_b_re[l], ssm_b_im[l], ssm_c_re[l], ssm_c_im[l], ssm_d[l], ssm_log_dt[l],
               w_glu[l], b_glu[l], w_out[l], g_xattn[l], w_q[l], w_o[l], g_mlp[l], w_up[l], w_down[l])
        mk, mv = mem_kv(mem_prompt, g_mem[l], w_k[l], w_v[l])
        hist0 = jnp.zeros((Bp, POOL_HIST, D_POOL), xp.dtype)
        zs = jnp.zeros((Bp, N_SSM_GROUPS, SSM_STATE), state_ssm_re.dtype)
        xp, ph, hr, hi = layer(xp, hist0, 0, zs, zs, mk, mv, *wts)
        mk_p.append(mk); mv_p.append(mv); pool_p.append(ph); sre_p.append(hr); sim_p.append(hi)
        xs, sh, shr, shi = layer(xs, state_pool[l], PAST_LEN, state_ssm_re[l], state_ssm_im[l],
                                 cache_mem_k[l], cache_mem_v[l], *wts)
        pool_s.append(sh); sre_s.append(shr); sim_s.append(shi)
    y_prompt = rmsnorm(xp, g_final)
    y_sample = rmsnorm(xs, g_final)
    return (y_prompt, y_sample,
            jnp.stack(mk_p), jnp.stack(mv_p), jnp.stack(pool_p), jnp.stack(sre_p), jnp.stack(sim_p),
            jnp.stack(pool_s), jnp.stack(sre_s), jnp.stack(sim_s))


_drawn_inputs = setup_inputs


def setup_inputs(seed=0):
    import zlib

    import numpy as np

    out = dict(_drawn_inputs(seed))
    spreads = {}
    factors = {'g_mix': 2.961,
     'ssm_a_re': 3.982,
     'b_glu': 8.0,
     'g_xattn': 8.0,
     'g_mem': 2.847,
     'g_mlp': 3.555,
     'g_final': 2.76}
    for name, (base, spread) in spreads.items():
        noise = np.random.default_rng([zlib.crc32(name.encode()), seed]).standard_normal(out[name].shape)
        drawn = base * np.exp(spread * noise) if base else spread * noise
        out[name] = __import__('jax').numpy.asarray(drawn.astype(out[name].dtype))
    for name, factor in factors.items():
        out[name] = (out[name] * factor).astype(out[name].dtype)
    return out
```

```python
import math
from contextlib import ExitStack

import concourse.bass as bass
from concourse import mybir

F32 = mybir.dt.float32
F32R = mybir.dt.float32r
I32 = mybir.dt.int32
ALU = mybir.AluOpType
ACT = mybir.ActivationFunctionType
AX_X = mybir.AxisListType.X

P = 128
D = 1024
KD = D // P
SEQ = 2048
STREAMS = 8
STEP = 16
CH = SEQ // STEP
NC = CH + STREAMS
TILES = STEP + 1
DP = D // 2
GROUPS = 32
SG = 16
SS = 64
PAIRS = GROUPS // 2
HIST = 15
MEM = 256
HEADS = 4
HD = D // HEADS
FF = 4 * D
EPS = 1e-6
BT = 4
LN2_HI = 0.693359375
LN2_LO = math.log(2.0) - LN2_HI
TWO_PI_A = 6.28125
TWO_PI_B = 0.001934051513671875
TWO_PI_C = 2 * math.pi - TWO_PI_A - TWO_PI_B
MAGIC = 1.5 * 2.0 ** 23


class Room:

    def __init__(self, nc, ctx, tag):
        self.nc, self.ctx, self.tag = nc, ctx, tag

    def sb(self, name, shape, dt=F32):
        return self.ctx.enter_context(self.nc.sbuf_tensor(f"{self.tag}_{name}", shape, dt))

    def ps(self, name, shape, dt=F32):
        return self.ctx.enter_context(self.nc.psum_tensor(f"{self.tag}_ps_{name}", shape, dt))


class Semaphores:

    def __init__(self, nc):
        self.nc, self.held = nc, []

    def __enter__(self):
        return self

    def __exit__(self, *error):
        return False

    def new(self, name):
        self.held.append(self.nc.alloc_semaphore(name=name))
        return self.held[-1]

    def clear(self):
        self.nc.clear_and_free_semaphores(self.held)
        self.nc.all_engine_barrier()
        self.held = []


def product3(nc, out, w_hi, w_lo, x_hi, x_lo, first, last):
    nc.tensor.matmul(out, w_hi, x_hi, start=first, stop=False)
    nc.tensor.matmul(out, w_hi, x_lo, start=False, stop=False)
    return nc.tensor.matmul(out, w_lo, x_hi, start=False, stop=last)


def identity_matrix(nc, pool, ident, filled, done):
    nc.gpsimd.memset(ident[:], 0.0).then_inc(filled, 1)
    pool.wait_ge(filled, 1)
    nc.gpsimd.affine_select(out=ident[:], in_=ident[:], compare_op=ALU.not_equal, fill=1.0, base=0,
                            pattern=[[-1, P]], channel_multiplier=1).then_inc(done, 1)


def memory_and_tables(nc, outer, io, scr):
    sem = lambda n: outer.new("s1_" + n)
    with ExitStack() as ctx:
        room = Room(nc, ctx, "s1")
        sb, ps = room.sb, room.ps
        ident = sb("ident", [P, P])
        memx = sb("memx", [P, 2, D])
        memn = sb("memn", [P, 2, D])
        memT = sb("memT", [P, KD, MEM])
        kv = sb("kv", [P, 2, 2, D])
        kT = sb("kT", [P, KD, MEM])
        g_mem = sb("g_mem", [P, KD])
        wring = sb("wring", [P, 4, D])
        pn = sb("pn", [P, P])
        ldt = sb("ldt", [P, 2])
        pt = sb("pt", [P, P])
        braw = sb("braw", [P, 2, PAIRS, SG])
        cnat = sb("cnat", [P, 2, 2, P])
        ct = sb("ct", [P, 2, PAIRS, SG])
        bbar = sb("bbar", [P, 2, PAIRS, SG])
        powers = sb("powers", [P, 2, PAIRS, STEP + 1])
        small = sb("small", [P, 32, PAIRS])
        smalli = sb("smalli", [P, PAIRS], I32)
        stat = sb("stat", [P, 8])
        expo = sb("expo", [P, 1])
        inj = sb("inj", [P, 2, PAIRS, STEP, SG])
        outm = sb("outm", [P, 2, PAIRS, STEP + 1, SG])
        work = sb("work", [P, 2, PAIRS, STEP + 1, SG])
        injT = sb("injT", [P, 2, 4, P])
        taps = sb("taps", [SG, 2, 2, STEP, SG])
        acc = ps("acc", [P, 4, 512])
        tr = ps("tr", [P, 4, 512])

        ldt_in, ldt_ok = sem("ldt_in"), sem("ldt")
        ident0, ident_ok, mem_in, par_in, gm_in = (sem(n) for n in ("ident0", "ident", "mem_in", "par_in", "gm_in"))
        w_in, w_free = [sem(f"w_in{i}") for i in range(4)], sem("w_free")
        cleared, sumsq, var, rstd, memn_ok = (sem(n) for n in ("cleared", "sumsq", "var", "rstd", "memn"))
        memT_tr, memT_ok, kv_ok, kT_tr, kT_ok = (sem(n) for n in ("memT_tr", "memT", "kv", "kT_tr", "kT"))
        par_tr, par_ok, ang_ok, sin_ok = (sem(n) for n in ("par_tr", "par", "ang", "sin"))
        c_tr, c_ok, inj_ok, outm_ok = (sem(n) for n in ("c_tr", "c_ok", "inj", "outm"))
        injT_tr, injT_ok, tap_mm, tap_ok, tap_st = (sem(n) for n in ("injT_tr", "injT", "tap_mm", "tap", "tap_st"))
        injT_st = [sem(f"injT_st{i}") for i in range(2)]
        chain, stored = sem("chain"), sem("stored")

        def weight_slice(n):
            w = io["w_k"] if n < KD else io["w_v"]
            return w[0].rearrange("(k p) n -> k p n", p=P)[n % KD]

        with nc.Block() as block:

            @block.sync
            def _(sp):
                sp.wait_ge(cleared, 1)
                sp.dma_start(pn[0:PAIRS, :], io["ssm_a_re"][0].rearrange("(q t) s -> q (t s)", t=2)).then_inc(par_in, 16)
                sp.dma_start(pn[32:32 + PAIRS, :], io["ssm_a_im"][0].rearrange("(q t) s -> q (t s)", t=2)).then_inc(par_in, 16)
                sp.dma_start(ldt[64:64 + PAIRS, :], io["ssm_log_dt"][0].rearrange("(q t) -> q t", t=2)).then_inc(ldt_in, 16)
                for t in range(2):
                    sp.dma_start(memx[:, t], io["mem_prompt"][0, t * P:(t + 1) * P]).then_inc(mem_in, 16)
                for part, name in enumerate(("ssm_c_re", "ssm_c_im")):
                    c = io[name][0].rearrange("(x q t) h s -> x q h t s", x=2, t=2)
                    for x in range(2):
                        for q in range(8):
                            sp.dma_start(cnat[q * SG:(q + 1) * SG, part, x].rearrange("h (t s) -> h t s", t=2),
                                         c[x, q]).then_inc(par_in, 16)
                for part, name in enumerate(("ssm_b_re", "ssm_b_im")):
                    sp.dma_start(braw[:, part], io[name][0].rearrange("(q t) s h -> (t s) q h", t=2)).then_inc(par_in, 16)
                sp.dma_start(g_mem[:], io["g_mem"][0].rearrange("(k p) -> p k", p=P), allow_slow_non_contiguous=True).then_inc(gm_in, 16)
                for n in range(2 * KD):
                    if n >= 4:
                        sp.wait_ge(w_free, n - 3)
                    sp.dma_start(wring[:, n % 4], weight_slice(n)).then_inc(w_in[n % 4], 16)
                for m, name in enumerate(("new_mem_k", "new_mem_v")):
                    sp.wait_ge(kv_ok, 4 * (m + 1))
                    sp.dma_start(io[name].rearrange("l b (t p) h e -> p (l b t) (h e)", p=P), kv[:, m]).then_inc(stored, 16)
                sp.dma_start(scr["v"], kv[:, 1]).then_inc(stored, 16)
                sp.wait_ge(kT_ok, KD)
                sp.dma_start(scr["kT"], kT[:]).then_inc(stored, 16)
                sp.wait_ge(outm_ok, 1)
                sp.dma_start(scr["pow16"], powers[:, :, :, STEP], allow_slow_non_contiguous=True).then_inc(stored, 16)
                sp.dma_start(scr["outm"], outm[:]).then_inc(stored, 16)
                for n in range(PAIRS):
                    sp.wait_ge(injT_ok, n + 1)
                    sp.dma_start(scr["injT"][:, n], injT[:, n % 2]).then_inc(injT_st[n % 2], 16)
                for n in range(GROUPS // 4):
                    sp.wait_ge(tap_ok, 2 * (n + 1))
                    sp.dma_start(scr["taps"][:, 4 * n:4 * n + 4], taps[:].rearrange("h a b k c -> h (a b) k c")).then_inc(tap_st, 16)
                sp.wait_ge(stored, 6 * 16)
                for i in range(2):
                    sp.wait_ge(injT_st[i], PAIRS // 2 * 16)
                sp.wait_ge(tap_st, GROUPS // 4 * 16)

            @block.gpsimd
            def _(pool):
                nc.gpsimd.memset(expo[:], -0.5)
                identity_matrix(nc, pool, ident, ident0, ident_ok)
                for t in range(2):
                    pool.wait_ge(var, t + 1)
                    nc.gpsimd.tensor_tensor(stat[:, 4 + t:5 + t], stat[:, 2 + t:3 + t], expo[:], ALU.pow).then_inc(rstd, 1)

            @block.scalar
            def _(act):
                for t in range(2):
                    act.wait_ge(mem_in, 32)
                    nc.scalar.activation(memn[:, t], memx[:, t], ACT.Square, accum_out=stat[:, t:t + 1]).then_inc(sumsq, 1)
                act.wait_ge(gm_in, 16)
                for k in range(KD):
                    act.wait_ge(memT_tr, k // 2 + 1)
                    src = tr[:, k // 2].rearrange("p (a n) -> p a n", a=2)[:, k % 2]
                    nc.scalar.activation(memT[:, k], src, ACT.Copy, scale=g_mem[:, k:k + 1]).then_inc(memT_ok, 1)
                act.wait_ge(ang_ok, 1)
                nc.scalar.activation(small[:, 12], small[:, 10], ACT.Sin).then_inc(sin_ok, 1)
                nc.scalar.activation(small[:, 13], small[:, 11], ACT.Sin).then_inc(sin_ok, 1)
                for m in range(2):
                    act.wait_ge(w_free, (m + 1) * KD)
                    for t in range(2):
                        for h in range(2):
                            nc.scalar.activation(kv[:, m, t, h * 512:(h + 1) * 512], acc[:, 2 * t + h], ACT.Copy).then_inc(kv_ok, 1)
                for k in range(KD):
                    act.wait_ge(kT_tr, k // 2 + 1)
                    src = acc[:, k // 2].rearrange("p (a n) -> p a n", a=2)[:, k % 2]
                    nc.scalar.activation(kT[:, k], src, ACT.Copy).then_inc(kT_ok, 1)
                for n in range(PAIRS):
                    act.wait_ge(injT_tr, n + 1)
                    if n >= 2:
                        act.wait_ge(injT_st[n % 2], 16 * (n // 2))
                    nc.scalar.activation(injT[:, n % 2], tr[:, n % 4].rearrange("p (a n) -> p a n", a=4), ACT.Copy).then_inc(injT_ok, 1)
                for n in range(GROUPS // 4):
                    if n >= 1:
                        act.wait_ge(tap_st, 16 * n)
                    act.wait_ge(tap_mm, n + 1)
                    for t in range(2):
                        b = 2 * (n % 2) + t
                        nc.scalar.activation(taps[:, :, t], acc[0:SG, b].rearrange("h (a k c) -> h a k c", a=2, c=SG),
                                             ACT.Copy).then_inc(tap_ok, 1)

            @block.vector
            def _(dve):
                links = [0]

                def then(*instructions):
                    for ins in instructions:
                        ins.then_inc(chain, 1)
                    links[0] += len(instructions)
                    dve.wait_ge(chain, links[0])

                tt, ts, stt = nc.vector.tensor_tensor, nc.vector.tensor_scalar, nc.vector.scalar_tensor_tensor
                nc.vector.memset(pn[:], 0.0).then_inc(cleared, 1)
                dve.wait_ge(ldt_in, 16)
                dve.wait_ge(cleared, 1)
                for t in range(2):
                    ins = nc.vector.tensor_copy(pn[64:64 + PAIRS, t * SS:(t + 1) * SS],
                                                ldt[64:64 + PAIRS, t:t + 1].to_broadcast([PAIRS, SS]))
                ins.then_inc(ldt_ok, 1)
                for t in range(2):
                    dve.wait_ge(sumsq, t + 1)
                    ts(stat[:, 2 + t:3 + t], stat[:, t:t + 1], 1.0 / D, EPS, ALU.mult, ALU.add).then_inc(var, 1)
                for t in range(2):
                    dve.wait_ge(rstd, t + 1)
                    ts(memn[:, t], memx[:, t], stat[:, 4 + t:5 + t], None, ALU.mult).then_inc(memn_ok, 1)
                dve.wait_ge(par_tr, 1)
                then(nc.vector.tensor_copy(pt[:], acc[:, 3, 0:P]))
                a_re, a_im, log_dt = pt[:, 0:PAIRS], pt[:, 32:32 + PAIRS], pt[:, 64:64 + PAIRS]
                S = lambda n: small[:, n]

                def exp_parts(x):
                    then(ts(S(0), x, 88.0, -87.0, ALU.min, ALU.max))
                    then(ts(S(1), S(0), 1.0 / math.log(2.0), MAGIC, ALU.mult, ALU.add))
                    then(ts(S(1), S(1), -MAGIC, None, ALU.add))
                    then(stt(S(0), S(1), -LN2_HI, S(0), ALU.mult, ALU.add))
                    then(stt(S(0), S(1), -LN2_LO, S(0), ALU.mult, ALU.add))
                    then(ts(smalli[:], S(1), 127.0, None, ALU.add))
                    then(ts(small[:, 2].bitcast(I32), smalli[:], 23, None, ALU.logical_shift_left))
                    then(ts(S(3), S(0), 1.0 / math.factorial(8), None, ALU.mult))
                    for n in range(7, 0, -1):
                        then(stt(S(3), S(3), 1.0 / math.factorial(n), S(0), ALU.add, ALU.mult))

                exp_parts(log_dt)
                then(stt(S(4), S(3), 1.0, S(2), ALU.add, ALU.mult))
                then(tt(S(5), a_re, S(4), ALU.mult), tt(S(6), a_im, S(4), ALU.mult))
                then(ts(S(7), S(6), 1.0 / (2 * math.pi), MAGIC, ALU.mult, ALU.add))
                then(ts(S(7), S(7), -MAGIC, None, ALU.add))
                then(stt(S(8), S(7), -TWO_PI_A, S(6), ALU.mult, ALU.add))
                then(stt(S(8), S(7), -TWO_PI_B, S(8), ALU.mult, ALU.add))
                then(stt(S(8), S(7), -TWO_PI_C, S(8), ALU.mult, ALU.add))
                then(ts(S(10), S(8), 0.5, math.pi / 2, ALU.mult, ALU.min))
                then(ts(S(10), S(10), -math.pi / 2, None, ALU.max))
                then(stt(S(9), S(10), -1.0, S(10), ALU.mult, ALU.max))
                then(ts(S(11), S(9), -1.0, math.pi / 2, ALU.mult, ALU.add))
                dve.sem_inc(ang_ok, 1)
                exp_parts(S(5))
                then(tt(S(15), S(2), S(3), ALU.mult), ts(S(16), S(2), -1.0, None, ALU.add))
                then(tt(S(15), S(15), S(16), ALU.add))
                dve.wait_ge(sin_ok, 2)
                then(stt(S(17), S(12), -2.0, S(12), ALU.mult, ALU.mult), stt(S(18), S(12), 2.0, S(13), ALU.mult, ALU.mult))
                then(ts(S(19), S(17), 1.0, None, ALU.add), ts(S(20), S(15), 1.0, None, ALU.add))
                then(tt(S(21), S(15), S(19), ALU.mult), tt(S(22), S(20), S(18), ALU.mult))
                then(tt(S(21), S(21), S(17), ALU.add))
                pw = lambda part, k: powers[:, part, :, k]
                then(nc.vector.memset(pw(0, 0), 1.0), nc.vector.memset(pw(1, 0), 0.0),
                     ts(pw(0, 1), S(21), 1.0, None, ALU.add), ts(pw(1, 1), S(22), 1.0, None, ALU.mult))
                then(tt(S(23), a_re, a_re, ALU.mult), tt(S(24), a_im, a_im, ALU.mult))
                then(tt(S(23), S(23), S(24), ALU.add))
                then(nc.vector.reciprocal(S(23), S(23)))
                then(tt(S(24), S(21), a_re, ALU.mult), tt(S(25), S(22), a_im, ALU.mult),
                     tt(S(26), S(22), a_re, ALU.mult), tt(S(27), S(21), a_im, ALU.mult))
                then(tt(S(24), S(24), S(25), ALU.add), tt(S(26), S(26), S(27), ALU.subtract))
                then(tt(S(28), S(24), S(23), ALU.mult), tt(S(29), S(26), S(23), ALU.mult))

                def times(out, x, y, flip=1.0):
                    shape = x[0].shape
                    size = 1
                    for s in shape[1:]:
                        size *= s

                    def like(flat):
                        if len(shape) == 2:
                            return flat
                        if len(shape) == 3:
                            return flat.rearrange("p (a b) -> p a b", a=shape[1])
                        return flat.rearrange("p (a b c) -> p a b c", a=shape[1], b=shape[2])
                    scratch = work[:].rearrange("p r a b c -> p (r a b c)")
                    t0, t1 = like(scratch[:, 0:size]), like(scratch[:, size:2 * size])
                    then(tt(t0, x[0], y[0], ALU.mult), tt(t1, x[1], y[1], ALU.mult))
                    then(tt(out[0], t0, t1, ALU.subtract))
                    then(tt(t0, x[0], y[1], ALU.mult), tt(t1, x[1], y[0], ALU.mult))
                    if flip == 1.0:
                        then(tt(out[1], t0, t1, ALU.add))
                    else:
                        flat = lambda v: v.rearrange("p a b c -> p (a b c)") if len(shape) == 4 else v
                        then(stt(flat(out[1]), flat(t0), -1.0, flat(t1), ALU.mult, ALU.subtract))

                k = 1
                while k < STEP:
                    y = [powers[:, part, :, k:k + 1].to_broadcast([P, PAIRS, k]) for part in range(2)]
                    times([powers[:, part, :, k + 1:2 * k + 1] for part in range(2)],
                          [powers[:, part, :, 1:k + 1] for part in range(2)], y)
                    k *= 2
                dve.wait_ge(par_in, 36 * 16)
                f = [S(28 + part).unsqueeze(2).to_broadcast([P, PAIRS, SG]) for part in range(2)]
                times([bbar[:, part] for part in range(2)], [braw[:, part] for part in range(2)], f)
                dve.wait_ge(c_tr, 1)
                then(*(nc.vector.tensor_copy(ct[:, part, 8 * x:8 * x + 8], tr[:, 2 * part + x, 0:P].rearrange("p (q h) -> p q h", h=SG))
                       for part in range(2) for x in range(2)))
                bb = [bbar[:, part].unsqueeze(2).to_broadcast([P, PAIRS, STEP, SG]) for part in range(2)]
                pr = [bass.AP(tensor=powers, offset=part * PAIRS * (STEP + 1) + STEP - 1,
                              ap=[[2 * PAIRS * (STEP + 1), P], [STEP + 1, PAIRS], [-1, STEP], [0, SG]]) for part in range(2)]
                times([inj[:, part] for part in range(2)], pr, bb)
                dve.sem_inc(inj_ok, 1)
                cc = [ct[:, part].unsqueeze(2).to_broadcast([P, PAIRS, STEP + 1, SG]) for part in range(2)]
                pf = [powers[:, part].unsqueeze(3).to_broadcast([P, PAIRS, STEP + 1, SG]) for part in range(2)]
                times([outm[:, part] for part in range(2)], pf, cc, flip=-1.0)
                dve.sem_inc(outm_ok, 1)

            @block.tensor
            def _(pe):
                pe.wait_ge(ident_ok, 1)
                for k in range(KD):
                    for t in range(2):
                        pe.wait_ge(memn_ok, t + 1)
                        ins = nc.tensor.transpose(tr[:, k // 2, (k % 2) * MEM + t * P:(k % 2) * MEM + (t + 1) * P],
                                                  memn[:, t, k * P:(k + 1) * P], ident[:])
                    if k % 2:
                        ins.then_inc(memT_tr, 1)
                pe.wait_ge(par_in, 36 * 16)
                pe.wait_ge(ldt_ok, 1)
                nc.tensor.transpose(acc[:, 3, 0:P], pn[:], ident[:]).then_inc(par_tr, 1)
                pe.wait_ge(memT_ok, KD)
                for part in range(2):
                    for x in range(2):
                        ins = nc.tensor.transpose(tr[:, 2 * part + x, 0:P], cnat[:, part, x], ident[:])
                ins.then_inc(c_tr, 1)
                pe.wait_ge(ang_ok, 1)
                for m in range(2):
                    if m:
                        pe.wait_ge(kv_ok, 4)
                    for k in range(KD):
                        n = m * KD + k
                        pe.wait_ge(w_in[n % 4], 16 * (n // 4 + 1))
                        for t in range(2):
                            for h in range(2):
                                ins = nc.tensor.matmul(acc[:, 2 * t + h], memT[:, k, t * P:(t + 1) * P],
                                                       wring[:, n % 4, h * 512:(h + 1) * 512], start=k == 0, stop=k == KD - 1)
                        ins.then_inc(w_free, 1)
                pe.wait_ge(kv_ok, 8)
                for k in range(KD):
                    for t in range(2):
                        ins = nc.tensor.transpose(acc[:, k // 2, (k % 2) * MEM + t * P:(k % 2) * MEM + (t + 1) * P],
                                                  kv[:, 0, t, k * P:(k + 1) * P], ident[:])
                    if k % 2:
                        ins.then_inc(kT_tr, 1)
                pe.wait_ge(inj_ok, 1)
                for n in range(PAIRS):
                    if n >= 4:
                        pe.wait_ge(injT_ok, n - 3)
                    for part in range(2):
                        for jh in range(2):
                            ins = nc.tensor.transpose(tr[:, n % 4, (2 * part + jh) * P:(2 * part + jh + 1) * P],
                                                      inj[:, part, n, 8 * jh:8 * jh + 8].rearrange("p j h -> p (j h)"), ident[:])
                    ins.then_inc(injT_tr, 1)
                pe.wait_ge(outm_ok, 1)
                pe.wait_ge(kT_ok, KD)
                for n in range(GROUPS // 4):
                    if n >= 2:
                        pe.wait_ge(tap_ok, 2 * (n - 1))
                    for a in range(2):
                        for t in range(2):
                            for part in range(2):
                                q = 2 * n + a
                                rows = slice(t * SS, (t + 1) * SS)
                                ins = nc.tensor.matmul(acc[0:SG, 2 * (n % 2) + t, a * 256:(a + 1) * 256], bbar[rows, part, q],
                                                       outm[rows, part, q, 0:STEP].rearrange("p k h -> p (k h)"),
                                                       start=part == 0, stop=part == 1)
                    ins.then_inc(tap_mm, 1)


def first_input_projection(nc, outer, io, scr):
    sem = lambda n: outer.new("s2_" + n)
    with ExitStack() as ctx:
        room = Room(nc, ctx, "s2")
        sb, ps = room.sb, room.ps
        ident = sb("ident", [P, P])
        expo = sb("expo", [P, 1])
        g = sb("g", [P, KD])
        raw = sb("raw", [P, 2, D])
        w_hi, w_lo = sb("w_hi", [P, KD, D], F32R), sb("w_lo", [P, KD, D], F32R)
        x = sb("x", [P, 3, D])
        junk = sb("junk", [P, D])
        stat = sb("stat", [P, 3, TILES])
        h = sb("h", [P, 2, 2, BT, KD, P], F32R)
        zst = sb("zst", [P, 2, BT * P])
        acc = ps("acc", [P, 4, 512])
        tr = ps("tr", [P, 2, 2, 512])

        ident0, ident_ok, g_in = sem("ident0"), sem("ident"), sem("g_in")
        raw_in, raw_used, hi_ok = [sem(f"raw_in{i}") for i in range(2)], sem("w_lo"), sem("w_hi")
        x_in = [sem(f"x_in{i}") for i in range(3)]
        sumsq, var, rstd, xn_ok = sem("sumsq"), sem("var"), sem("rstd"), sem("xn")
        tr_ok, th_ok, tl_ok = sem("tr"), sem("th"), sem("tl")
        z_mm, z_ok, z_st = sem("z_mm"), sem("z"), [sem(f"z_st{i}") for i in range(2)]

        BLOCKS = TILES // BT + 1

        def tiles_of(b):
            return range(BT * b, min(BT * b + BT, TILES))

        with nc.Block() as block:

            @block.sync
            def _(sp):
                xp = io["x_prompt"][0].rearrange("(c j) d -> j c d", j=STEP)
                xs = io["x_sample"].rearrange("b j d -> j b d")
                w = io["w_in"][0].rearrange("(k p) n -> k p n", p=P)

                def load_x(t):
                    if t >= 3:
                        sp.wait_ge(tr_ok, t - 2)
                    sp.dma_start(x[:, t % 3], xp[t] if t < STEP else xs).then_inc(x_in[t % 3], 16)

                sp.dma_start(g[:], io["g_mix"][0].rearrange("(k p) -> p k", p=P), allow_slow_non_contiguous=True).then_inc(g_in, 16)
                for t in range(3):
                    load_x(t)
                for k in range(KD):
                    if k >= 2:
                        sp.wait_ge(raw_used, k - 1)
                    sp.dma_start(raw[:, k % 2], w[k]).then_inc(raw_in[k % 2], 16)
                    if k % 2:
                        load_x(k // 2 + 3)
                load_x(7)
                for b in range(BLOCKS):
                    for m in range(KD):
                        n = b * KD + m
                        sp.wait_ge(z_ok, n + 1)
                        if b < BLOCKS - 1:
                            dst = scr["z"][m][:, BT * b:BT * b + BT, 0:CH]
                            src = zst[:, n % 2].rearrange("p (j c) -> p j c", j=BT)
                        else:
                            dst = scr["z"][m][:, :, CH:NC]
                            src = zst[:, n % 2, 0:P].rearrange("p (j b) -> p j b", b=STREAMS)
                        sp.dma_start(dst, src).then_inc(z_st[n % 2], 16)
                        if m % 2 and b < BLOCKS - 2 and BT * (b + 2) + m // 2 < TILES:
                            load_x(BT * (b + 2) + m // 2)
                for i in range(2):
                    sp.wait_ge(z_st[i], BLOCKS * KD // 2 * 16)

            @block.gpsimd
            def _(pool):
                nc.gpsimd.memset(expo[:], -0.5)
                identity_matrix(nc, pool, ident, ident0, ident_ok)
                for t in range(TILES):
                    pool.wait_ge(var, t + 1)
                    nc.gpsimd.tensor_tensor(stat[:, 2, t:t + 1], stat[:, 1, t:t + 1], expo[:], ALU.pow).then_inc(rstd, 1)

            @block.scalar
            def _(act):
                def square(t):
                    act.wait_ge(x_in[t % 3], 16 * (t // 3 + 1))
                    if t:
                        act.wait_ge(sumsq, t)
                    nc.scalar.activation(junk[:], x[:, t % 3], ACT.Square, accum_out=stat[:, 0, t:t + 1]).then_inc(sumsq, 1)

                def upper_half(t):
                    b, j = divmod(t, BT)
                    act.wait_ge(tr_ok, t + 1)
                    if b >= 2:
                        act.wait_ge(z_mm, (b - 1) * KD)
                    for a in range(2):
                        nc.scalar.activation(h[:, b % 2, 0, j, 4 * a:4 * a + 4].rearrange("p k n -> p (k n)"), tr[:, t % 2, a],
                                             ACT.Copy).then_inc(th_ok, 1)

                square(0)
                square(1)
                act.wait_ge(g_in, 16)
                for k in range(KD):
                    act.wait_ge(raw_in[k % 2], 16 * (k // 2 + 1))
                    nc.scalar.activation(w_hi[:, k], raw[:, k % 2], ACT.Copy, scale=g[:, k:k + 1]).then_inc(hi_ok, 1)
                    if k % 2:
                        upper_half(k // 2)
                        square(k // 2 + 2)
                for b in range(BLOCKS):
                    for m in range(KD):
                        n = b * KD + m
                        act.wait_ge(z_mm, n + 1)
                        if n >= 2:
                            act.wait_ge(z_st[n % 2], 16 * (n // 2))
                        wide = P * len(tiles_of(b))
                        nc.scalar.activation(zst[:, n % 2, 0:wide], acc[:, n % 4, 0:wide], ACT.Copy).then_inc(z_ok, 1)
                        t = BT * (b + 1) + m // 2
                        if m % 2 and t < TILES:
                            upper_half(t)
                            if t + 2 < TILES:
                                square(t + 2)

            @block.vector
            def _(dve):
                def norm(t):
                    dve.wait_ge(sumsq, t + 1)
                    nc.vector.tensor_scalar(stat[:, 1, t:t + 1], stat[:, 0, t:t + 1], 1.0 / D, EPS, ALU.mult, ALU.add).then_inc(var, 1)
                    dve.wait_ge(rstd, t + 1)
                    nc.vector.tensor_scalar(x[:, t % 3], x[:, t % 3], stat[:, 2, t:t + 1], None, ALU.mult).then_inc(xn_ok, 1)

                def lower_half(t):
                    b, j = divmod(t, BT)
                    for a in range(2):
                        dve.wait_ge(th_ok, 2 * t + a + 1)
                        up = h[:, b % 2, 0, j, 4 * a:4 * a + 4].rearrange("p k n -> p (k n)").bitcast(F32)
                        nc.vector.tensor_tensor(h[:, b % 2, 1, j, 4 * a:4 * a + 4].rearrange("p k n -> p (k n)"), tr[:, t % 2, a], up,
                                                ALU.subtract).then_inc(tl_ok, 1)

                norm(0)
                norm(1)
                for k in range(KD):
                    dve.wait_ge(hi_ok, k + 1)
                    nc.vector.scalar_tensor_tensor(w_lo[:, k], raw[:, k % 2], g[:, k:k + 1], w_hi[:, k].bitcast(F32),
                                                   ALU.mult, ALU.subtract).then_inc(raw_used, 1)
                    if k % 2:
                        lower_half(k // 2)
                        norm(k // 2 + 2)
                for t in range(BT, TILES):
                    lower_half(t)
                    if t + 2 < TILES:
                        norm(t + 2)

            @block.tensor
            def _(pe):
                def turn(t):
                    pe.wait_ge(xn_ok, t + 1)
                    if t >= 2:
                        pe.wait_ge(tl_ok, 2 * (t - 1))
                    for k in range(KD):
                        ins = nc.tensor.transpose(tr[:, t % 2, k // 4, (k % 4) * P:(k % 4 + 1) * P],
                                                  x[:, t % 3, k * P:(k + 1) * P], ident[:])
                    ins.then_inc(tr_ok, 1)

                pe.wait_ge(ident_ok, 1)
                for t in range(BT):
                    turn(t)
                for b in range(BLOCKS):
                    nt = len(tiles_of(b))
                    pe.wait_ge(tl_ok, 2 * (tiles_of(b)[-1] + 1))
                    for m in range(KD):
                        n = b * KD + m
                        if n >= 4:
                            pe.wait_ge(z_ok, n - 3)
                        for k in range(KD):
                            if n == 0:
                                pe.wait_ge(raw_used, k + 1)
                            cols = slice(m * P, (m + 1) * P)
                            ins = product3(nc, acc[:, n % 4, 0:nt * P], w_hi[:, k, cols], w_lo[:, k, cols],
                                           h[:, b % 2, 0, 0:nt, k], h[:, b % 2, 1, 0:nt, k], k == 0, k == KD - 1)
                        ins.then_inc(z_mm, 1)
                        if m % 2 and BT * (b + 1) + m // 2 < TILES:
                            turn(BT * (b + 1) + m // 2)


def mixers(nc, outer, io, scr):
    sem = lambda n: outer.new("s3_" + n)
    with ExitStack() as ctx:
        room = Room(nc, ctx, "s3")
        sb, ps = room.sb, room.ps
        ident = sb("ident", [P, P])
        u = sb("u", [P, 2, GROUPS, NC])
        injT = sb("injT", [P, PAIRS, 4, P])
        outm = sb("outm", [P, 2, PAIRS, STEP + 1, SG])
        toep = sb("toep", [P, GROUPS, 2 * P])
        ha = sb("ha", [P, 2, PAIRS, NC])
        hb = sb("hb", [P, 2, PAIRS, NC])
        LV = 7
        lev = sb("lev", [P, LV, 3, PAIRS])
        lt = sb("lt", [P, 2, PAIRS])
        h0n = sb("h0n", [P, 2, P])
        h0 = sb("h0", [P, 2, STREAMS, PAIRS])
        ends = sb("ends", [P, 2, STREAMS, PAIRS])
        last = sb("last", [P, 2, P])
        lastp = sb("lastp", [PAIRS, 2, P])
        inj_ps = ps("inj", [P, 2, 512])
        out_ps = ps("out", [P, 3, 512])
        misc = ps("misc", [P, 512])

        ident0, ident_ok, zero_ok = sem("ident0"), sem("ident"), sem("zero")
        inj_in, u_in, outm_in, lev_in, h0_in, toep_in = (sem(n) for n in ("inj_in", "u_in", "outm_in", "lev_in", "h0_in", "toep_in"))
        inj_mm, inj_ok, h0_tr, h0_ok = sem("inj_mm"), sem("inj_ok"), sem("h0_tr"), sem("h0_ok")
        chain, scan_ok, start_ok, last_tr, last_ok = sem("chain"), sem("scan"), sem("start"), sem("last_tr"), sem("last")
        out_mm, out_even, out_odd, stored = sem("out_mm"), sem("out_even"), sem("out_odd"), sem("stored")

        with nc.Block() as block:

            @block.sync
            def _(sp):
                sp.dma_start(injT[:], scr["injT"]).then_inc(inj_in, 16)
                zs = scr["z"].rearrange("m (g h) j c -> m h g j c", h=SG)
                for j in range(STEP):
                    for m in range(4):
                        sp.dma_start(u[SG * (j % 8):SG * (j % 8) + SG, j // 8, 8 * m:8 * m + 8], zs[4 + m][:, :, j]).then_inc(u_in, 16)
                sp.dma_start(lev[:, 0, 0:2], scr["pow16"]).then_inc(lev_in, 16)
                for part, name in enumerate(("state_ssm_re", "state_ssm_im")):
                    sp.dma_start(h0n[:, part], io[name][0].rearrange("b (q t) s -> (b q) (t s)", t=2)).then_inc(h0_in, 16)
                sp.dma_start(outm[:], scr["outm"]).then_inc(outm_in, 16)
                sp.wait_ge(zero_ok, 1)
                for i in range(8):
                    rows = slice(SG * i, SG * i + SG)
                    sp.dma_start(toep[rows, :, SG * i:P], scr["taps"][:, :, 0:8 - i].rearrange("h g k c -> h g (k c)")).then_inc(toep_in, 16)
                    sp.dma_start(toep[rows, :, P:2 * P], scr["taps"][:, :, 8 - i:16 - i].rearrange("h g k c -> h g (k c)")).then_inc(toep_in, 16)
                sp.wait_ge(last_ok, 4)
                for part, name in enumerate(("new_ssm_re", "new_ssm_im")):
                    sp.dma_start(io[name + "_s"][0].rearrange("b (q t) s -> (b q) (t s)", t=2), last[:, part]).then_inc(stored, 16)
                    sp.dma_start(io[name + "_p"][0, 0].rearrange("(q t) s -> q (t s)", t=2), lastp[:, part]).then_inc(stored, 16)
                for m in range(4):
                    sp.wait_ge(out_even, 4 * (m + 1))
                    sp.wait_ge(out_odd, 4 * (m + 1))
                    ys = scr["y"].rearrange("m (g h) j c -> m h g j c", h=SG)
                    for j in range(STEP):
                        sp.dma_start(ys[m][:, :, j], u[SG * (j % 8):SG * (j % 8) + SG, j // 8, 8 * m:8 * m + 8]).then_inc(stored, 16)
                sp.wait_ge(stored, (4 + 4 * STEP) * 16)

            @block.gpsimd
            def _(pool):
                identity_matrix(nc, pool, ident, ident0, ident_ok)
                nc.gpsimd.memset(toep[:, :, 0:P], 0.0).then_inc(zero_ok, 1)

            @block.scalar
            def _(act):
                for q in range(PAIRS):
                    act.wait_ge(inj_mm, q + 1)
                    nc.scalar.activation(ha[:, :, q], inj_ps[:, q % 2, 0:2 * NC].rearrange("p (r c) -> p r c", r=2),
                                         ACT.Copy).then_inc(inj_ok, 1)
                for part in range(2):
                    act.wait_ge(last_tr, 1)
                    nc.scalar.activation(last[:, part], misc[:, part * P:(part + 1) * P], ACT.Copy).then_inc(last_ok, 1)
                    nc.scalar.activation(lastp[:, part], misc[0:PAIRS, (2 + part) * P:(3 + part) * P], ACT.Copy).then_inc(last_ok, 1)
                for g in range(0, GROUPS, 2):
                    act.wait_ge(out_mm, g + 1)
                    nc.scalar.activation(u[:, :, g], out_ps[:, g % 3, 0:2 * NC].rearrange("p (a c) -> p a c", a=2),
                                         ACT.Copy).then_inc(out_even, 1)

            @block.vector
            def _(dve):
                links = [0]

                def then(*instructions):
                    for ins in instructions:
                        ins.then_inc(chain, 1)
                    links[0] += len(instructions)
                    dve.wait_ge(chain, links[0])

                tt, ts, stt = nc.vector.tensor_tensor, nc.vector.tensor_scalar, nc.vector.scalar_tensor_tensor
                dve.wait_ge(lev_in, 16)
                for l in range(LV):
                    if l:
                        a, b = lev[:, l - 1, 0], lev[:, l - 1, 1]
                        then(tt(lt[:, 0], a, a, ALU.mult), tt(lt[:, 1], b, b, ALU.mult),
                             stt(lev[:, l, 1], a, 2.0, b, ALU.mult, ALU.mult))
                        then(tt(lev[:, l, 0], lt[:, 0], lt[:, 1], ALU.subtract))
                    then(ts(lev[:, l, 2], lev[:, l, 1], -1.0, None, ALU.mult))
                dve.wait_ge(h0_tr, 1)
                nc.vector.tensor_copy(h0[:].rearrange("p r b q -> p (r b q)"), misc[:, 0:2 * P]).then_inc(h0_ok, 1)
                dve.wait_ge(h0_ok, 1)
                dve.wait_ge(inj_ok, PAIRS)
                src, dst = ha, hb
                for l in range(LV):
                    s = 1 << l
                    one, two = [], []
                    for q in range(PAIRS):
                        are, aim, neg = (lev[:, l, i, q:q + 1] for i in range(3))
                        for part, other, cross in ((0, 1, neg), (1, 0, aim)):
                            one.append(stt(dst[:, part, q, s:CH], src[:, part, q, 0:CH - s], are, src[:, part, q, s:CH], ALU.mult, ALU.add))
                    one.append(nc.vector.tensor_copy(dst[:, :, :, 0:s].rearrange("p r q c -> p (r q) c"),
                                                     src[:, :, :, 0:s].rearrange("p r q c -> p (r q) c")))
                    then(*one)
                    for q in range(PAIRS):
                        are, aim, neg = (lev[:, l, i, q:q + 1] for i in range(3))
                        for part, other, cross in ((0, 1, neg), (1, 0, aim)):
                            two.append(stt(dst[:, part, q, s:CH], src[:, other, q, 0:CH - s], cross, dst[:, part, q, s:CH], ALU.mult, ALU.add))
                    then(*two)
                    src, dst = dst, src
                wide = lambda i: lev[:, 0, i].unsqueeze(2).to_broadcast([P, PAIRS, STREAMS])
                st = lambda part: h0[:, part].rearrange("p b q -> p q b")
                end = lambda part: hb[:, part, :, CH:NC]
                own = lambda part: ha[:, part, :, CH:NC]
                then(tt(end(0), st(0), wide(0), ALU.mult), tt(end(1), st(1), wide(0), ALU.mult))
                then(tt(own(0), own(0), end(0), ALU.add), tt(own(1), own(1), end(1), ALU.add))
                then(tt(end(0), st(1), wide(2), ALU.mult), tt(end(1), st(0), wide(1), ALU.mult))
                then(tt(end(0), own(0), end(0), ALU.add), tt(end(1), own(1), end(1), ALU.add))
                then(*(nc.vector.tensor_copy(ends[:, part].rearrange("p b q -> p q b"), end(part)) for part in range(2)))
                dve.sem_inc(scan_ok, 1)
                flat = lambda buf: buf[:].rearrange("p r q c -> p (r q) c")
                then(nc.vector.tensor_copy(flat(ha)[:, :, 1:CH], flat(hb)[:, :, 0:CH - 1]),
                     nc.vector.memset(flat(ha)[:, :, 0:1], 0.0),
                     nc.vector.tensor_copy(own(0), st(0)), nc.vector.tensor_copy(own(1), st(1)))
                dve.sem_inc(start_ok, 1)
                for g in range(1, GROUPS, 2):
                    dve.wait_ge(out_mm, g + 1)
                    nc.vector.tensor_copy(u[:, :, g], out_ps[:, g % 3, 0:2 * NC].rearrange("p (a c) -> p a c", a=2)).then_inc(out_odd, 1)

            @block.tensor
            def _(pe):
                pe.wait_ge(ident_ok, 1)
                pe.wait_ge(h0_in, 32)
                for part in range(2):
                    ins = nc.tensor.transpose(misc[:, part * P:(part + 1) * P], h0n[:, part], ident[:])
                ins.then_inc(h0_tr, 1)
                pe.wait_ge(inj_in, 16)
                pe.wait_ge(u_in, 4 * STEP * 16)
                for q in range(PAIRS):
                    if q >= 2:
                        pe.wait_ge(inj_ok, q - 1)
                    for part in range(2):
                        for t in range(2):
                            for jh in range(2):
                                ins = nc.tensor.matmul(inj_ps[t * SS:(t + 1) * SS, q % 2, part * NC:(part + 1) * NC],
                                                       injT[:, q, 2 * part + jh, t * SS:(t + 1) * SS], u[:, jh, 2 * q + t],
                                                       start=jh == 0, stop=jh == 1)
                    ins.then_inc(inj_mm, 1)
                pe.wait_ge(scan_ok, 1)
                pe.wait_ge(h0_ok, 1)
                for part in range(2):
                    nc.tensor.transpose(misc[:, part * P:(part + 1) * P], ends[:, part].rearrange("p b q -> p (b q)"), ident[:])
                    ins = nc.tensor.transpose(misc[0:PAIRS, (2 + part) * P:(3 + part) * P], hb[:, part, :, CH - 1], ident[:])
                ins.then_inc(last_tr, 1)
                pe.wait_ge(start_ok, 1)
                pe.wait_ge(outm_in, 16)
                pe.wait_ge(toep_in, 16 * 16)
                for g in range(GROUPS):
                    q, t = divmod(g, 2)
                    rows = slice(t * SS, (t + 1) * SS)
                    if g >= 3:
                        pe.wait_ge(out_odd if (g - 3) % 2 else out_even, (g - 3) // 2 + 1)
                    for jh in range(2):
                        to = out_ps[:, g % 3, jh * NC:(jh + 1) * NC]
                        nc.tensor.matmul(to, toep[:, g, 0:P], u[:, jh, g], start=True, stop=False)
                        if jh:
                            nc.tensor.matmul(to, toep[:, g, P:2 * P], u[:, 0, g], start=False, stop=False)
                        for part in range(2):
                            ins = nc.tensor.matmul(to, outm[rows, part, q, 1 + 8 * jh:9 + 8 * jh].rearrange("p k h -> p (k h)"),
                                                   ha[rows, part, q], start=False, stop=part == 1)
                    ins.then_inc(out_mm, 1)


def pooling(nc, outer, io, scr):
    sem = lambda n: outer.new("sp_" + n)
    with ExitStack() as ctx:
        room = Room(nc, ctx, "sp")
        sb, ps = room.sb, room.ps
        EX = HIST + STEP
        ident = sb("ident", [P, P])
        ext = sb("ext", [P, 2, EX, NC])
        sums = sb("sums", [P, 2, EX, NC])
        pooled = sb("pooled", [P, 2, STEP, NC])
        ost = sb("ost", [P, 2, STEP, NC])
        count = sb("count", [P, 4, STEP])
        wp = sb("wp", [P, 4, P])
        scale = sb("scale", [P, 4])
        hist = sb("hist", [STREAMS * HIST, DP])
        tail = sb("tail", [P, 4, HIST, STREAMS])
        tail1 = sb("tail1", [P, 4, HIST])
        tails = sb("tails", [STREAMS * HIST, DP])
        tailp = sb("tailp", [HIST, DP])
        hist_ps = ps("hist", [P, 512])
        tail_ps = ps("tail", [P, 512])
        tailp_ps = ps("tailp", [P, 512])
        out_ps = ps("out", [P, 3, 512])

        ident0, ident_ok, w_in, hist_in, tail_in = (sem(n) for n in ("ident0", "ident", "w_in", "hist_in", "tail_in"))
        ext_in = [sem(f"ext_in{i}") for i in range(2)]
        hist_tr, hist_ok, tail_tr, tail_ok, cnt_ok = (sem(n) for n in ("hist_tr", "hist", "tail_tr", "tail", "cnt"))
        chain, pooled_ok, out_mm, out_ok = sem("chain"), sem("pooled"), sem("out_mm"), sem("out_ok")
        out_st, stored = [sem(f"out_st{i}") for i in range(2)], sem("stored")
        NB = 8

        with nc.Block() as block:

            @block.sync
            def _(sp):
                sp.dma_start(hist[:], io["state_pool"][0].rearrange("b e c -> (b e) c")).then_inc(hist_in, 16)
                sp.dma_start(wp[:], io["w_pool"][0].rearrange("m c d -> c m d")).then_inc(w_in, 16)
                sp.dma_start(scale[:], io["pool_scale"][0].rearrange("(m p) -> p m", p=P), allow_slow_non_contiguous=True).then_inc(w_in, 16)

                def load(m):
                    if m >= 2:
                        sp.wait_ge(pooled_ok, m - 1)
                    z = scr["z"][m]
                    sp.dma_start(ext[:, m % 2, HIST:EX], z).then_inc(ext_in[m % 2], 16)
                    sp.dma_start(ext[:, m % 2, 0:HIST, 1:CH], z[:, 1:STEP, 0:CH - 1]).then_inc(ext_in[m % 2], 16)
                load(0)
                load(1)
                for m in range(4):
                    sp.dma_start(tail[:, m], scr["z"][m][:, 1:STEP, CH:NC]).then_inc(tail_in, 16)
                    sp.dma_start(tail1[:, m], scr["z"][m][:, 1:STEP, CH - 1], allow_slow_non_contiguous=True).then_inc(tail_in, 16)
                for m in range(4):
                    sp.wait_ge(out_ok, NB * (m + 1))
                    sp.dma_start(scr["c"][0:STEP, :, m].rearrange("j p c -> p j c"), ost[:, m % 2, :, 0:CH]).then_inc(out_st[m % 2], 16)
                    sp.dma_start(scr["c"][STEP, :, m].rearrange("p (j b) -> p j b", b=STREAMS), ost[:, m % 2, :, CH:NC]).then_inc(out_st[m % 2], 16)
                    if m < 2:
                        load(m + 2)
                sp.wait_ge(tail_ok, 2)
                sp.dma_start(io["new_pool_s"][0].rearrange("b e c -> e b c"), tails[:]).then_inc(stored, 16)
                sp.dma_start(io["new_pool_p"][0, 0], tailp[:]).then_inc(stored, 16)
                sp.wait_ge(stored, 32)
                for i in range(2):
                    sp.wait_ge(out_st[i], 64)

            @block.gpsimd
            def _(pool):
                identity_matrix(nc, pool, ident, ident0, ident_ok)
                for m in range(4):
                    w = 2 << m
                    for j in range(STEP):
                        ins = nc.gpsimd.memset(count[:, m, j:j + 1], w / min(j + 1, w))
                ins.then_inc(cnt_ok, 1)

            @block.scalar
            def _(act):
                act.wait_ge(w_in, 32)
                for m in range(4):
                    if m >= 2:
                        act.wait_ge(out_st[m % 2], 32 * (m // 2))
                    for i in range(NB):
                        n = NB * m + i
                        act.wait_ge(out_mm, n + 1)
                        nc.scalar.activation(ost[:, m % 2, 2 * i:2 * i + 2].rearrange("p j c -> p (j c)"), out_ps[:, n % 3, 0:2 * NC],
                                             ACT.Copy, scale=scale[:, m:m + 1]).then_inc(out_ok, 1)
                act.wait_ge(tail_tr, 1)
                nc.scalar.activation(tails[:], tail_ps[0:STREAMS * HIST, :], ACT.Copy).then_inc(tail_ok, 1)
                nc.scalar.activation(tailp[:], tailp_ps[0:HIST, :], ACT.Copy).then_inc(tail_ok, 1)

            @block.vector
            def _(dve):
                links = [0]

                def then(*instructions):
                    for ins in instructions:
                        ins.then_inc(chain, 1)
                    links[0] += len(instructions)
                    dve.wait_ge(chain, links[0])

                dve.wait_ge(hist_tr, 1)
                dve.wait_ge(cnt_ok, 1)
                for m in range(4):
                    e = ext[:, m % 2]
                    dve.wait_ge(ext_in[m % 2], 32 * (m // 2 + 1))
                    then(nc.vector.memset(e[:, 0:HIST, 0:1], 0.0),
                         nc.vector.tensor_copy(e[:, 0:HIST, CH:NC], hist_ps[:, m * P:m * P + STREAMS * HIST].rearrange("p (b e) -> p e b", b=STREAMS)))
                    src, low = e, 0
                    for l in range(m + 1):
                        s = 1 << l
                        low += s
                        dst = sums[:, l % 2]
                        flat = lambda buf, a, b: buf[:, a:b].rearrange("p e c -> p (e c)")
                        then(nc.vector.tensor_tensor(flat(dst, low, EX), flat(src, low, EX), flat(src, low - s, EX - s), ALU.add))
                        src = dst
                    then(nc.vector.tensor_tensor(src[:, HIST:EX, 0], src[:, HIST:EX, 0], count[:, m], ALU.mult))
                    if m >= 2:
                        dve.wait_ge(out_mm, NB * (m - 1))
                    nc.vector.scalar_tensor_tensor(pooled[:, m % 2].rearrange("p j c -> p (j c)"), flat(src, HIST, EX), 1.0 / (2 << m),
                                                   flat(e, HIST, EX), ALU.mult, ALU.subtract).then_inc(pooled_ok, 1)
                    dve.wait_ge(pooled_ok, m + 1)

            @block.tensor
            def _(pe):
                pe.wait_ge(ident_ok, 1)
                pe.wait_ge(hist_in, 16)
                for m in range(4):
                    ins = nc.tensor.transpose(hist_ps[:, m * P:m * P + STREAMS * HIST], hist[:, m * P:(m + 1) * P],
                                              ident[0:STREAMS * HIST, 0:STREAMS * HIST])
                ins.then_inc(hist_tr, 1)
                pe.wait_ge(tail_in, 128)
                for m in range(4):
                    nc.tensor.transpose(tail_ps[0:STREAMS * HIST, m * P:(m + 1) * P], tail[:, m].rearrange("p e b -> p (e b)"), ident[:])
                    ins = nc.tensor.transpose(tailp_ps[0:HIST, m * P:(m + 1) * P], tail1[:, m], ident[:])
                ins.then_inc(tail_tr, 1)
                pe.wait_ge(w_in, 32)
                for m in range(4):
                    pe.wait_ge(pooled_ok, m + 1)
                    for i in range(NB):
                        n = NB * m + i
                        if n >= 3:
                            pe.wait_ge(out_ok, n - 2)
                        nc.tensor.matmul(out_ps[:, n % 3, 0:2 * NC], wp[:, m], pooled[:, m % 2, 2 * i:2 * i + 2].rearrange("p j c -> p (j c)"),
                                         start=True, stop=True).then_inc(out_mm, 1)


def gelu_glu(nc, outer, io, scr):
    sem = lambda n: outer.new("s4_" + n)
    with ExitStack() as ctx:
        room = Room(nc, ctx, "s4")
        sb, ps = room.sb, room.ps
        NB, WB = STEP // 2, 2 * NC
        raw = sb("raw", [P, 4, DP])
        w_hi, w_lo = sb("w_hi", [P, 4, DP], F32R), sb("w_lo", [P, 4, DP], F32R)
        skip, bias = sb("skip", [P, 4]), sb("bias", [P, 4])
        y = sb("y", [P, 2, 4, WB])
        z = sb("z", [P, 2, 4, WB])
        v = sb("v", [P, NB, 4, WB])
        g_hi, g_lo = sb("g_hi", [P, 2, 4, WB], F32R), sb("g_lo", [P, 2, 4, WB], F32R)
        gate = sb("gate", [P, 4, WB])
        out = sb("out", [P, 2, 4, WB])
        outs = sb("outs", [P, 4, STEP, STREAMS])
        acc = ps("acc", [P, 4, 512])

        w_in, c_in = sem("w_in"), sem("c_in")
        yz_in = [sem(f"yz_in{i}") for i in range(2)]
        whi_ok, wlo_ok = sem("whi"), sem("wlo")
        v_ok, gelu_ok, hi_ok, lo_ok, mm, gate_ok, out_ok, outs_ok = (
            sem(n) for n in ("v", "gelu", "hi", "lo", "mm", "gate", "out", "outs"))
        out_st, stored = [sem(f"out_st{i}") for i in range(2)], sem("stored")

        with nc.Block() as block:

            @block.sync
            def _(sp):
                sp.dma_start(skip[:], io["ssm_d"][0].rearrange("(m g) h -> (g h) m", m=4), allow_slow_non_contiguous=True).then_inc(c_in, 16)
                sp.dma_start(bias[:], io["b_glu"][0].rearrange("(m p) -> p m", p=P), allow_slow_non_contiguous=True).then_inc(c_in, 16)

                def load(i):
                    if i >= 2:
                        sp.wait_ge(v_ok, 4 * (i - 1))
                    sp.dma_start(y[:, i % 2].rearrange("p m (j c) -> p m j c", j=2),
                                 scr["y"][:, :, 2 * i:2 * i + 2].rearrange("m p j c -> p m j c")).then_inc(yz_in[i % 2], 16)
                    sp.dma_start(z[:, i % 2].rearrange("p m (j c) -> p m j c", j=2),
                                 scr["z"][4:8, :, 2 * i:2 * i + 2].rearrange("m p j c -> p m j c")).then_inc(yz_in[i % 2], 16)
                load(0)
                load(1)
                sp.dma_start(raw[:], io["w_glu"][0].rearrange("(k p) n -> p k n", p=P)).then_inc(w_in, 16)
                for i in range(2, NB):
                    load(i)
                for i in range(NB):
                    sp.wait_ge(out_ok, 4 * (i + 1))
                    for j in range(2):
                        sp.dma_start(scr["c"][2 * i + j][:, 4:8], out[:, i % 2, :, j * NC:j * NC + CH]).then_inc(out_st[i % 2], 16)
                sp.wait_ge(outs_ok, NB)
                sp.dma_start(scr["c"][STEP][:, 4:8].rearrange("p m (j b) -> p m j b", b=STREAMS), outs[:]).then_inc(stored, 16)
                sp.wait_ge(stored, 16)
                for i in range(2):
                    sp.wait_ge(out_st[i], NB // 2 * 32)

            @block.scalar
            def _(act):
                for i in range(NB):
                    act.wait_ge(v_ok, 4 * (i + 1))
                    flat = v[:, i].rearrange("p m n -> p (m n)")
                    nc.scalar.activation(flat, flat, ACT.Gelu_apprx_tanh).then_inc(gelu_ok, 1)
                act.wait_ge(w_in, 16)
                nc.scalar.activation(w_hi[:], raw[:], ACT.Copy).then_inc(whi_ok, 1)
                act.wait_ge(c_in, 32)

                def upper_half(i):
                    act.wait_ge(gelu_ok, i + 1)
                    if i >= 2:
                        act.wait_ge(mm, 4 * (i - 1))
                    nc.scalar.activation(g_hi[:, i % 2], v[:, i], ACT.Copy).then_inc(hi_ok, 1)
                upper_half(0)
                for i in range(NB):
                    if i + 1 < NB:
                        upper_half(i + 1)
                    for m in range(4):
                        n = 4 * i + m
                        act.wait_ge(mm, n + 1)
                        if i:
                            act.wait_ge(out_ok, n - 3)
                        nc.scalar.activation(gate[:, m], acc[:, m, 0:WB], ACT.Sigmoid, bias=bias[:, m:m + 1]).then_inc(gate_ok, 1)

            @block.vector
            def _(dve):
                dve.wait_ge(c_in, 32)
                for i in range(NB):
                    dve.wait_ge(yz_in[i % 2], 32 * (i // 2 + 1))
                    for m in range(4):
                        nc.vector.scalar_tensor_tensor(v[:, i, m], z[:, i % 2, m], skip[:, m:m + 1], y[:, i % 2, m],
                                                       ALU.mult, ALU.add).then_inc(v_ok, 1)
                dve.wait_ge(whi_ok, 1)
                nc.vector.tensor_tensor(w_lo[:], raw[:], w_hi[:].bitcast(F32), ALU.subtract).then_inc(wlo_ok, 1)

                def lower_half(i):
                    dve.wait_ge(hi_ok, i + 1)
                    nc.vector.tensor_tensor(g_lo[:, i % 2], v[:, i], g_hi[:, i % 2].bitcast(F32), ALU.subtract).then_inc(lo_ok, 1)
                lower_half(0)
                for i in range(NB):
                    if i + 1 < NB:
                        lower_half(i + 1)
                    if i >= 2:
                        dve.wait_ge(out_st[i % 2], 32 * (i // 2))
                    for m in range(4):
                        n = 4 * i + m
                        dve.wait_ge(gate_ok, n + 1)
                        nc.vector.tensor_tensor(out[:, i % 2, m], v[:, i, m], gate[:, m], ALU.mult).then_inc(out_ok, 1)
                    dve.wait_ge(out_ok, 4 * (i + 1))
                    src = out[:, i % 2].rearrange("p m (j c) -> p m j c", j=2)[:, :, :, CH:NC]
                    nc.vector.tensor_copy(outs[:, :, 2 * i:2 * i + 2], src).then_inc(outs_ok, 1)

            @block.tensor
            def _(pe):
                pe.wait_ge(wlo_ok, 1)
                for i in range(NB):
                    pe.wait_ge(lo_ok, i + 1)
                    for m in range(4):
                        n = 4 * i + m
                        if n >= 4:
                            pe.wait_ge(gate_ok, n - 3)
                        for k in range(4):
                            cols = slice(m * P, (m + 1) * P)
                            ins = product3(nc, acc[:, m, 0:WB], w_hi[:, k, cols], w_lo[:, k, cols], g_hi[:, i % 2, k], g_lo[:, i % 2, k],
                                           k == 0, k == 3)
                        ins.then_inc(mm, 1)


def output_projection(nc, outer, io, scr, tag, weight, source, first, target, normed):
    sem = lambda n: outer.new(f"{tag}_{n}")
    with ExitStack() as ctx:
        room = Room(nc, ctx, tag)
        sb, ps = room.sb, room.ps
        ident = sb("ident", [P, P])
        expo = sb("expo", [P, 1])
        raw = sb("raw", [P, 2, D])
        w_hi, w_lo = sb("w_hi", [P, KD, D], F32R), sb("w_lo", [P, KD, D], F32R)
        s = sb("s", [P, 2, KD, P])
        s_hi, s_lo = sb("s_hi", [P, 2, KD, P], F32R), sb("s_lo", [P, 2, KD, P], F32R)
        x = sb("x", [P, 2, D])
        xn = sb("xn", [P, 2, D])
        junk = sb("junk", [P, D])
        stat = sb("stat", [P, 2, 3])
        ht = sb("ht", [P, 2, KD, P])
        acc = ps("acc", [P, 2, 2, 512])
        tr = ps("tr", [P, 2, 2, 512])

        ident0, ident_ok = sem("ident0"), sem("ident")
        raw_in, whi_ok, wlo_ok = [sem(f"raw_in{i}") for i in range(2)], sem("whi"), sem("wlo")
        s_in, x_in = [sem(f"s_in{i}") for i in range(2)], [sem(f"x_in{i}") for i in range(2)]
        shi_ok, slo_ok, mm, x_ok, sumsq, var, rstd, xn_ok, tr_ok, ht_ok = (
            sem(n) for n in ("shi", "slo", "mm", "x", "sumsq", "var", "rstd", "xn", "tr", "ht"))
        x_st, ht_st = [sem(f"x_st{i}") for i in range(2)], [sem(f"ht_st{i}") for i in range(2)]
        LAST = TILES - 1

        with nc.Block() as block:

            @block.sync
            def _(sp):
                w = io[weight][0].rearrange("(k p) n -> k p n", p=P)

                def load_source(t, i):
                    sp.dma_start(s[:, i], source[t]).then_inc(s_in[i], 16)

                def load_x(t, i):
                    sp.dma_start(x[:, i], first(t)).then_inc(x_in[i], 16)

                def store_x(t, i):
                    sp.wait_ge(x_ok, 2 * t + 2)
                    sp.dma_start(target[t], x[:, i]).then_inc(x_st[i], 16)

                def store_normed(t, i):
                    sp.wait_ge(ht_ok, 2 * t + 2)
                    sp.dma_start(normed[t], ht[:, i]).then_inc(ht_st[i], 16)

                def next_loads(t, i, uses):
                    sp.wait_ge(slo_ok, t + 1)
                    load_source(t + 2, i)
                    sp.wait_ge(xn_ok, t + 1)
                    sp.wait_ge(x_st[i], 16 * uses)
                    load_x(t + 2, i)

                load_source(0, 0)
                for k in range(KD):
                    if k >= 2:
                        sp.wait_ge(wlo_ok, k - 1)
                    sp.dma_start(raw[:, k % 2], w[k]).then_inc(raw_in[k % 2], 16)
                    if k == 1:
                        load_source(1, 1)
                        load_x(0, 0)
                        load_x(1, 1)
                store_x(0, 0)
                next_loads(0, 0, 1)
                with sp.Fori(0, 6) as r:
                    for half in range(2):
                        t = 2 * r + 1 + half
                        i = 1 - half
                        store_x(t, i)
                        store_normed(t - 1, 1 - i)
                        next_loads(t, i, r + 1 + half)
                for t in range(13, TILES):
                    store_x(t, t % 2)
                    store_normed(t - 1, (t - 1) % 2)
                    if t + 2 < TILES:
                        next_loads(t, t % 2, t // 2 + 1)
                store_normed(LAST, LAST % 2)
                for i in range(2):
                    sp.wait_ge(x_st[i], 16 * ((TILES + 1 - i) // 2))
                    sp.wait_ge(ht_st[i], 16 * ((TILES + 1 - i) // 2))

            @block.gpsimd
            def _(pool):
                nc.gpsimd.memset(expo[:], -0.5)
                identity_matrix(nc, pool, ident, ident0, ident_ok)
                for t in range(TILES):
                    pool.wait_ge(var, t + 1)
                    nc.gpsimd.tensor_tensor(stat[:, t % 2, 2:3], stat[:, t % 2, 1:2], expo[:], ALU.pow).then_inc(rstd, 1)

            @block.scalar
            def _(act):
                def source_half(t, i, uses):
                    act.wait_ge(s_in[i], 16 * uses)
                    if not isinstance(t, int) or t >= 2:
                        act.wait_ge(mm, t - 1)
                    nc.scalar.activation(s_hi[:, i], s[:, i], ACT.Copy).then_inc(shi_ok, 1)

                def square(t, i):
                    act.wait_ge(x_ok, 2 * t + 2)
                    if not isinstance(t, int) or t >= 1:
                        act.wait_ge(xn_ok, t)
                    nc.scalar.activation(junk[:], x[:, i], ACT.Square, accum_out=stat[:, i, 0:1]).then_inc(sumsq, 1)

                def take_normed(t, i, uses):
                    act.wait_ge(tr_ok, t + 1)
                    if uses is not None:
                        act.wait_ge(ht_st[i], 16 * uses)
                    for a in range(2):
                        nc.scalar.activation(ht[:, i, 4 * a:4 * a + 4].rearrange("p k n -> p (k n)"), tr[:, i, a], ACT.Copy).then_inc(ht_ok, 1)

                source_half(0, 0, 1)
                for k in range(KD):
                    act.wait_ge(raw_in[k % 2], 16 * (k // 2 + 1))
                    nc.scalar.activation(w_hi[:, k], raw[:, k % 2], ACT.Copy).then_inc(whi_ok, 1)
                source_half(1, 1, 1)
                square(0, 0)
                for t in (1, 2):
                    source_half(t + 1, (t + 1) % 2, t // 2 + 1 + t % 2)
                    square(t, t % 2)
                    take_normed(t - 1, (t - 1) % 2, None)
                with act.Fori(0, 6) as r:
                    for half in range(2):
                        t = 2 * r + 3 + half
                        i = 1 - half
                        source_half(t + 1, 1 - i, r + 3)
                        square(t, i)
                        take_normed(t - 1, 1 - i, r + 1)
                source_half(LAST, 0, 9)
                square(LAST - 1, 1)
                take_normed(LAST - 2, 0, 7)
                square(LAST, 0)
                take_normed(LAST - 1, 1, 7)
                take_normed(LAST, 0, 8)

            @block.vector
            def _(dve):
                def source_half(t, i):
                    dve.wait_ge(shi_ok, t + 1)
                    nc.vector.tensor_tensor(s_lo[:, i], s[:, i], s_hi[:, i].bitcast(F32), ALU.subtract).then_inc(slo_ok, 1)

                def residual_and_norm(t, i, uses):
                    dve.wait_ge(mm, t + 1)
                    dve.wait_ge(x_in[i], 16 * uses)
                    for a in range(2):
                        half = x[:, i, a * 512:(a + 1) * 512]
                        nc.vector.tensor_tensor(half, half, acc[:, i, a], ALU.add).then_inc(x_ok, 1)
                    dve.wait_ge(sumsq, t + 1)
                    nc.vector.tensor_scalar(stat[:, i, 1:2], stat[:, i, 0:1], 1.0 / D, EPS, ALU.mult, ALU.add).then_inc(var, 1)
                    dve.wait_ge(rstd, t + 1)
                    if not isinstance(t, int) or t >= 2:
                        dve.wait_ge(tr_ok, t - 1)
                    nc.vector.tensor_scalar(xn[:, i], x[:, i], stat[:, i, 2:3], None, ALU.mult).then_inc(xn_ok, 1)

                source_half(0, 0)
                for k in range(KD):
                    dve.wait_ge(whi_ok, k + 1)
                    nc.vector.tensor_tensor(w_lo[:, k], raw[:, k % 2], w_hi[:, k].bitcast(F32), ALU.subtract).then_inc(wlo_ok, 1)
                source_half(1, 1)
                residual_and_norm(0, 0, 1)
                source_half(2, 0)
                residual_and_norm(1, 1, 1)
                with dve.Fori(0, 7) as r:
                    for half in range(2):
                        t = 2 * r + 2 + half
                        source_half(t + 1, 1 - half)
                        residual_and_norm(t, half, r + 2)
                residual_and_norm(LAST, 0, 9)

            @block.tensor
            def _(pe):
                def multiply(t, i, first_tile=False):
                    pe.wait_ge(slo_ok, t + 1)
                    if not isinstance(t, int) or t >= 2:
                        pe.wait_ge(x_ok, 2 * t - 2)
                    for k in range(KD):
                        if first_tile:
                            pe.wait_ge(wlo_ok, k + 1)
                        for a in range(2):
                            cols = slice(a * 512, (a + 1) * 512)
                            ins = product3(nc, acc[:, i, a], s_hi[:, i, k], s_lo[:, i, k], w_hi[:, k, cols], w_lo[:, k, cols],
                                           k == 0, k == KD - 1)
                    ins.then_inc(mm, 1)

                def turn(t, i):
                    pe.wait_ge(xn_ok, t + 1)
                    if not isinstance(t, int) or t >= 2:
                        pe.wait_ge(ht_ok, 2 * t - 2)
                    for k in range(KD):
                        ins = nc.tensor.transpose(tr[:, i, k // 4, (k % 4) * P:(k % 4 + 1) * P], xn[:, i, k * P:(k + 1) * P], ident[:])
                    ins.then_inc(tr_ok, 1)

                pe.wait_ge(ident_ok, 1)
                multiply(0, 0, True)
                multiply(1, 1)
                turn(0, 0)
                multiply(2, 0)
                turn(1, 1)
                with pe.Fori(0, 7) as r:
                    for half in range(2):
                        t = 2 * r + 3 + half
                        multiply(t, 1 - half)
                        turn(t - 1, half)
                turn(LAST, 0)


def query_projection(nc, outer, io, scr):
    sem = lambda n: outer.new("s6_" + n)
    with ExitStack() as ctx:
        room = Room(nc, ctx, "s6")
        sb, ps = room.sb, room.ps
        g = sb("g", [P, KD])
        raw = sb("raw", [P, 2, D])
        w_hi, w_lo = sb("w_hi", [P, KD, D], F32R), sb("w_lo", [P, KD, D], F32R)
        t_in = sb("t_in", [P, 3, KD, P])
        h = sb("h", [P, 2, 2, BT, KD, P], F32R)
        st = sb("st", [P, 2, BT * P])
        acc = ps("acc", [P, 4, 512])
        g_in, raw_in, whi_ok, wlo_ok = sem("g_in"), [sem(f"raw_in{i}") for i in range(2)], sem("whi"), sem("wlo")
        h_in, hi_ok, lo_ok = [sem(f"h_in{i}") for i in range(3)], sem("hi"), sem("lo")
        mm, q_ok, q_st = sem("mm"), sem("q"), [sem(f"q_st{i}") for i in range(2)]
        BLOCKS = TILES // BT + 1

        def tiles_of(b):
            return range(BT * b, min(BT * b + BT, TILES))

        with nc.Block() as block:

            @block.sync
            def _(sp):
                w = io["w_q"][0].rearrange("(k p) n -> k p n", p=P)

                def load(t):
                    if t >= 3:
                        sp.wait_ge(lo_ok, t - 2)
                    sp.dma_start(t_in[:, t % 3], scr["h"][t]).then_inc(h_in[t % 3], 16)
                sp.dma_start(g[:], io["g_xattn"][0].rearrange("(k p) -> p k", p=P), allow_slow_non_contiguous=True).then_inc(g_in, 16)
                for t in range(3):
                    load(t)
                for k in range(KD):
                    if k >= 2:
                        sp.wait_ge(wlo_ok, k - 1)
                    sp.dma_start(raw[:, k % 2], w[k]).then_inc(raw_in[k % 2], 16)
                for t in range(3, 2 * BT):
                    load(t)
                for b in range(BLOCKS):
                    for m in range(KD):
                        n = b * KD + m
                        sp.wait_ge(q_ok, n + 1)
                        nt = len(tiles_of(b))
                        sp.dma_start(scr["q"][BT * b:BT * b + nt, :, m].rearrange("t p n -> p t n"),
                                     st[:, n % 2, 0:nt * P].rearrange("p (t n) -> p t n", t=nt)).then_inc(q_st[n % 2], 16)
                        if m % 2 and BT * (b + 2) + m // 2 < TILES:
                            load(BT * (b + 2) + m // 2)
                for i in range(2):
                    sp.wait_ge(q_st[i], BLOCKS * KD // 2 * 16)

            @block.scalar
            def _(act):
                def upper_half(t):
                    b, j = divmod(t, BT)
                    act.wait_ge(h_in[t % 3], 16 * (t // 3 + 1))
                    if b >= 2:
                        act.wait_ge(mm, (b - 1) * KD)
                    nc.scalar.activation(h[:, b % 2, 0, j], t_in[:, t % 3], ACT.Copy).then_inc(hi_ok, 1)
                act.wait_ge(g_in, 16)
                for t in range(3):
                    upper_half(t)
                for k in range(KD):
                    act.wait_ge(raw_in[k % 2], 16 * (k // 2 + 1))
                    nc.scalar.activation(w_hi[:, k], raw[:, k % 2], ACT.Copy, scale=g[:, k:k + 1]).then_inc(whi_ok, 1)
                upper_half(3)
                for b in range(BLOCKS):
                    for m in range(KD):
                        n = b * KD + m
                        act.wait_ge(mm, n + 1)
                        if n >= 2:
                            act.wait_ge(q_st[n % 2], 16 * (n // 2))
                        wide = P * len(tiles_of(b))
                        nc.scalar.activation(st[:, n % 2, 0:wide], acc[:, n % 4, 0:wide], ACT.Copy).then_inc(q_ok, 1)
                        if m % 2 and BT * (b + 1) + m // 2 < TILES:
                            upper_half(BT * (b + 1) + m // 2)

            @block.vector
            def _(dve):
                def lower_half(t):
                    b, j = divmod(t, BT)
                    dve.wait_ge(hi_ok, t + 1)
                    nc.vector.tensor_tensor(h[:, b % 2, 1, j], t_in[:, t % 3], h[:, b % 2, 0, j].bitcast(F32), ALU.subtract).then_inc(lo_ok, 1)
                for t in range(3):
                    lower_half(t)
                for k in range(KD):
                    dve.wait_ge(whi_ok, k + 1)
                    nc.vector.scalar_tensor_tensor(w_lo[:, k], raw[:, k % 2], g[:, k:k + 1], w_hi[:, k].bitcast(F32),
                                                   ALU.mult, ALU.subtract).then_inc(wlo_ok, 1)
                for t in range(3, TILES):
                    lower_half(t)

            @block.tensor
            def _(pe):
                for b in range(BLOCKS):
                    nt = len(tiles_of(b))
                    pe.wait_ge(lo_ok, tiles_of(b)[-1] + 1)
                    for m in range(KD):
                        n = b * KD + m
                        if n >= 4:
                            pe.wait_ge(q_ok, n - 3)
                        for k in range(KD):
                            if n == 0:
                                pe.wait_ge(wlo_ok, k + 1)
                            cols = slice(m * P, (m + 1) * P)
                            ins = product3(nc, acc[:, n % 4, 0:nt * P], w_hi[:, k, cols], w_lo[:, k, cols],
                                           h[:, b % 2, 0, 0:nt, k], h[:, b % 2, 1, 0:nt, k], k == 0, k == KD - 1)
                        ins.then_inc(mm, 1)


def prompt_attention(nc, outer, io, scr):
    sem = lambda n: outer.new("s7_" + n)
    with ExitStack() as ctx:
        room = Room(nc, ctx, "s7")
        sb, ps = room.sb, room.ps
        SCALE = float(HD) ** -0.5
        ident = sb("ident", [P, P])
        kraw, vraw = sb("kraw", [P, KD, MEM]), sb("vraw", [P, 2, D])
        k_hi, k_lo = sb("k_hi", [P, KD, MEM], F32R), sb("k_lo", [P, KD, MEM], F32R)
        v_hi, v_lo = sb("v_hi", [P, 2, D], F32R), sb("v_lo", [P, 2, D], F32R)
        q = sb("q", [P, 2, KD, P])
        q_hi, q_lo = sb("q_hi", [P, 2, KD, P], F32R), sb("q_lo", [P, 2, KD, P], F32R)
        prob = sb("prob", [P, 2, D])
        top, ntop, den, rden = (sb(n, [P, 2, HEADS]) for n in ("top", "ntop", "den", "rden"))
        pt = sb("pt", [P, 2, 2, KD, BT * P], F32R)
        ost = sb("ost", [P, 2, BT * P])
        score = ps("score", [P, 2, 2, 512])
        tr = ps("tr", [P, 2, 512])
        o_ps = ps("o", [P, 2, 512])
        ident0, ident_ok, kv_in, khi_ok, klo_ok = (sem(n) for n in ("ident0", "ident", "kv_in", "khi", "klo"))
        q_in, qhi_ok, qlo_ok = [sem(f"q_in{i}") for i in range(2)], sem("qhi"), sem("qlo")
        sc_mm, top_ok, ntop_ok, exp_ok, rden_ok, prob_ok = (sem(n) for n in ("sc_mm", "top", "ntop", "exp", "rden", "prob"))
        tr_ok, phi_ok, plo_ok, o_mm, o_ok = (sem(n) for n in ("tr", "phi", "plo", "o_mm", "o"))
        o_st = [sem(f"o_st{i}") for i in range(2)]
        T = STEP
        B = T // BT

        with nc.Block() as block:

            @block.sync
            def _(sp):
                sp.dma_start(kraw[:], scr["kT"]).then_inc(kv_in, 16)
                sp.dma_start(vraw[:], scr["v"]).then_inc(kv_in, 16)

                def load(t):
                    if t >= 2:
                        sp.wait_ge(qlo_ok, t - 1)
                    sp.dma_start(q[:, t % 2], scr["q"][t]).then_inc(q_in[t % 2], 16)
                for t in range(BT + 2):
                    load(t)
                for b in range(B):
                    for m in range(KD):
                        n = b * KD + m
                        t = BT * (b + 1) + 2 + m // 2
                        if m % 2 == 0 and t < T:
                            load(t)
                        sp.wait_ge(o_ok, n + 1)
                        sp.dma_start(scr["o"][BT * b:BT * b + BT, :, m].rearrange("t p n -> p t n"),
                                     ost[:, n % 2].rearrange("p (t n) -> p t n", t=BT)).then_inc(o_st[n % 2], 16)
                for i in range(2):
                    sp.wait_ge(o_st[i], B * KD // 2 * 16)

            @block.gpsimd
            def _(pool):
                identity_matrix(nc, pool, ident, ident0, ident_ok)

            @block.scalar
            def _(act):
                def query_half(t):
                    act.wait_ge(q_in[t % 2], 16 * (t // 2 + 1))
                    if t >= 2:
                        act.wait_ge(sc_mm, t - 1)
                    nc.scalar.activation(q_hi[:, t % 2], q[:, t % 2], ACT.Copy).then_inc(qhi_ok, 1)

                def exponentials(t):
                    act.wait_ge(ntop_ok, t + 1)
                    if t >= 2:
                        act.wait_ge(tr_ok, 2 * (t - 1))
                    for hd in range(HEADS):
                        cols = slice(hd * MEM, (hd + 1) * MEM)
                        nc.scalar.activation(prob[:, t % 2, cols], score[:, t % 2, hd // 2, (hd % 2) * MEM:(hd % 2 + 1) * MEM], ACT.Exp,
                                             bias=ntop[:, t % 2, hd:hd + 1], scale=SCALE,
                                             accum_out=den[:, t % 2, hd:hd + 1]).then_inc(exp_ok, 1)

                def upper_half(t):
                    b, j = divmod(t, BT)
                    for a in range(2):
                        act.wait_ge(tr_ok, 2 * t + a + 1)
                        if b >= 2:
                            act.wait_ge(o_mm, (b - 1) * KD)
                        nc.scalar.activation(pt[:, b % 2, 0, 4 * a:4 * a + 4, j * P:(j + 1) * P],
                                             tr[:, a].rearrange("p (k n) -> p k n", k=4), ACT.Copy).then_inc(phi_ok, 1)

                def take_outputs(b):
                    for m in range(KD):
                        n = b * KD + m
                        act.wait_ge(o_mm, n + 1)
                        if n >= 2:
                            act.wait_ge(o_st[n % 2], 16 * (n // 2))
                        nc.scalar.activation(ost[:, n % 2], o_ps[:, n % 2], ACT.Copy).then_inc(o_ok, 1)

                act.wait_ge(kv_in, 32)
                nc.scalar.activation(k_hi[:], kraw[:], ACT.Copy).then_inc(khi_ok, 1)
                nc.scalar.activation(v_hi[:], vraw[:], ACT.Copy).then_inc(khi_ok, 1)
                query_half(0)
                query_half(1)
                for t in range(T):
                    exponentials(t)
                    if t + 2 < T:
                        query_half(t + 2)
                    if t:
                        upper_half(t - 1)
                        if t % BT == 0:
                            take_outputs(t // BT - 1)
                upper_half(T - 1)
                take_outputs(B - 1)

            @block.vector
            def _(dve):
                def query_half(t):
                    dve.wait_ge(qhi_ok, t + 1)
                    nc.vector.tensor_tensor(q_lo[:, t % 2], q[:, t % 2], q_hi[:, t % 2].bitcast(F32), ALU.subtract).then_inc(qlo_ok, 1)

                def maxima(t):
                    dve.wait_ge(sc_mm, t + 1)
                    if t >= 2:
                        dve.wait_ge(exp_ok, HEADS * (t - 1))
                    nc.vector.reduce_max(top[:, t % 2], score[:, t % 2].rearrange("p a (b n) -> p (a b) n", b=2), AX_X).then_inc(top_ok, 1)
                    dve.wait_ge(top_ok, t + 1)
                    nc.vector.tensor_scalar(ntop[:, t % 2], top[:, t % 2], -SCALE, None, ALU.mult).then_inc(ntop_ok, 1)

                def normalise(t):
                    dve.wait_ge(exp_ok, HEADS * (t + 1))
                    nc.vector.reciprocal(rden[:, t % 2], den[:, t % 2]).then_inc(rden_ok, 1)
                    dve.wait_ge(rden_ok, t + 1)
                    for hd in range(HEADS):
                        cols = prob[:, t % 2, hd * MEM:(hd + 1) * MEM]
                        nc.vector.tensor_scalar(cols, cols, rden[:, t % 2, hd:hd + 1], None, ALU.mult).then_inc(prob_ok, 1)

                def lower_half(t):
                    b, j = divmod(t, BT)
                    for a in range(2):
                        dve.wait_ge(phi_ok, 2 * t + a + 1)
                        to = lambda half: pt[:, b % 2, half, 4 * a:4 * a + 4, j * P:(j + 1) * P]
                        nc.vector.tensor_tensor(to(1), tr[:, a].rearrange("p (k n) -> p k n", k=4), to(0).bitcast(F32),
                                                ALU.subtract).then_inc(plo_ok, 1)

                dve.wait_ge(khi_ok, 2)
                nc.vector.tensor_tensor(k_lo[:], kraw[:], k_hi[:].bitcast(F32), ALU.subtract).then_inc(klo_ok, 1)
                nc.vector.tensor_tensor(v_lo[:], vraw[:], v_hi[:].bitcast(F32), ALU.subtract).then_inc(klo_ok, 1)
                query_half(0)
                query_half(1)
                for t in range(T):
                    maxima(t)
                    if t + 2 < T:
                        query_half(t + 2)
                    normalise(t)
                    if t:
                        lower_half(t - 1)
                lower_half(T - 1)

            @block.tensor
            def _(pe):
                def scores(t):
                    pe.wait_ge(qlo_ok, t + 1)
                    if t >= 2:
                        pe.wait_ge(exp_ok, HEADS * (t - 1))
                    for hd in range(HEADS):
                        for k in (2 * hd, 2 * hd + 1):
                            ins = product3(nc, score[:, t % 2, hd // 2, (hd % 2) * MEM:(hd % 2 + 1) * MEM], q_hi[:, t % 2, k],
                                           q_lo[:, t % 2, k], k_hi[:, k], k_lo[:, k], k % 2 == 0, k % 2 == 1)
                    ins.then_inc(sc_mm, 1)

                def turn(t):
                    pe.wait_ge(prob_ok, HEADS * (t + 1))
                    for a in range(2):
                        if t:
                            pe.wait_ge(plo_ok, 2 * (t - 1) + a + 1)
                        for k in range(4 * a, 4 * a + 4):
                            ins = nc.tensor.transpose(tr[:, a, (k % 4) * P:(k % 4 + 1) * P], prob[:, t % 2, k * P:(k + 1) * P], ident[:])
                        ins.then_inc(tr_ok, 1)

                def outputs(b):
                    pe.wait_ge(plo_ok, 2 * BT * (b + 1))
                    for m in range(KD):
                        n = b * KD + m
                        if n >= 2:
                            pe.wait_ge(o_ok, n - 1)
                        for kt in range(2):
                            cols = slice(m * P, (m + 1) * P)
                            row = (m // 2) * 2 + kt
                            ins = product3(nc, o_ps[:, n % 2], v_hi[:, kt, cols], v_lo[:, kt, cols], pt[:, b % 2, 0, row], pt[:, b % 2, 1, row],
                                           kt == 0, kt == 1)
                        ins.then_inc(o_mm, 1)

                pe.wait_ge(ident_ok, 1)
                pe.wait_ge(klo_ok, 2)
                for t in range(T):
                    scores(t)
                    if t:
                        turn(t - 1)
                        if t % BT == 0:
                            outputs(t // BT - 1)
                turn(T - 1)
                outputs(B - 1)


def stream_attention(nc, outer, io, scr):
    sem = lambda n: outer.new("sb_" + n)
    with ExitStack() as ctx:
        room = Room(nc, ctx, "sb")
        sb, ps = room.sb, room.ps
        SCALE = float(HD) ** -0.5
        RB = 32
        ident = sb("ident", [P, P])
        q = sb("q", [P, KD, P])
        qs = sb("qs", [P, KD, STREAMS, RB])
        keys = sb("keys", [P, 2, 2, D])
        values = sb("values", [P, STREAMS, 2, D])
        kT = sb("kT", [P, 2, KD, MEM])
        prob = sb("prob", [P, 2, D])
        top, ntop, den, rden = (sb(n, [P, 2, HEADS]) for n in ("top", "ntop", "den", "rden"))
        pt = sb("pt", [P, 2, KD, P])
        ot = sb("ot", [P, KD, STEP, STREAMS])
        score = ps("score", [P, 2, 512])
        tr = ps("tr", [P, 4, 512])
        o_ps = ps("o", [P, 2, 512])
        ident0, ident_ok, q_in, zero_ok, qs_ok = (sem(n) for n in ("ident0", "ident", "q_in", "zero", "qs"))
        k_in, v_in = [sem(f"k_in{i}") for i in range(2)], [sem(f"v_in{i}") for i in range(2)]
        kT_tr, kT_ok, sc_mm, top_ok, ntop_ok, exp_ok, rden_ok, prob_ok = (
            sem(n) for n in ("kT_tr", "kT", "sc_mm", "top", "ntop", "exp", "rden", "prob"))
        p_tr, pt_ok, o_mm, o_ok, stored = sem("p_tr"), sem("pt"), sem("o_mm"), sem("o"), sem("stored")

        with nc.Block() as block:

            @block.sync
            def _(sp):
                sp.dma_start(q[:], scr["q"][STEP]).then_inc(q_in, 16)
                for b in range(STREAMS):
                    if b >= 2:
                        sp.wait_ge(kT_tr, 4 * (b - 1))
                    sp.dma_start(keys[:, b % 2], io["cache_mem_k"][0, b].rearrange("(t p) h e -> p t (h e)", p=P)).then_inc(k_in[b % 2], 16)
                    sp.dma_start(values[:, b], io["cache_mem_v"][0, b].rearrange("(t p) h e -> p t (h e)", p=P)).then_inc(v_in[b // 4], 16)
                sp.wait_ge(o_ok, STREAMS)
                sp.dma_start(scr["o"][STEP].rearrange("p m n -> p (m n)"), ot[:].rearrange("p m j b -> p (m j b)")).then_inc(stored, 16)
                sp.wait_ge(stored, 16)

            @block.gpsimd
            def _(pool):
                identity_matrix(nc, pool, ident, ident0, ident_ok)
                nc.gpsimd.memset(qs[:, :, :, STEP:RB], 0.0).then_inc(zero_ok, 1)

            @block.scalar
            def _(act):
                def take_keys(b):
                    for c in range(4):
                        act.wait_ge(kT_tr, 4 * b + c + 1)
                        if b >= 2:
                            act.wait_ge(sc_mm, b - 1)
                        nc.scalar.activation(kT[:, b % 2, 2 * c:2 * c + 2].rearrange("p k n -> p (k n)"), tr[:, c], ACT.Copy).then_inc(kT_ok, 1)
                for half in range(2):
                    for b in range(4 * half, 4 * half + 4):
                        take_keys(b)
                    act.wait_ge(ntop_ok, half + 1)
                    for hd in range(HEADS):
                        cols = slice(hd * MEM, (hd + 1) * MEM)
                        nc.scalar.activation(prob[:, half, cols], score[:, hd // 2, (hd % 2) * MEM:(hd % 2 + 1) * MEM], ACT.Exp,
                                             bias=ntop[:, half, hd:hd + 1], scale=SCALE, accum_out=den[:, half, hd:hd + 1]).then_inc(exp_ok, 1)

            @block.vector
            def _(dve):
                dve.wait_ge(q_in, 16)
                for b in range(STREAMS):
                    nc.vector.tensor_copy(qs[:, :, b, 0:STEP], q[:].rearrange("p k (j b) -> p k j b", b=STREAMS)[:, :, :, b]).then_inc(qs_ok, 1)
                for half in range(2):
                    dve.wait_ge(sc_mm, 4 * (half + 1))
                    nc.vector.reduce_max(top[:, half], score[:].rearrange("p a (b n) -> p (a b) n", b=2), AX_X).then_inc(top_ok, 1)
                    dve.wait_ge(top_ok, half + 1)
                    nc.vector.tensor_scalar(ntop[:, half], top[:, half], -SCALE, None, ALU.mult).then_inc(ntop_ok, 1)
                    dve.wait_ge(exp_ok, HEADS * (half + 1))
                    nc.vector.reciprocal(rden[:, half], den[:, half]).then_inc(rden_ok, 1)
                    dve.wait_ge(rden_ok, half + 1)
                    for hd in range(HEADS):
                        cols = prob[:, half, hd * MEM:(hd + 1) * MEM]
                        nc.vector.tensor_scalar(cols, cols, rden[:, half, hd:hd + 1], None, ALU.mult).then_inc(prob_ok, 1)
                    for a in range(2):
                        dve.wait_ge(p_tr, 2 * half + a + 1)
                        nc.vector.tensor_copy(pt[:, half, 4 * a:4 * a + 4].rearrange("p k n -> p (k n)"), o_ps[:, a]).then_inc(pt_ok, 1)
                    for s in range(4):
                        b = 4 * half + s
                        dve.wait_ge(o_mm, b + 1)
                        nc.vector.tensor_copy(ot[:, :, :, b], o_ps[:, s % 2, 0:KD * STEP].rearrange("p (m j) -> p m j", m=KD)).then_inc(o_ok, 1)

            @block.tensor
            def _(pe):
                pe.wait_ge(ident_ok, 1)
                pe.wait_ge(zero_ok, 1)
                pe.wait_ge(qs_ok, STREAMS)

                def turn_keys(b):
                    pe.wait_ge(k_in[b % 2], 16 * (b // 2 + 1))
                    for c in range(4):
                        if b >= 1:
                            pe.wait_ge(kT_ok, 4 * (b - 1) + c + 1)
                        for k in (2 * c, 2 * c + 1):
                            for t in range(2):
                                ins = nc.tensor.transpose(tr[:, c, (k % 2) * MEM + t * P:(k % 2) * MEM + (t + 1) * P],
                                                          keys[:, b % 2, t, k * P:(k + 1) * P], ident[:])
                        ins.then_inc(kT_tr, 1)

                turn_keys(0)
                for half in range(2):
                    for s in range(4):
                        b = 4 * half + s
                        if b + 1 < STREAMS:
                            turn_keys(b + 1)
                        pe.wait_ge(kT_ok, 4 * (b + 1))
                        if half and s == 0:
                            pe.wait_ge(exp_ok, HEADS)
                        rows = slice(RB * s, RB * s + RB)
                        for hd in range(HEADS):
                            for k in (2 * hd, 2 * hd + 1):
                                ins = nc.tensor.matmul(score[rows, hd // 2, (hd % 2) * MEM:(hd % 2 + 1) * MEM], qs[:, k, b],
                                                       kT[:, b % 2, k], start=k % 2 == 0, stop=k % 2 == 1)
                        ins.then_inc(sc_mm, 1)
                    pe.wait_ge(prob_ok, HEADS * (half + 1))
                    for a in range(2):
                        if half:
                            pe.wait_ge(o_ok, 3 + a)
                        for k in range(4 * a, 4 * a + 4):
                            ins = nc.tensor.transpose(o_ps[:, a, (k % 4) * P:(k % 4 + 1) * P], prob[:, half, k * P:(k + 1) * P], ident[:])
                        ins.then_inc(p_tr, 1)
                    pe.wait_ge(pt_ok, 2 * (half + 1))
                    pe.wait_ge(v_in[half], 16 * 4)
                    for s in range(4):
                        b = 4 * half + s
                        if s >= 2:
                            pe.wait_ge(o_ok, b - 1)
                        for m in range(KD):
                            for t in range(2):
                                ins = nc.tensor.matmul(o_ps[:, s % 2, m * STEP:(m + 1) * STEP], values[:, b, t, m * P:(m + 1) * P],
                                                       pt[:, half, (m // 2) * 2 + t, RB * s:RB * s + STEP], start=t == 0, stop=t == 1)
                        ins.then_inc(o_mm, 1)


def mlp(nc, outer, io, scr):
    sem = lambda n: outer.new("s9_" + n)
    FC = 256
    FT = FC // P
    CHUNKS = FF // FC
    BM = 3
    WB = BM * P
    GROUP = 9
    J = GROUP // BM
    with ExitStack() as ctx:
        room = Room(nc, ctx, "s9")
        sb, ps = room.sb, room.ps
        g = sb("g", [P, KD])
        g_last = sb("g_last", [P, D])
        expo = sb("expo", [P, 1])
        stat = sb("stat", [P, 3, GROUP])
        xs = sb("xs", [P, GROUP, D])
        h_hi, h_lo = sb("h_hi", [P, GROUP, KD, P], F32R), sb("h_lo", [P, GROUP, KD, P], F32R)
        up_raw, dn_raw = sb("up_raw", [P, KD, FC]), sb("dn_raw", [P, FT, D])
        up_hi, up_lo = sb("up_hi", [P, 2, KD, FC], F32R), sb("up_lo", [P, 2, KD, FC], F32R)
        dn_hi, dn_lo = sb("dn_hi", [P, 2, FT, D], F32R), sb("dn_lo", [P, 2, FT, D], F32R)
        r = sb("r", [P, FT, WB])
        a_hi, a_lo = sb("a_hi", [P, 2, FT, WB], F32R), sb("a_lo", [P, 2, FT, WB], F32R)
        up_ps = ps("up", [P, 4, 512])
        dn_ps = ps("dn", [P, 2, 2, 512])

        g_in, gl_in = sem("g_in"), sem("gl_in")
        h_in, x_in, y_st = ([sem(f"{n}{t}") for t in range(GROUP)] for n in ("h_in", "x_in", "y_st"))
        hhi_ok, hlo_ok = sem("hhi"), sem("hlo")
        up_in, dn_in, uphi_ok, uplo_ok, dnhi_ok, dnlo_ok = (sem(n) for n in ("up_in", "dn_in", "uphi", "uplo", "dnhi", "dnlo"))
        up_mm, relu_ok, sq_ok, ahi_ok, alo_ok, dn_mm, sum_ok = (
            sem(n) for n in ("up_mm", "relu", "sq", "ahi", "alo", "dn_mm", "sum"))
        expo_ok, sumsq, var, rstd, y_ok = sem("expo"), sem("sumsq"), sem("var"), sem("rstd"), sem("y")

        groups = [(0, GROUP), (GROUP, TILES - GROUP)]

        class Place:

            def __init__(self, gi, c, odd, j):
                self.t0, self.nt = groups[gi]
                self.sizes = [min(BM, self.nt - BM * i) for i in range(J)]
                self.gi, self.c, self.odd, self.j = gi, c, odd, j
                self.chunk = gi * CHUNKS + c
                self.block = self.chunk * J + j
                self.side = (odd * J + j) % 2
                self.before = sum(self.sizes[:j])
                self.tile = gi * CHUNKS * GROUP + c * self.nt + self.before
                self.size = self.sizes[j]
                self.wide = self.size * P
                self.early = isinstance(c, int) and c * J + j < 2

            def back(self, n):
                c, odd, j = self.c, self.odd, self.j - n
                while j < 0:
                    c, odd, j = c - 1, 1 - odd, j + J
                return Place(self.gi, c, odd, j)

            def tiles_two_blocks_ago(self):
                if self.early:
                    return self.gi * CHUNKS * GROUP
                p = self.back(2)
                return p.tile + p.size

        def over_chunks(eng, gi, body):
            for c in (0, 1):
                body(gi, c, c)
            with eng.Fori(1, CHUNKS // 2 - 1) as pair:
                for odd in range(2):
                    body(gi, 2 * pair + odd, odd)
            for c in (CHUNKS - 2, CHUNKS - 1):
                body(gi, c, c % 2)

        with nc.Block() as block:

            @block.sync
            def _(sp):
                up = io["w_up"][0].rearrange("(k p) (c f) -> c p k f", p=P, f=FC)
                down = io["w_down"][0].rearrange("(c t p) n -> c p t n", p=P, t=FT)
                yp = io["y_prompt"][0].rearrange("(c j) d -> j c d", j=STEP)
                ys = io["y_sample"].rearrange("b j d -> j b d")
                sp.dma_start(g[:], io["g_mlp"][0].rearrange("(k p) -> p k", p=P), allow_slow_non_contiguous=True).then_inc(g_in, 16)
                sp.dma_start(up_raw[:], up[0]).then_inc(up_in, 16)
                sp.dma_start(dn_raw[:], down[0]).then_inc(dn_in, 16)
                sp.dma_start(g_last[:], io["g_final"].partition_broadcast(P)).then_inc(gl_in, 16)
                for gi, (t0, nt) in enumerate(groups):
                    for t in range(nt):
                        if gi:
                            sp.wait_ge(y_st[t], 16)
                        sp.dma_start(xs[:, t].rearrange("p (k n) -> p k n", k=KD), scr["h2"][t0 + t]).then_inc(h_in[t], 16)
                    for t in range(nt):
                        sp.wait_ge(hlo_ok, t0 + t + 1)
                        sp.dma_start(xs[:, t], scr["x2"][t0 + t]).then_inc(x_in[t], 16)
                    with sp.Fori(1, CHUNKS) as c:
                        n = gi * CHUNKS + c
                        sp.wait_ge(uplo_ok, KD * n)
                        sp.dma_start(up_raw[:], up[c]).then_inc(up_in, 16)
                        sp.wait_ge(dnlo_ok, FT * n)
                        sp.dma_start(dn_raw[:], down[c]).then_inc(dn_in, 16)
                    if gi == 0:
                        sp.wait_ge(uplo_ok, KD * CHUNKS)
                        sp.dma_start(up_raw[:], up[0]).then_inc(up_in, 16)
                        sp.wait_ge(dnlo_ok, FT * CHUNKS)
                        sp.dma_start(dn_raw[:], down[0]).then_inc(dn_in, 16)
                    for t in range(nt):
                        sp.wait_ge(y_ok, t0 + t + 1)
                        sp.dma_start(yp[t0 + t] if t0 + t < STEP else ys, xs[:, t]).then_inc(y_st[t], 16)
                for t in range(GROUP):
                    sp.wait_ge(y_st[t], 32 if t < groups[1][1] else 16)

            @block.gpsimd
            def _(pool):
                nc.gpsimd.memset(expo[:], -0.5).then_inc(expo_ok, 1)
                pool.wait_ge(expo_ok, 1)
                for t0, nt in groups:
                    for t in range(nt):
                        pool.wait_ge(var, t0 + t + 1)
                        nc.gpsimd.tensor_tensor(stat[:, 2, t:t + 1], stat[:, 1, t:t + 1], expo[:], ALU.pow).then_inc(rstd, 1)

            @block.scalar
            def _(act):
                def split_up(gi, c, odd):
                    n = gi * CHUNKS + c
                    act.wait_ge(up_in, 16 * (n + 1))
                    if not isinstance(n, int) or n >= 2:
                        act.wait_ge(up_mm, FT * J * (n - 1))
                    for k in range(KD):
                        nc.scalar.activation(up_hi[:, odd, k], up_raw[:, k], ACT.Copy, scale=g[:, k:k + 1]).then_inc(uphi_ok, 1)

                def split_down(gi, c, odd):
                    n = gi * CHUNKS + c
                    act.wait_ge(dn_in, 16 * (n + 1))
                    if not isinstance(n, int) or n >= 2:
                        before = n * GROUP if gi == 0 else CHUNKS * GROUP + c * groups[1][1]
                        act.wait_ge(dn_mm, before - groups[gi][1] if not isinstance(c, int) or c >= 1 else before - GROUP)
                    for k in range(FT):
                        nc.scalar.activation(dn_hi[:, odd, k], dn_raw[:, k], ACT.Copy).then_inc(dnhi_ok, 1)

                def hidden(at):
                    for f in range(FT):
                        act.wait_ge(up_mm, FT * at.block + f + 1)
                        if not isinstance(at.block, int) or at.block >= 1:
                            act.wait_ge(alo_ok, FT * at.block + f - 1)
                        nc.scalar.activation(r[:, f, 0:at.wide], up_ps[:, 2 * at.side + f, 0:at.wide], ACT.Relu).then_inc(relu_ok, 1)
                    if at.gi or not at.early:
                        act.wait_ge(dn_mm, at.tiles_two_blocks_ago())
                    for f in range(FT):
                        act.wait_ge(sq_ok, FT * at.block + f + 1)
                        nc.scalar.activation(a_hi[:, at.side, f, 0:at.wide], r[:, f, 0:at.wide], ACT.Copy).then_inc(ahi_ok, 1)

                def chunk(gi, c, odd):
                    last = isinstance(c, int) and c == CHUNKS - 1
                    more = not (last and gi == 1)
                    following = (gi + 1, 0, 0) if last else (gi, c + 1, 1 - odd)
                    hidden(Place(gi, c, odd, 0))
                    if more:
                        split_up(*following)
                    hidden(Place(gi, c, odd, 1))
                    if more:
                        split_down(*following)
                    hidden(Place(gi, c, odd, 2))

                act.wait_ge(g_in, 16)
                split_up(0, 0, 0)
                split_down(0, 0, 0)
                for gi, (t0, nt) in enumerate(groups):
                    for t in range(nt):
                        act.wait_ge(h_in[t], 16 * (gi + 1))
                        nc.scalar.activation(h_hi[:, t].rearrange("p k n -> p (k n)"), xs[:, t], ACT.Copy).then_inc(hhi_ok, 1)
                    over_chunks(act, gi, chunk)
                    for t in range(nt):
                        act.wait_ge(sum_ok, gi * CHUNKS * GROUP + (CHUNKS - 1) * nt + t + 1)
                        act.wait_ge(sq_ok, FT * J * CHUNKS * (gi + 1))
                        if t0 + t:
                            act.wait_ge(sumsq, t0 + t)
                        nc.scalar.activation(up_ps[:, 0:2].rearrange("p a n -> p (a n)"), xs[:, t], ACT.Square,
                                             accum_out=stat[:, 0, t:t + 1]).then_inc(sumsq, 1)

            @block.vector
            def _(dve):
                def split_up(gi, c, odd):
                    n = gi * CHUNKS + c
                    for k in range(KD):
                        dve.wait_ge(uphi_ok, KD * n + k + 1)
                        nc.vector.scalar_tensor_tensor(up_lo[:, odd, k], up_raw[:, k], g[:, k:k + 1], up_hi[:, odd, k].bitcast(F32),
                                                       ALU.mult, ALU.subtract).then_inc(uplo_ok, 1)

                def split_down(gi, c, odd):
                    n = gi * CHUNKS + c
                    for k in range(FT):
                        dve.wait_ge(dnhi_ok, FT * n + k + 1)
                        nc.vector.tensor_tensor(dn_lo[:, odd, k], dn_raw[:, k], dn_hi[:, odd, k].bitcast(F32), ALU.subtract).then_inc(dnlo_ok, 1)

                def hidden(at):
                    for f in range(FT):
                        dve.wait_ge(relu_ok, FT * at.block + f + 1)
                        rf = r[:, f, 0:at.wide]
                        nc.vector.scalar_tensor_tensor(rf, up_ps[:, 2 * at.side + f, 0:at.wide], 0.0, rf, ALU.max, ALU.mult).then_inc(sq_ok, 1)
                    for f in range(FT):
                        dve.wait_ge(ahi_ok, FT * at.block + f + 1)
                        nc.vector.tensor_tensor(a_lo[:, at.side, f, 0:at.wide], r[:, f, 0:at.wide], a_hi[:, at.side, f, 0:at.wide].bitcast(F32),
                                                ALU.subtract).then_inc(alo_ok, 1)

                def sums(at):
                    for i in range(at.size):
                        t = at.before + i
                        dve.wait_ge(dn_mm, at.tile + i + 1)
                        if isinstance(at.c, int) and at.c == 0:
                            dve.wait_ge(x_in[t], 16 * (at.gi + 1))
                        else:
                            dve.wait_ge(sum_ok, at.tile + i + 1 - at.nt)
                        bank = (at.odd * at.nt + t) % 2
                        nc.vector.tensor_tensor(xs[:, t], xs[:, t], dn_ps[:, bank].rearrange("p a n -> p (a n)"), ALU.add).then_inc(sum_ok, 1)

                def chunk(gi, c, odd):
                    last = isinstance(c, int) and c == CHUNKS - 1
                    more = not (last and gi == 1)
                    following = (gi + 1, 0, 0) if last else (gi, c + 1, 1 - odd)
                    hidden(Place(gi, c, odd, 0))
                    if more:
                        split_up(*following)
                    if not isinstance(c, int) or c > 0:
                        sums(Place(gi, c, odd, 0).back(1))
                    hidden(Place(gi, c, odd, 1))
                    if more:
                        split_down(*following)
                    sums(Place(gi, c, odd, 0))
                    hidden(Place(gi, c, odd, 2))
                    sums(Place(gi, c, odd, 1))

                dve.wait_ge(g_in, 16)
                split_up(0, 0, 0)
                split_down(0, 0, 0)
                for gi, (t0, nt) in enumerate(groups):
                    for t in range(nt):
                        dve.wait_ge(hhi_ok, t0 + t + 1)
                        nc.vector.tensor_tensor(h_lo[:, t].rearrange("p k n -> p (k n)"), xs[:, t],
                                                h_hi[:, t].rearrange("p k n -> p (k n)").bitcast(F32), ALU.subtract).then_inc(hlo_ok, 1)
                    over_chunks(dve, gi, chunk)
                    sums(Place(gi, CHUNKS - 1, 1, 2))
                    dve.wait_ge(gl_in, 16)
                    for t in range(nt):
                        dve.wait_ge(sumsq, t0 + t + 1)
                        nc.vector.tensor_scalar(stat[:, 1, t:t + 1], stat[:, 0, t:t + 1], 1.0 / D, EPS, ALU.mult, ALU.add).then_inc(var, 1)
                        dve.wait_ge(rstd, t0 + t + 1)
                        nc.vector.scalar_tensor_tensor(xs[:, t], xs[:, t], stat[:, 2, t:t + 1], g_last[:], ALU.mult, ALU.mult).then_inc(y_ok, 1)

            @block.tensor
            def _(pe):
                def up(at):
                    if at.j == 0:
                        pe.wait_ge(uplo_ok, KD * (at.chunk + 1))
                    if not isinstance(at.block, int) or at.block >= 2:
                        pe.wait_ge(sq_ok, FT * (at.block - 1))
                    tiles = slice(at.before, at.before + at.size)
                    for f in range(FT):
                        for k in range(KD):
                            cols = slice(f * P, (f + 1) * P)
                            ins = product3(nc, up_ps[:, 2 * at.side + f, 0:at.wide], up_hi[:, at.odd, k, cols], up_lo[:, at.odd, k, cols],
                                           h_hi[:, tiles, k], h_lo[:, tiles, k], k == 0, k == KD - 1)
                        ins.then_inc(up_mm, 1)

                def down(at):
                    if at.j == 0:
                        pe.wait_ge(dnlo_ok, FT * (at.chunk + 1))
                    pe.wait_ge(alo_ok, FT * (at.block + 1))
                    for i in range(at.size):
                        bank = (at.odd * at.nt + at.before + i) % 2
                        if not isinstance(at.tile, int) or at.tile + i >= 2:
                            pe.wait_ge(sum_ok, at.tile + i - 1)
                        rows = slice(i * P, (i + 1) * P)
                        for a in range(2):
                            cols = slice(a * 512, (a + 1) * 512)
                            for f in range(FT):
                                ins = product3(nc, dn_ps[:, bank, a], a_hi[:, at.side, f, rows], a_lo[:, at.side, f, rows],
                                               dn_hi[:, at.odd, f, cols], dn_lo[:, at.odd, f, cols], f == 0, f == FT - 1)
                        ins.then_inc(dn_mm, 1)

                def chunk(gi, c, odd):
                    for j in range(J):
                        at = Place(gi, c, odd, j)
                        up(at)
                        if not isinstance(c, int) or c > 0 or j > 0:
                            down(at.back(1))

                for gi, (t0, nt) in enumerate(groups):
                    pe.wait_ge(hlo_ok, t0 + nt)
                    over_chunks(pe, gi, chunk)
                    down(Place(gi, CHUNKS - 1, 1, J - 1))


def program(nc, io):
    with Semaphores(nc) as outer:
        scr = {
            "kT": nc.dram_tensor("scr_kT", (P, KD, MEM), F32).ap(),
            "v": nc.dram_tensor("scr_v", (P, 2, D), F32).ap(),
            "injT": nc.dram_tensor("scr_injT", (P, PAIRS, 4, P), F32).ap(),
            "outm": nc.dram_tensor("scr_outm", (P, 2, PAIRS, STEP + 1, SG), F32).ap(),
            "taps": nc.dram_tensor("scr_taps", (SG, GROUPS, STEP, SG), F32).ap(),
        }
        scr["pow16"] = nc.dram_tensor("scr_pow16", (P, 2, PAIRS), F32).ap()
        scr["z"] = nc.dram_tensor("scr_z", (KD, P, STEP, NC), F32).ap()
        scr["y"] = nc.dram_tensor("scr_y", (4, P, STEP, NC), F32).ap()
        scr["c"] = nc.dram_tensor("scr_c", (TILES, P, KD, P), F32).ap()
        memory_and_tables(nc, outer, io, scr)
        first_input_projection(nc, outer, io, scr)
        mixers(nc, outer, io, scr)
        pooling(nc, outer, io, scr)
        for name in ("h", "q", "o", "h2"):
            scr[name] = nc.dram_tensor("scr_" + name, (TILES, P, KD, P), F32).ap()
        for name in ("x1", "x2"):
            scr[name] = nc.dram_tensor("scr_" + name, (TILES, P, D), F32).ap()
        xp, xs = io["x_prompt"][0].rearrange("(c j) d -> j c d", j=STEP), io["x_sample"].rearrange("b j d -> j b d")
        gelu_glu(nc, outer, io, scr)
        outer.clear()
        output_projection(nc, outer, io, scr, "s5", "w_out", scr["c"], lambda t: xs if isinstance(t, int) and t == STEP else xp[t],
                          scr["x1"], scr["h"])
        query_projection(nc, outer, io, scr)
        prompt_attention(nc, outer, io, scr)
        stream_attention(nc, outer, io, scr)
        outer.clear()
        output_projection(nc, outer, io, scr, "s8", "w_o", scr["o"], lambda t: scr["x1"][t], scr["x2"], scr["h2"])
        mlp(nc, outer, io, scr)


_INS = ["x_prompt", "x_sample", "cache_mem_k", "cache_mem_v", "state_pool", "state_ssm_re", "state_ssm_im", "mem_prompt",
        "g_mix", "w_in", "w_pool", "pool_scale", "ssm_a_re", "ssm_a_im", "ssm_b_re", "ssm_b_im", "ssm_c_re", "ssm_c_im",
        "ssm_d", "ssm_log_dt", "w_glu", "b_glu", "w_out", "g_xattn", "g_mem", "w_q", "w_k", "w_v", "w_o", "g_mlp",
        "w_up", "w_down", "g_final"]
_OUTS = {
    "y_prompt": (1, SEQ, D), "y_sample": (STREAMS, STEP, D), "new_mem_k": (1, 1, MEM, HEADS, HD), "new_mem_v": (1, 1, MEM, HEADS, HD),
    "new_pool_p": (1, 1, HIST, DP), "new_ssm_re_p": (1, 1, GROUPS, SS), "new_ssm_im_p": (1, 1, GROUPS, SS),
    "new_pool_s": (1, STREAMS, HIST, DP), "new_ssm_re_s": (1, STREAMS, GROUPS, SS), "new_ssm_im_s": (1, STREAMS, GROUPS, SS),
}


def kernel(**inputs):
    import numpy as np
    import concourse.bacc as bacc
    from concourse.bass_utils import run_bass_kernel_spmd

    nc = bacc.Bacc("TRN2", target_bir_lowering=False, num_devices=1)
    arrays, io = {}, {}
    for name in _INS:
        a = np.ascontiguousarray(inputs[name])
        arrays[f"in_{name}_dram"] = a
        io[name] = nc.dram_tensor(f"in_{name}_dram", a.shape, mybir.dt.from_np(a.dtype), kind="ExternalInput").ap()
    for name, shape in _OUTS.items():
        io[name] = nc.dram_tensor(f"out_{name}_dram", shape, F32, kind="ExternalOutput").ap()
    program(nc, io)
    got = run_bass_kernel_spmd(nc, [arrays], core_ids=[0]).results[0]
    return tuple(got[f"out_{name}_dram"] for name in _OUTS)
```

```python
import math
from contextlib import ExitStack

import concourse.bass as bass
from concourse import mybir

F32 = mybir.dt.float32
F32R = mybir.dt.float32r
I32 = mybir.dt.int32
ALU = mybir.AluOpType
ACT = mybir.ActivationFunctionType
AX_X = mybir.AxisListType.X

P = 128
D = 1024
KD = D // P
SEQ = 2048
STREAMS = 8
STEP = 16
CH = SEQ // STEP
NC = CH + STREAMS
TILES = STEP + 1
DP = D // 2
GROUPS = 32
SG = 16
SS = 64
PAIRS = GROUPS // 2
HIST = 15
MEM = 256
HEADS = 4
HD = D // HEADS
FF = 4 * D
EPS = 1e-6
BT = 4
LN2_HI = 0.693359375
LN2_LO = math.log(2.0) - LN2_HI
TWO_PI_A = 6.28125
TWO_PI_B = 0.001934051513671875
TWO_PI_C = 2 * math.pi - TWO_PI_A - TWO_PI_B
MAGIC = 1.5 * 2.0 ** 23


class Room:

    def __init__(self, nc, ctx, tag):
        self.nc, self.ctx, self.tag = nc, ctx, tag

    def sb(self, name, shape, dt=F32):
        return self.ctx.enter_context(self.nc.sbuf_tensor(f"{self.tag}_{name}", shape, dt))

    def ps(self, name, shape, dt=F32):
        return self.ctx.enter_context(self.nc.psum_tensor(f"{self.tag}_ps_{name}", shape, dt))


class Semaphores:

    def __init__(self, nc):
        self.nc, self.held = nc, []

    def __enter__(self):
        return self

    def __exit__(self, *error):
        return False

    def new(self, name):
        self.held.append(self.nc.alloc_semaphore(name=name))
        return self.held[-1]

    def clear(self):
        self.nc.clear_and_free_semaphores(self.held)
        self.nc.all_engine_barrier()
        self.held = []


def product3(nc, out, w_hi, w_lo, x_hi, x_lo, first, last):
    nc.tensor.matmul(out, w_hi, x_hi, start=first, stop=False)
    nc.tensor.matmul(out, w_hi, x_lo, start=False, stop=False)
    return nc.tensor.matmul(out, w_lo, x_hi, start=False, stop=last)


def identity_matrix(nc, pool, ident, filled, done):
    nc.gpsimd.memset(ident[:], 0.0).then_inc(filled, 1)
    pool.wait_ge(filled, 1)
    nc.gpsimd.affine_select(out=ident[:], in_=ident[:], compare_op=ALU.not_equal, fill=1.0, base=0,
                            pattern=[[-1, P]], channel_multiplier=1).then_inc(done, 1)


def memory_and_tables(nc, outer, io, scr):
    sem = lambda n: outer.new("s1_" + n)
    with ExitStack() as ctx:
        room = Room(nc, ctx, "s1")
        sb, ps = room.sb, room.ps
        ident = sb("ident", [P, P])
        memx = sb("memx", [P, 2, D])
        memn = sb("memn", [P, 2, D])
        memT = sb("memT", [P, KD, MEM])
        kv = sb("kv", [P, 2, 2, D])
        kT = sb("kT", [P, KD, MEM])
        g_mem = sb("g_mem", [P, KD])
        wring = sb("wring", [P, 4, D])
        pn = sb("pn", [P, P])
        ldt = sb("ldt", [P, 2])
        pt = sb("pt", [P, P])
        braw = sb("braw", [P, 2, PAIRS, SG])
        cnat = sb("cnat", [P, 2, 2, P])
        ct = sb("ct", [P, 2, PAIRS, SG])
        bbar = sb("bbar", [P, 2, PAIRS, SG])
        powers = sb("powers", [P, 2, PAIRS, STEP + 1])
        small = sb("small", [P, 32, PAIRS])
        turn = sb("turn", [P, 3, PAIRS])
        smalli = sb("smalli", [P, PAIRS], I32)
        stat = sb("stat", [P, 8])
        expo = sb("expo", [P, 1])
        inj = sb("inj", [P, 2, PAIRS, STEP, SG])
        outm = sb("outm", [P, 2, PAIRS, STEP + 1, SG])
        work = sb("work", [P, 2, PAIRS, STEP + 1, SG])
        injT = sb("injT", [P, 2, 4, P])
        taps = sb("taps", [SG, 2, 2, STEP, SG])
        acc = ps("acc", [P, 4, 512])
        tr = ps("tr", [P, 4, 512])

        ldt_in, ldt_ok = sem("ldt_in"), sem("ldt")
        ident0, ident_ok, mem_in, par_in, gm_in = (sem(n) for n in ("ident0", "ident", "mem_in", "par_in", "gm_in"))
        w_in, w_free = [sem(f"w_in{i}") for i in range(4)], sem("w_free")
        cleared, sumsq, var, rstd, memn_ok = (sem(n) for n in ("cleared", "sumsq", "var", "rstd", "memn"))
        memT_tr, memT_ok, kv_ok, kT_tr, kT_ok = (sem(n) for n in ("memT_tr", "memT", "kv", "kT_tr", "kT"))
        par_tr, par_ok, ang_ok, sin_ok = (sem(n) for n in ("par_tr", "par", "ang", "sin"))
        c_tr, c_ok, inj_ok, outm_ok = (sem(n) for n in ("c_tr", "c_ok", "inj", "outm"))
        injT_tr, injT_ok, tap_mm, tap_ok, tap_st = (sem(n) for n in ("injT_tr", "injT", "tap_mm", "tap", "tap_st"))
        injT_st = [sem(f"injT_st{i}") for i in range(2)]
        chain, stored = sem("chain"), sem("stored")

        def weight_slice(n):
            w = io["w_k"] if n < KD else io["w_v"]
            return w[0].rearrange("(k p) n -> k p n", p=P)[n % KD]

        with nc.Block() as block:

            @block.sync
            def _(sp):
                sp.wait_ge(cleared, 1)
                sp.dma_start(pn[0:PAIRS, :], io["ssm_a_re"][0].rearrange("(q t) s -> q (t s)", t=2)).then_inc(par_in, 16)
                sp.dma_start(pn[32:32 + PAIRS, :], io["ssm_a_im"][0].rearrange("(q t) s -> q (t s)", t=2)).then_inc(par_in, 16)
                sp.dma_start(ldt[64:64 + PAIRS, :], io["ssm_log_dt"][0].rearrange("(q t) -> q t", t=2)).then_inc(ldt_in, 16)
                for t in range(2):
                    sp.dma_start(memx[:, t], io["mem_prompt"][0, t * P:(t + 1) * P]).then_inc(mem_in, 16)
                for part, name in enumerate(("ssm_c_re", "ssm_c_im")):
                    c = io[name][0].rearrange("(x q t) h s -> x q h t s", x=2, t=2)
                    for x in range(2):
                        for q in range(8):
                            sp.dma_start(cnat[q * SG:(q + 1) * SG, part, x].rearrange("h (t s) -> h t s", t=2),
                                         c[x, q]).then_inc(par_in, 16)
                for part, name in enumerate(("ssm_b_re", "ssm_b_im")):
                    sp.dma_start(braw[:, part], io[name][0].rearrange("(q t) s h -> (t s) q h", t=2)).then_inc(par_in, 16)
                sp.dma_start(g_mem[:], io["g_mem"][0].rearrange("(k p) -> p k", p=P), allow_slow_non_contiguous=True).then_inc(gm_in, 16)
                for n in range(2 * KD):
                    if n >= 4:
                        sp.wait_ge(w_free, n - 3)
                    sp.dma_start(wring[:, n % 4], weight_slice(n)).then_inc(w_in[n % 4], 16)
                for m, name in enumerate(("new_mem_k", "new_mem_v")):
                    sp.wait_ge(kv_ok, 4 * (m + 1))
                    sp.dma_start(io[name].rearrange("l b (t p) h e -> p (l b t) (h e)", p=P), kv[:, m]).then_inc(stored, 16)
                sp.dma_start(scr["v"], kv[:, 1]).then_inc(stored, 16)
                sp.wait_ge(kT_ok, KD)
                sp.dma_start(scr["kT"], kT[:]).then_inc(stored, 16)
                sp.wait_ge(outm_ok, 1)
                sp.dma_start(scr["pow16"], powers[:, :, :, STEP], allow_slow_non_contiguous=True).then_inc(stored, 16)
                sp.dma_start(scr["turn"], turn[:]).then_inc(stored, 16)
                sp.dma_start(scr["outm"], outm[:]).then_inc(stored, 16)
                for n in range(PAIRS):
                    sp.wait_ge(injT_ok, n + 1)
                    sp.dma_start(scr["injT"][:, n], injT[:, n % 2]).then_inc(injT_st[n % 2], 16)
                for n in range(GROUPS // 4):
                    sp.wait_ge(tap_ok, 2 * (n + 1))
                    sp.dma_start(scr["taps"][:, 4 * n:4 * n + 4], taps[:].rearrange("h a b k c -> h (a b) k c")).then_inc(tap_st, 16)
                sp.wait_ge(stored, 7 * 16)
                for i in range(2):
                    sp.wait_ge(injT_st[i], PAIRS // 2 * 16)
                sp.wait_ge(tap_st, GROUPS // 4 * 16)

            @block.gpsimd
            def _(pool):
                nc.gpsimd.memset(expo[:], -0.5)
                identity_matrix(nc, pool, ident, ident0, ident_ok)
                for t in range(2):
                    pool.wait_ge(var, t + 1)
                    nc.gpsimd.tensor_tensor(stat[:, 4 + t:5 + t], stat[:, 2 + t:3 + t], expo[:], ALU.pow).then_inc(rstd, 1)

            @block.scalar
            def _(act):
                for t in range(2):
                    act.wait_ge(mem_in, 32)
                    nc.scalar.activation(memn[:, t], memx[:, t], ACT.Square, accum_out=stat[:, t:t + 1]).then_inc(sumsq, 1)
                act.wait_ge(gm_in, 16)
                for k in range(KD):
                    act.wait_ge(memT_tr, k // 2 + 1)
                    src = tr[:, k // 2].rearrange("p (a n) -> p a n", a=2)[:, k % 2]
                    nc.scalar.activation(memT[:, k], src, ACT.Copy, scale=g_mem[:, k:k + 1]).then_inc(memT_ok, 1)
                act.wait_ge(ang_ok, 1)
                nc.scalar.activation(small[:, 12], small[:, 10], ACT.Sin).then_inc(sin_ok, 1)
                nc.scalar.activation(small[:, 13], small[:, 11], ACT.Sin).then_inc(sin_ok, 1)
                for m in range(2):
                    act.wait_ge(w_free, (m + 1) * KD)
                    for t in range(2):
                        for h in range(2):
                            nc.scalar.activation(kv[:, m, t, h * 512:(h + 1) * 512], acc[:, 2 * t + h], ACT.Copy).then_inc(kv_ok, 1)
                for k in range(KD):
                    act.wait_ge(kT_tr, k // 2 + 1)
                    src = acc[:, k // 2].rearrange("p (a n) -> p a n", a=2)[:, k % 2]
                    nc.scalar.activation(kT[:, k], src, ACT.Copy).then_inc(kT_ok, 1)
                for n in range(PAIRS):
                    act.wait_ge(injT_tr, n + 1)
                    if n >= 2:
                        act.wait_ge(injT_st[n % 2], 16 * (n // 2))
                    nc.scalar.activation(injT[:, n % 2], tr[:, n % 4].rearrange("p (a n) -> p a n", a=4), ACT.Copy).then_inc(injT_ok, 1)
                for n in range(GROUPS // 4):
                    if n >= 1:
                        act.wait_ge(tap_st, 16 * n)
                    act.wait_ge(tap_mm, n + 1)
                    for t in range(2):
                        b = 2 * (n % 2) + t
                        nc.scalar.activation(taps[:, :, t], acc[0:SG, b].rearrange("h (a k c) -> h a k c", a=2, c=SG),
                                             ACT.Copy).then_inc(tap_ok, 1)

            @block.vector
            def _(dve):
                links = [0]

                def then(*instructions):
                    for ins in instructions:
                        ins.then_inc(chain, 1)
                    links[0] += len(instructions)
                    dve.wait_ge(chain, links[0])

                tt, ts, stt = nc.vector.tensor_tensor, nc.vector.tensor_scalar, nc.vector.scalar_tensor_tensor
                nc.vector.memset(pn[:], 0.0).then_inc(cleared, 1)
                dve.wait_ge(ldt_in, 16)
                dve.wait_ge(cleared, 1)
                for t in range(2):
                    ins = nc.vector.tensor_copy(pn[64:64 + PAIRS, t * SS:(t + 1) * SS],
                                                ldt[64:64 + PAIRS, t:t + 1].to_broadcast([PAIRS, SS]))
                ins.then_inc(ldt_ok, 1)
                for t in range(2):
                    dve.wait_ge(sumsq, t + 1)
                    ts(stat[:, 2 + t:3 + t], stat[:, t:t + 1], 1.0 / D, EPS, ALU.mult, ALU.add).then_inc(var, 1)
                for t in range(2):
                    dve.wait_ge(rstd, t + 1)
                    ts(memn[:, t], memx[:, t], stat[:, 4 + t:5 + t], None, ALU.mult).then_inc(memn_ok, 1)
                dve.wait_ge(par_tr, 1)
                then(nc.vector.tensor_copy(pt[:], acc[:, 3, 0:P]))
                a_re, a_im, log_dt = pt[:, 0:PAIRS], pt[:, 32:32 + PAIRS], pt[:, 64:64 + PAIRS]
                S = lambda n: small[:, n]

                def exp_parts(x):
                    then(ts(S(0), x, 88.0, -87.0, ALU.min, ALU.max))
                    then(ts(S(1), S(0), 1.0 / math.log(2.0), MAGIC, ALU.mult, ALU.add))
                    then(ts(S(1), S(1), -MAGIC, None, ALU.add))
                    then(stt(S(0), S(1), -LN2_HI, S(0), ALU.mult, ALU.add))
                    then(stt(S(0), S(1), -LN2_LO, S(0), ALU.mult, ALU.add))
                    then(ts(smalli[:], S(1), 127.0, None, ALU.add))
                    then(ts(small[:, 2].bitcast(I32), smalli[:], 23, None, ALU.logical_shift_left))
                    then(ts(S(3), S(0), 1.0 / math.factorial(8), None, ALU.mult))
                    for n in range(7, 0, -1):
                        then(stt(S(3), S(3), 1.0 / math.factorial(n), S(0), ALU.add, ALU.mult))

                exp_parts(log_dt)
                then(stt(S(4), S(3), 1.0, S(2), ALU.add, ALU.mult))
                then(tt(S(5), a_re, S(4), ALU.mult), tt(S(6), a_im, S(4), ALU.mult))
                then(ts(S(7), S(6), 1.0 / (2 * math.pi), MAGIC, ALU.mult, ALU.add))
                then(ts(S(7), S(7), -MAGIC, None, ALU.add))
                then(stt(S(8), S(7), -TWO_PI_A, S(6), ALU.mult, ALU.add))
                then(stt(S(8), S(7), -TWO_PI_B, S(8), ALU.mult, ALU.add))
                then(stt(S(8), S(7), -TWO_PI_C, S(8), ALU.mult, ALU.add))
                then(ts(S(10), S(8), 0.5, math.pi / 2, ALU.mult, ALU.min))
                then(ts(S(10), S(10), -math.pi / 2, None, ALU.max))
                then(stt(S(9), S(10), -1.0, S(10), ALU.mult, ALU.max))
                then(ts(S(11), S(9), -1.0, math.pi / 2, ALU.mult, ALU.add))
                dve.sem_inc(ang_ok, 1)
                exp_parts(S(5))
                then(tt(S(15), S(2), S(3), ALU.mult), ts(S(16), S(2), -1.0, None, ALU.add))
                then(tt(S(15), S(15), S(16), ALU.add))
                dve.wait_ge(sin_ok, 2)
                then(stt(S(17), S(12), -2.0, S(12), ALU.mult, ALU.mult), stt(S(18), S(12), 2.0, S(13), ALU.mult, ALU.mult))
                then(ts(S(19), S(17), 1.0, None, ALU.add), ts(S(20), S(15), 1.0, None, ALU.add))
                then(tt(S(21), S(15), S(19), ALU.mult), tt(S(22), S(20), S(18), ALU.mult))
                then(tt(S(21), S(21), S(17), ALU.add))
                pw = lambda part, k: powers[:, part, :, k]
                then(nc.vector.memset(pw(0, 0), 1.0), nc.vector.memset(pw(1, 0), 0.0),
                     ts(pw(0, 1), S(21), 1.0, None, ALU.add), ts(pw(1, 1), S(22), 1.0, None, ALU.mult))
                size, cosine, sine = (turn[:, i] for i in range(3))
                then(tt(size, S(20), S(20), ALU.mult), ts(cosine, S(19), 1.0, None, ALU.mult), ts(sine, S(18), 1.0, None, ALU.mult))
                for n in range(4):
                    then(tt(S(23), cosine, cosine, ALU.mult), tt(S(24), sine, sine, ALU.mult), tt(S(25), cosine, sine, ALU.mult))
                    then(tt(cosine, S(23), S(24), ALU.subtract), ts(sine, S(25), 2.0, None, ALU.mult))
                    then(tt(S(23), cosine, cosine, ALU.mult), tt(S(24), sine, sine, ALU.mult))
                    then(tt(S(23), S(23), S(24), ALU.add))
                    then(ts(S(23), S(23), -0.5, 1.5, ALU.mult, ALU.add))
                    then(tt(cosine, cosine, S(23), ALU.mult), tt(sine, sine, S(23), ALU.mult))
                    if n:
                        then(tt(size, size, size, ALU.mult))
                then(tt(S(23), a_re, a_re, ALU.mult), tt(S(24), a_im, a_im, ALU.mult))
                then(tt(S(23), S(23), S(24), ALU.add))
                then(nc.vector.reciprocal(S(23), S(23)))
                then(tt(S(24), S(21), a_re, ALU.mult), tt(S(25), S(22), a_im, ALU.mult),
                     tt(S(26), S(22), a_re, ALU.mult), tt(S(27), S(21), a_im, ALU.mult))
                then(tt(S(24), S(24), S(25), ALU.add), tt(S(26), S(26), S(27), ALU.subtract))
                then(tt(S(28), S(24), S(23), ALU.mult), tt(S(29), S(26), S(23), ALU.mult))

                def times(out, x, y, flip=1.0):
                    shape = x[0].shape
                    size = 1
                    for s in shape[1:]:
                        size *= s

                    def like(flat):
                        if len(shape) == 2:
                            return flat
                        if len(shape) == 3:
                            return flat.rearrange("p (a b) -> p a b", a=shape[1])
                        return flat.rearrange("p (a b c) -> p a b c", a=shape[1], b=shape[2])
                    scratch = work[:].rearrange("p r a b c -> p (r a b c)")
                    t0, t1 = like(scratch[:, 0:size]), like(scratch[:, size:2 * size])
                    then(tt(t0, x[0], y[0], ALU.mult), tt(t1, x[1], y[1], ALU.mult))
                    then(tt(out[0], t0, t1, ALU.subtract))
                    then(tt(t0, x[0], y[1], ALU.mult), tt(t1, x[1], y[0], ALU.mult))
                    if flip == 1.0:
                        then(tt(out[1], t0, t1, ALU.add))
                    else:
                        flat = lambda v: v.rearrange("p a b c -> p (a b c)") if len(shape) == 4 else v
                        then(stt(flat(out[1]), flat(t0), -1.0, flat(t1), ALU.mult, ALU.subtract))

                k = 1
                while k < STEP:
                    y = [powers[:, part, :, k:k + 1].to_broadcast([P, PAIRS, k]) for part in range(2)]
                    times([powers[:, part, :, k + 1:2 * k + 1] for part in range(2)],
                          [powers[:, part, :, 1:k + 1] for part in range(2)], y)
                    k *= 2
                dve.wait_ge(par_in, 36 * 16)
                f = [S(28 + part).unsqueeze(2).to_broadcast([P, PAIRS, SG]) for part in range(2)]
                times([bbar[:, part] for part in range(2)], [braw[:, part] for part in range(2)], f)
                dve.wait_ge(c_tr, 1)
                then(*(nc.vector.tensor_copy(ct[:, part, 8 * x:8 * x + 8], tr[:, 2 * part + x, 0:P].rearrange("p (q h) -> p q h", h=SG))
                       for part in range(2) for x in range(2)))
                bb = [bbar[:, part].unsqueeze(2).to_broadcast([P, PAIRS, STEP, SG]) for part in range(2)]
                pr = [bass.AP(tensor=powers, offset=part * PAIRS * (STEP + 1) + STEP - 1,
                              ap=[[2 * PAIRS * (STEP + 1), P], [STEP + 1, PAIRS], [-1, STEP], [0, SG]]) for part in range(2)]
                times([inj[:, part] for part in range(2)], pr, bb)
                dve.sem_inc(inj_ok, 1)
                cc = [ct[:, part].unsqueeze(2).to_broadcast([P, PAIRS, STEP + 1, SG]) for part in range(2)]
                pf = [powers[:, part].unsqueeze(3).to_broadcast([P, PAIRS, STEP + 1, SG]) for part in range(2)]
                times([outm[:, part] for part in range(2)], pf, cc, flip=-1.0)
                dve.sem_inc(outm_ok, 1)

            @block.tensor
            def _(pe):
                pe.wait_ge(ident_ok, 1)
                for k in range(KD):
                    for t in range(2):
                        pe.wait_ge(memn_ok, t + 1)
                        ins = nc.tensor.transpose(tr[:, k // 2, (k % 2) * MEM + t * P:(k % 2) * MEM + (t + 1) * P],
                                                  memn[:, t, k * P:(k + 1) * P], ident[:])
                    if k % 2:
                        ins.then_inc(memT_tr, 1)
                pe.wait_ge(par_in, 36 * 16)
                pe.wait_ge(ldt_ok, 1)
                nc.tensor.transpose(acc[:, 3, 0:P], pn[:], ident[:]).then_inc(par_tr, 1)
                pe.wait_ge(memT_ok, KD)
                for part in range(2):
                    for x in range(2):
                        ins = nc.tensor.transpose(tr[:, 2 * part + x, 0:P], cnat[:, part, x], ident[:])
                ins.then_inc(c_tr, 1)
                pe.wait_ge(ang_ok, 1)
                for m in range(2):
                    if m:
                        pe.wait_ge(kv_ok, 4)
                    for k in range(KD):
                        n = m * KD + k
                        pe.wait_ge(w_in[n % 4], 16 * (n // 4 + 1))
                        for t in range(2):
                            for h in range(2):
                                ins = nc.tensor.matmul(acc[:, 2 * t + h], memT[:, k, t * P:(t + 1) * P],
                                                       wring[:, n % 4, h * 512:(h + 1) * 512], start=k == 0, stop=k == KD - 1)
                        ins.then_inc(w_free, 1)
                pe.wait_ge(kv_ok, 8)
                for k in range(KD):
                    for t in range(2):
                        ins = nc.tensor.transpose(acc[:, k // 2, (k % 2) * MEM + t * P:(k % 2) * MEM + (t + 1) * P],
                                                  kv[:, 0, t, k * P:(k + 1) * P], ident[:])
                    if k % 2:
                        ins.then_inc(kT_tr, 1)
                pe.wait_ge(inj_ok, 1)
                for n in range(PAIRS):
                    if n >= 4:
                        pe.wait_ge(injT_ok, n - 3)
                    for part in range(2):
                        for jh in range(2):
                            ins = nc.tensor.transpose(tr[:, n % 4, (2 * part + jh) * P:(2 * part + jh + 1) * P],
                                                      inj[:, part, n, 8 * jh:8 * jh + 8].rearrange("p j h -> p (j h)"), ident[:])
                    ins.then_inc(injT_tr, 1)
                pe.wait_ge(outm_ok, 1)
                pe.wait_ge(kT_ok, KD)
                for n in range(GROUPS // 4):
                    if n >= 2:
                        pe.wait_ge(tap_ok, 2 * (n - 1))
                    for a in range(2):
                        for t in range(2):
                            for part in range(2):
                                q = 2 * n + a
                                rows = slice(t * SS, (t + 1) * SS)
                                ins = nc.tensor.matmul(acc[0:SG, 2 * (n % 2) + t, a * 256:(a + 1) * 256], bbar[rows, part, q],
                                                       outm[rows, part, q, 0:STEP].rearrange("p k h -> p (k h)"),
                                                       start=part == 0, stop=part == 1)
                    ins.then_inc(tap_mm, 1)


def first_input_projection(nc, outer, io, scr):
    sem = lambda n: outer.new("s2_" + n)
    with ExitStack() as ctx:
        room = Room(nc, ctx, "s2")
        sb, ps = room.sb, room.ps
        ident = sb("ident", [P, P])
        expo = sb("expo", [P, 1])
        g = sb("g", [P, KD])
        raw = sb("raw", [P, 2, D])
        w_hi, w_lo = sb("w_hi", [P, KD, D], F32R), sb("w_lo", [P, KD, D], F32R)
        x = sb("x", [P, 3, D])
        junk = sb("junk", [P, D])
        stat = sb("stat", [P, 3, TILES])
        h = sb("h", [P, 2, 2, BT, KD, P], F32R)
        zst = sb("zst", [P, 2, BT * P])
        acc = ps("acc", [P, 4, 512])
        tr = ps("tr", [P, 2, 2, 512])

        ident0, ident_ok, g_in = sem("ident0"), sem("ident"), sem("g_in")
        raw_in, raw_used, hi_ok = [sem(f"raw_in{i}") for i in range(2)], sem("w_lo"), sem("w_hi")
        x_in = [sem(f"x_in{i}") for i in range(3)]
        sumsq, var, rstd, xn_ok = sem("sumsq"), sem("var"), sem("rstd"), sem("xn")
        tr_ok, th_ok, tl_ok = sem("tr"), sem("th"), sem("tl")
        z_mm, z_ok, z_st = sem("z_mm"), sem("z"), [sem(f"z_st{i}") for i in range(2)]

        BLOCKS = TILES // BT + 1

        def tiles_of(b):
            return range(BT * b, min(BT * b + BT, TILES))

        with nc.Block() as block:

            @block.sync
            def _(sp):
                xp = io["x_prompt"][0].rearrange("(c j) d -> j c d", j=STEP)
                xs = io["x_sample"].rearrange("b j d -> j b d")
                w = io["w_in"][0].rearrange("(k p) n -> k p n", p=P)

                def load_x(t):
                    if t >= 3:
                        sp.wait_ge(tr_ok, t - 2)
                    sp.dma_start(x[:, t % 3], xp[t] if t < STEP else xs).then_inc(x_in[t % 3], 16)

                sp.dma_start(g[:], io["g_mix"][0].rearrange("(k p) -> p k", p=P), allow_slow_non_contiguous=True).then_inc(g_in, 16)
                for t in range(3):
                    load_x(t)
                for k in range(KD):
                    if k >= 2:
                        sp.wait_ge(raw_used, k - 1)
                    sp.dma_start(raw[:, k % 2], w[k]).then_inc(raw_in[k % 2], 16)
                    if k % 2:
                        load_x(k // 2 + 3)
                load_x(7)
                for b in range(BLOCKS):
                    for m in range(KD):
                        n = b * KD + m
                        sp.wait_ge(z_ok, n + 1)
                        if b < BLOCKS - 1:
                            dst = scr["z"][m][:, BT * b:BT * b + BT, 0:CH]
                            src = zst[:, n % 2].rearrange("p (j c) -> p j c", j=BT)
                        else:
                            dst = scr["z"][m][:, :, CH:NC]
                            src = zst[:, n % 2, 0:P].rearrange("p (j b) -> p j b", b=STREAMS)
                        sp.dma_start(dst, src).then_inc(z_st[n % 2], 16)
                        if m % 2 and b < BLOCKS - 2 and BT * (b + 2) + m // 2 < TILES:
                            load_x(BT * (b + 2) + m // 2)
                for i in range(2):
                    sp.wait_ge(z_st[i], BLOCKS * KD // 2 * 16)

            @block.gpsimd
            def _(pool):
                nc.gpsimd.memset(expo[:], -0.5)
                identity_matrix(nc, pool, ident, ident0, ident_ok)
                for t in range(TILES):
                    pool.wait_ge(var, t + 1)
                    nc.gpsimd.tensor_tensor(stat[:, 2, t:t + 1], stat[:, 1, t:t + 1], expo[:], ALU.pow).then_inc(rstd, 1)

            @block.scalar
            def _(act):
                def square(t):
                    act.wait_ge(x_in[t % 3], 16 * (t // 3 + 1))
                    if t:
                        act.wait_ge(sumsq, t)
                    nc.scalar.activation(junk[:], x[:, t % 3], ACT.Square, accum_out=stat[:, 0, t:t + 1]).then_inc(sumsq, 1)

                def upper_half(t):
                    b, j = divmod(t, BT)
                    act.wait_ge(tr_ok, t + 1)
                    if b >= 2:
                        act.wait_ge(z_mm, (b - 1) * KD)
                    for a in range(2):
                        nc.scalar.activation(h[:, b % 2, 0, j, 4 * a:4 * a + 4].rearrange("p k n -> p (k n)"), tr[:, t % 2, a],
                                             ACT.Copy).then_inc(th_ok, 1)

                square(0)
                square(1)
                act.wait_ge(g_in, 16)
                for k in range(KD):
                    act.wait_ge(raw_in[k % 2], 16 * (k // 2 + 1))
                    nc.scalar.activation(w_hi[:, k], raw[:, k % 2], ACT.Copy, scale=g[:, k:k + 1]).then_inc(hi_ok, 1)
                    if k % 2:
                        upper_half(k // 2)
                        square(k // 2 + 2)
                for b in range(BLOCKS):
                    for m in range(KD):
                        n = b * KD + m
                        act.wait_ge(z_mm, n + 1)
                        if n >= 2:
                            act.wait_ge(z_st[n % 2], 16 * (n // 2))
                        wide = P * len(tiles_of(b))
                        nc.scalar.activation(zst[:, n % 2, 0:wide], acc[:, n % 4, 0:wide], ACT.Copy).then_inc(z_ok, 1)
                        t = BT * (b + 1) + m // 2
                        if m % 2 and t < TILES:
                            upper_half(t)
                            if t + 2 < TILES:
                                square(t + 2)

            @block.vector
            def _(dve):
                def norm(t):
                    dve.wait_ge(sumsq, t + 1)
                    nc.vector.tensor_scalar(stat[:, 1, t:t + 1], stat[:, 0, t:t + 1], 1.0 / D, EPS, ALU.mult, ALU.add).then_inc(var, 1)
                    dve.wait_ge(rstd, t + 1)
                    nc.vector.tensor_scalar(x[:, t % 3], x[:, t % 3], stat[:, 2, t:t + 1], None, ALU.mult).then_inc(xn_ok, 1)

                def lower_half(t):
                    b, j = divmod(t, BT)
                    for a in range(2):
                        dve.wait_ge(th_ok, 2 * t + a + 1)
                        up = h[:, b % 2, 0, j, 4 * a:4 * a + 4].rearrange("p k n -> p (k n)").bitcast(F32)
                        nc.vector.tensor_tensor(h[:, b % 2, 1, j, 4 * a:4 * a + 4].rearrange("p k n -> p (k n)"), tr[:, t % 2, a], up,
                                                ALU.subtract).then_inc(tl_ok, 1)

                norm(0)
                norm(1)
                for k in range(KD):
                    dve.wait_ge(hi_ok, k + 1)
                    nc.vector.scalar_tensor_tensor(w_lo[:, k], raw[:, k % 2], g[:, k:k + 1], w_hi[:, k].bitcast(F32),
                                                   ALU.mult, ALU.subtract).then_inc(raw_used, 1)
                    if k % 2:
                        lower_half(k // 2)
                        norm(k // 2 + 2)
                for t in range(BT, TILES):
                    lower_half(t)
                    if t + 2 < TILES:
                        norm(t + 2)

            @block.tensor
            def _(pe):
                def turn(t):
                    pe.wait_ge(xn_ok, t + 1)
                    if t >= 2:
                        pe.wait_ge(tl_ok, 2 * (t - 1))
                    for k in range(KD):
                        ins = nc.tensor.transpose(tr[:, t % 2, k // 4, (k % 4) * P:(k % 4 + 1) * P],
                                                  x[:, t % 3, k * P:(k + 1) * P], ident[:])
                    ins.then_inc(tr_ok, 1)

                pe.wait_ge(ident_ok, 1)
                for t in range(BT):
                    turn(t)
                for b in range(BLOCKS):
                    nt = len(tiles_of(b))
                    pe.wait_ge(tl_ok, 2 * (tiles_of(b)[-1] + 1))
                    for m in range(KD):
                        n = b * KD + m
                        if n >= 4:
                            pe.wait_ge(z_ok, n - 3)
                        for k in range(KD):
                            if n == 0:
                                pe.wait_ge(raw_used, k + 1)
                            cols = slice(m * P, (m + 1) * P)
                            ins = product3(nc, acc[:, n % 4, 0:nt * P], w_hi[:, k, cols], w_lo[:, k, cols],
                                           h[:, b % 2, 0, 0:nt, k], h[:, b % 2, 1, 0:nt, k], k == 0, k == KD - 1)
                        ins.then_inc(z_mm, 1)
                        if m % 2 and BT * (b + 1) + m // 2 < TILES:
                            turn(BT * (b + 1) + m // 2)


def mixers(nc, outer, io, scr):
    sem = lambda n: outer.new("s3_" + n)
    with ExitStack() as ctx:
        room = Room(nc, ctx, "s3")
        sb, ps = room.sb, room.ps
        ident = sb("ident", [P, P])
        u = sb("u", [P, 2, GROUPS, NC])
        injT = sb("injT", [P, PAIRS, 4, P])
        outm = sb("outm", [P, 2, PAIRS, STEP + 1, SG])
        toep = sb("toep", [P, GROUPS, 2 * P])
        ha = sb("ha", [P, 2, PAIRS, NC])
        hb = sb("hb", [P, 2, PAIRS, NC])
        QP = PAIRS // 4
        a16 = sb("a16", [P, 3, PAIRS])
        turn = sb("turn", [P, 3, PAIRS])
        phase = sb("phase", [P, 2, PAIRS, CH])
        parts = sb("parts", [P, 4, QP * CH])
        h0n = sb("h0n", [P, 2, P])
        h0 = sb("h0", [P, 2, STREAMS, PAIRS])
        ends = sb("ends", [P, 2, STREAMS, PAIRS])
        last = sb("last", [P, 2, P])
        lastp = sb("lastp", [PAIRS, 2, P])
        inj_ps = ps("inj", [P, 2, 512])
        out_ps = ps("out", [P, 3, 512])
        misc = ps("misc", [P, 512])

        ident0, ident_ok, zero_ok = sem("ident0"), sem("ident"), sem("zero")
        inj_in, u_in, outm_in, a16_in, h0_in, toep_in = ([sem(f"{n}{i}") for i in range(4)] if n in ("inj_in", "u_in") else sem(n) for n in ("inj_in", "u_in", "outm_in", "a16_in", "h0_in", "toep_in"))
        inj_mm, inj_ok, h0_tr, h0_ok = sem("inj_mm"), sem("inj_ok"), sem("h0_tr"), sem("h0_ok")
        chain, start_ok, last_tr, last_ok = sem("chain"), sem("start"), sem("last_tr"), sem("last")
        out_mm, out_even, out_odd, stored = sem("out_mm"), sem("out_even"), sem("out_odd"), sem("stored")

        with nc.Block() as block:

            @block.sync
            def _(sp):
                sp.dma_start(a16[:, 0:2], scr["pow16"]).then_inc(a16_in, 16)
                sp.dma_start(turn[:], scr["turn"]).then_inc(a16_in, 16)
                for part, name in enumerate(("state_ssm_re", "state_ssm_im")):
                    sp.dma_start(h0n[:, part], io[name][0].rearrange("b (q t) s -> (b q) (t s)", t=2)).then_inc(h0_in, 16)
                zs = scr["z"].rearrange("m (g h) j c -> m h g j c", h=SG)
                for m in range(4):
                    sp.dma_start(injT[:, QP * m:QP * m + QP], scr["injT"][:, QP * m:QP * m + QP]).then_inc(inj_in[m], 16)
                    for j in range(STEP):
                        sp.dma_start(u[SG * (j % 8):SG * (j % 8) + SG, j // 8, 8 * m:8 * m + 8], zs[4 + m][:, :, j]).then_inc(u_in[m], 16)
                sp.dma_start(outm[:], scr["outm"]).then_inc(outm_in, 16)
                sp.wait_ge(zero_ok, 1)
                for i in range(8):
                    rows = slice(SG * i, SG * i + SG)
                    sp.dma_start(toep[rows, :, SG * i:P], scr["taps"][:, :, 0:8 - i].rearrange("h g k c -> h g (k c)")).then_inc(toep_in, 16)
                    sp.dma_start(toep[rows, :, P:2 * P], scr["taps"][:, :, 8 - i:16 - i].rearrange("h g k c -> h g (k c)")).then_inc(toep_in, 16)
                for m in range(4):
                    sp.wait_ge(out_even, 4 * (m + 1))
                    sp.wait_ge(out_odd, 4 * (m + 1))
                    ys = scr["y"].rearrange("m (g h) j c -> m h g j c", h=SG)
                    for j in range(STEP):
                        sp.dma_start(ys[m][:, :, j], u[SG * (j % 8):SG * (j % 8) + SG, j // 8, 8 * m:8 * m + 8]).then_inc(stored, 16)
                sp.wait_ge(last_ok, 4)
                for part, name in enumerate(("new_ssm_re", "new_ssm_im")):
                    sp.dma_start(io[name + "_s"][0].rearrange("b (q t) s -> (b q) (t s)", t=2), last[:, part]).then_inc(stored, 16)
                    sp.dma_start(io[name + "_p"][0, 0].rearrange("(q t) s -> q (t s)", t=2), lastp[:, part]).then_inc(stored, 16)
                sp.wait_ge(stored, (4 + 4 * STEP) * 16)

            @block.gpsimd
            def _(pool):
                identity_matrix(nc, pool, ident, ident0, ident_ok)
                nc.gpsimd.memset(toep[:, :, 0:P], 0.0).then_inc(zero_ok, 1)

            @block.scalar
            def _(act):
                for q in range(PAIRS):
                    act.wait_ge(inj_mm, q + 1)
                    nc.scalar.activation(ha[:, :, q], inj_ps[:, q % 2, 0:2 * NC].rearrange("p (r c) -> p r c", r=2),
                                         ACT.Copy).then_inc(inj_ok, 1)
                for g in range(0, GROUPS, 2):
                    act.wait_ge(out_mm, g + 1)
                    nc.scalar.activation(u[:, :, g], out_ps[:, g % 3, 0:2 * NC].rearrange("p (a c) -> p a c", a=2),
                                         ACT.Copy).then_inc(out_even, 1)
                for part in range(2):
                    act.wait_ge(last_tr, 1)
                    nc.scalar.activation(last[:, part], misc[:, part * P:(part + 1) * P], ACT.Copy).then_inc(last_ok, 1)
                    nc.scalar.activation(lastp[:, part], misc[0:PAIRS, (2 + part) * P:(3 + part) * P], ACT.Copy).then_inc(last_ok, 1)

            @block.vector
            def _(dve):
                links = [0]

                def then(*instructions):
                    for ins in instructions:
                        ins.then_inc(chain, 1)
                    links[0] += len(instructions)
                    dve.wait_ge(chain, links[0])

                tt, ts, stt = nc.vector.tensor_tensor, nc.vector.tensor_scalar, nc.vector.scalar_tensor_tensor
                dve.wait_ge(a16_in, 32)
                ts(a16[:, 2], a16[:, 1], -1.0, None, ALU.mult).then_inc(h0_ok, 1)
                cosine, sine = phase[:, 0], phase[:, 1]
                then(nc.vector.memset(cosine[:, :, 0:1], 1.0), nc.vector.memset(sine[:, :, 0:1], 0.0),
                     nc.vector.tensor_copy(cosine[:, :, 1], turn[:, 1]), nc.vector.tensor_copy(sine[:, :, 1], turn[:, 2]))
                scratch = parts[:].rearrange("p a n -> p (a n)")
                k = 1
                while k < CH - 1:
                    n = min(k, CH - 1 - k)
                    t0, t1 = (scratch[:, i * PAIRS * n:(i + 1) * PAIRS * n].rearrange("p (q c) -> p q c", q=PAIRS) for i in range(2))
                    c0, s0 = cosine[:, :, 1:1 + n], sine[:, :, 1:1 + n]
                    ck, sk = (x[:, :, k:k + 1].to_broadcast([P, PAIRS, n]) for x in (cosine, sine))
                    then(tt(t0, c0, ck, ALU.mult), tt(t1, s0, sk, ALU.mult))
                    then(tt(cosine[:, :, k + 1:k + 1 + n], t0, t1, ALU.subtract))
                    then(tt(t0, c0, sk, ALU.mult), tt(t1, s0, ck, ALU.mult))
                    then(tt(sine[:, :, k + 1:k + 1 + n], t0, t1, ALU.add))
                    k += n
                row = lambda x, Q: x[:, Q * QP:Q * QP + QP].rearrange("p q c -> p (q c)")
                for Q in range(4):
                    c, s = row(cosine, Q), row(sine, Q)
                    then(tt(parts[:, 0], c, c, ALU.mult), tt(parts[:, 1], s, s, ALU.mult))
                    then(tt(parts[:, 0], parts[:, 0], parts[:, 1], ALU.add))
                    then(ts(parts[:, 0], parts[:, 0], -0.5, 1.5, ALU.mult, ALU.add))
                    then(tt(c, c, parts[:, 0], ALU.mult), tt(s, s, parts[:, 0], ALU.mult))
                dve.wait_ge(h0_tr, 1)
                nc.vector.tensor_copy(h0[:].rearrange("p r b q -> p (r b q)"), misc[:, 0:2 * P]).then_inc(h0_ok, 1)
                dve.wait_ge(h0_ok, 2)
                for Q in range(4):
                    pairs = slice(Q * QP, Q * QP + QP)
                    dve.wait_ge(inj_ok, QP * (Q + 1))
                    part = [parts[:, i].rearrange("p (q c) -> p q c", q=QP) for i in range(4)]
                    c, s = cosine[:, pairs], sine[:, pairs]
                    x, y = ha[:, 0, pairs, 0:CH], ha[:, 1, pairs, 0:CH]
                    then(tt(part[0], x, c, ALU.mult), tt(part[1], y, s, ALU.mult), tt(part[2], y, c, ALU.mult), tt(part[3], x, s, ALU.mult))
                    then(tt(hb[:, 0, pairs, 0:CH], part[0], part[1], ALU.add), tt(hb[:, 1, pairs, 0:CH], part[2], part[3], ALU.subtract))
                    then(*(nc.vector.tensor_tensor_scan(ha[:, i, q, 0:CH], turn[:, 0, q:q + 1].to_broadcast([P, CH]), hb[:, i, q, 0:CH],
                                                        0.0, ALU.mult, ALU.add) for i in range(2) for q in range(Q * QP, Q * QP + QP)))
                    then(tt(part[0], x, c, ALU.mult), tt(part[1], y, s, ALU.mult), tt(part[2], x, s, ALU.mult), tt(part[3], y, c, ALU.mult))
                    early, final = slice(0, CH - 1), slice(CH - 1, CH)
                    wide = lambda i: a16[:, i, pairs].unsqueeze(2).to_broadcast([P, QP, STREAMS])
                    st = lambda i: h0[:, i].rearrange("p b q -> p q b")[:, pairs]
                    end = lambda i: hb[:, i, pairs, CH:NC]
                    own = lambda i: ha[:, i, pairs, CH:NC]
                    then(tt(ha[:, 0, pairs, 1:CH], part[0][:, :, early], part[1][:, :, early], ALU.subtract),
                         tt(ha[:, 1, pairs, 1:CH], part[2][:, :, early], part[3][:, :, early], ALU.add),
                         tt(hb[:, 0, pairs, final], part[0][:, :, final], part[1][:, :, final], ALU.subtract),
                         tt(hb[:, 1, pairs, final], part[2][:, :, final], part[3][:, :, final], ALU.add),
                         nc.vector.memset(ha[:, 0, pairs, 0:1], 0.0), nc.vector.memset(ha[:, 1, pairs, 0:1], 0.0),
                         tt(end(0), st(0), wide(0), ALU.mult), tt(end(1), st(1), wide(0), ALU.mult))
                    then(tt(own(0), own(0), end(0), ALU.add), tt(own(1), own(1), end(1), ALU.add))
                    then(tt(end(0), st(1), wide(2), ALU.mult), tt(end(1), st(0), wide(1), ALU.mult))
                    then(tt(end(0), own(0), end(0), ALU.add), tt(end(1), own(1), end(1), ALU.add))
                    then(*(nc.vector.tensor_copy(ends[:, i].rearrange("p b q -> p q b")[:, pairs], end(i)) for i in range(2)),
                         *(nc.vector.tensor_copy(own(i), st(i)) for i in range(2)))
                    dve.sem_inc(start_ok, 1)
                for g in range(1, GROUPS, 2):
                    dve.wait_ge(out_mm, g + 1)
                    nc.vector.tensor_copy(u[:, :, g], out_ps[:, g % 3, 0:2 * NC].rearrange("p (a c) -> p a c", a=2)).then_inc(out_odd, 1)

            @block.tensor
            def _(pe):
                pe.wait_ge(ident_ok, 1)
                pe.wait_ge(h0_in, 32)
                for part in range(2):
                    ins = nc.tensor.transpose(misc[:, part * P:(part + 1) * P], h0n[:, part], ident[:])
                ins.then_inc(h0_tr, 1)
                for q in range(PAIRS):
                    pe.wait_ge(inj_in[q // QP], 16)
                    pe.wait_ge(u_in[q // QP], STEP * 16)
                    if q >= 2:
                        pe.wait_ge(inj_ok, q - 1)
                    for part in range(2):
                        for t in range(2):
                            for jh in range(2):
                                ins = nc.tensor.matmul(inj_ps[t * SS:(t + 1) * SS, q % 2, part * NC:(part + 1) * NC],
                                                       injT[:, q, 2 * part + jh, t * SS:(t + 1) * SS], u[:, jh, 2 * q + t],
                                                       start=jh == 0, stop=jh == 1)
                    ins.then_inc(inj_mm, 1)
                pe.wait_ge(outm_in, 16)
                pe.wait_ge(toep_in, 16 * 16)
                for g in range(GROUPS):
                    q, t = divmod(g, 2)
                    rows = slice(t * SS, (t + 1) * SS)
                    pe.wait_ge(start_ok, q // QP + 1)
                    if g >= 3:
                        pe.wait_ge(out_odd if (g - 3) % 2 else out_even, (g - 3) // 2 + 1)
                    for jh in range(2):
                        to = out_ps[:, g % 3, jh * NC:(jh + 1) * NC]
                        nc.tensor.matmul(to, toep[:, g, 0:P], u[:, jh, g], start=True, stop=False)
                        if jh:
                            nc.tensor.matmul(to, toep[:, g, P:2 * P], u[:, 0, g], start=False, stop=False)
                        for part in range(2):
                            ins = nc.tensor.matmul(to, outm[rows, part, q, 1 + 8 * jh:9 + 8 * jh].rearrange("p k h -> p (k h)"),
                                                   ha[rows, part, q], start=False, stop=part == 1)
                    ins.then_inc(out_mm, 1)
                pe.wait_ge(h0_ok, 2)
                for part in range(2):
                    nc.tensor.transpose(misc[:, part * P:(part + 1) * P], ends[:, part].rearrange("p b q -> p (b q)"), ident[:])
                    ins = nc.tensor.transpose(misc[0:PAIRS, (2 + part) * P:(3 + part) * P], hb[:, part, :, CH - 1], ident[:])
                ins.then_inc(last_tr, 1)


def pooling(nc, outer, io, scr):
    sem = lambda n: outer.new("sp_" + n)
    with ExitStack() as ctx:
        room = Room(nc, ctx, "sp")
        sb, ps = room.sb, room.ps
        EX = HIST + STEP
        ident = sb("ident", [P, P])
        ext = sb("ext", [P, 2, EX, NC])
        sums = sb("sums", [P, 2, EX, NC])
        pooled = sb("pooled", [P, 2, STEP, NC])
        ost = sb("ost", [P, 2, STEP, NC])
        count = sb("count", [P, 4, STEP])
        wp = sb("wp", [P, 4, P])
        scale = sb("scale", [P, 4])
        hist = sb("hist", [STREAMS * HIST, DP])
        tail = sb("tail", [P, 4, HIST, STREAMS])
        tail1 = sb("tail1", [P, 4, HIST])
        tails = sb("tails", [STREAMS * HIST, DP])
        tailp = sb("tailp", [HIST, DP])
        hist_ps = ps("hist", [P, 512])
        tail_ps = ps("tail", [P, 512])
        tailp_ps = ps("tailp", [P, 512])
        out_ps = ps("out", [P, 3, 512])

        ident0, ident_ok, w_in, hist_in, tail_in = (sem(n) for n in ("ident0", "ident", "w_in", "hist_in", "tail_in"))
        ext_in = [sem(f"ext_in{i}") for i in range(2)]
        hist_tr, hist_ok, tail_tr, tail_ok, cnt_ok = (sem(n) for n in ("hist_tr", "hist", "tail_tr", "tail", "cnt"))
        chain, pooled_ok, out_mm, out_ok = sem("chain"), sem("pooled"), sem("out_mm"), sem("out_ok")
        out_st, stored = [sem(f"out_st{i}") for i in range(2)], sem("stored")
        NB = 8

        with nc.Block() as block:

            @block.sync
            def _(sp):
                sp.dma_start(hist[:], io["state_pool"][0].rearrange("b e c -> (b e) c")).then_inc(hist_in, 16)
                sp.dma_start(wp[:], io["w_pool"][0].rearrange("m c d -> c m d")).then_inc(w_in, 16)
                sp.dma_start(scale[:], io["pool_scale"][0].rearrange("(m p) -> p m", p=P), allow_slow_non_contiguous=True).then_inc(w_in, 16)

                def load(m):
                    if m >= 2:
                        sp.wait_ge(pooled_ok, m - 1)
                    z = scr["z"][m]
                    sp.dma_start(ext[:, m % 2, HIST:EX], z).then_inc(ext_in[m % 2], 16)
                    sp.dma_start(ext[:, m % 2, 0:HIST, 1:CH], z[:, 1:STEP, 0:CH - 1]).then_inc(ext_in[m % 2], 16)
                load(0)
                load(1)
                for m in range(4):
                    sp.dma_start(tail[:, m], scr["z"][m][:, 1:STEP, CH:NC]).then_inc(tail_in, 16)
                    sp.dma_start(tail1[:, m], scr["z"][m][:, 1:STEP, CH - 1], allow_slow_non_contiguous=True).then_inc(tail_in, 16)
                for m in range(4):
                    sp.wait_ge(out_ok, NB * (m + 1))
                    sp.dma_start(scr["c"][0:STEP, :, m].rearrange("j p c -> p j c"), ost[:, m % 2, :, 0:CH]).then_inc(out_st[m % 2], 16)
                    sp.dma_start(scr["c"][STEP, :, m].rearrange("p (j b) -> p j b", b=STREAMS), ost[:, m % 2, :, CH:NC]).then_inc(out_st[m % 2], 16)
                    if m < 2:
                        load(m + 2)
                sp.wait_ge(tail_ok, 2)
                sp.dma_start(io["new_pool_s"][0].rearrange("b e c -> e b c"), tails[:]).then_inc(stored, 16)
                sp.dma_start(io["new_pool_p"][0, 0], tailp[:]).then_inc(stored, 16)
                sp.wait_ge(stored, 32)
                for i in range(2):
                    sp.wait_ge(out_st[i], 64)

            @block.gpsimd
            def _(pool):
                identity_matrix(nc, pool, ident, ident0, ident_ok)
                for m in range(4):
                    w = 2 << m
                    for j in range(STEP):
                        ins = nc.gpsimd.memset(count[:, m, j:j + 1], w / min(j + 1, w))
                ins.then_inc(cnt_ok, 1)

            @block.scalar
            def _(act):
                act.wait_ge(w_in, 32)
                for m in range(4):
                    if m >= 2:
                        act.wait_ge(out_st[m % 2], 32 * (m // 2))
                    for i in range(NB):
                        n = NB * m + i
                        act.wait_ge(out_mm, n + 1)
                        nc.scalar.activation(ost[:, m % 2, 2 * i:2 * i + 2].rearrange("p j c -> p (j c)"), out_ps[:, n % 3, 0:2 * NC],
                                             ACT.Copy, scale=scale[:, m:m + 1]).then_inc(out_ok, 1)
                act.wait_ge(tail_tr, 1)
                nc.scalar.activation(tails[:], tail_ps[0:STREAMS * HIST, :], ACT.Copy).then_inc(tail_ok, 1)
                nc.scalar.activation(tailp[:], tailp_ps[0:HIST, :], ACT.Copy).then_inc(tail_ok, 1)

            @block.vector
            def _(dve):
                links = [0]

                def then(*instructions):
                    for ins in instructions:
                        ins.then_inc(chain, 1)
                    links[0] += len(instructions)
                    dve.wait_ge(chain, links[0])

                dve.wait_ge(hist_tr, 1)
                dve.wait_ge(cnt_ok, 1)
                for m in range(4):
                    e = ext[:, m % 2]
                    dve.wait_ge(ext_in[m % 2], 32 * (m // 2 + 1))
                    then(nc.vector.memset(e[:, 0:HIST, 0:1], 0.0),
                         nc.vector.tensor_copy(e[:, 0:HIST, CH:NC], hist_ps[:, m * P:m * P + STREAMS * HIST].rearrange("p (b e) -> p e b", b=STREAMS)))
                    src, low = e, 0
                    for l in range(m + 1):
                        s = 1 << l
                        low += s
                        dst = sums[:, l % 2]
                        flat = lambda buf, a, b: buf[:, a:b].rearrange("p e c -> p (e c)")
                        then(nc.vector.tensor_tensor(flat(dst, low, EX), flat(src, low, EX), flat(src, low - s, EX - s), ALU.add))
                        src = dst
                    then(nc.vector.tensor_tensor(src[:, HIST:EX, 0], src[:, HIST:EX, 0], count[:, m], ALU.mult))
                    if m >= 2:
                        dve.wait_ge(out_mm, NB * (m - 1))
                    nc.vector.scalar_tensor_tensor(pooled[:, m % 2].rearrange("p j c -> p (j c)"), flat(src, HIST, EX), 1.0 / (2 << m),
                                                   flat(e, HIST, EX), ALU.mult, ALU.subtract).then_inc(pooled_ok, 1)
                    dve.wait_ge(pooled_ok, m + 1)

            @block.tensor
            def _(pe):
                pe.wait_ge(ident_ok, 1)
                pe.wait_ge(hist_in, 16)
                for m in range(4):
                    ins = nc.tensor.transpose(hist_ps[:, m * P:m * P + STREAMS * HIST], hist[:, m * P:(m + 1) * P],
                                              ident[0:STREAMS * HIST, 0:STREAMS * HIST])
                ins.then_inc(hist_tr, 1)
                pe.wait_ge(tail_in, 128)
                for m in range(4):
                    nc.tensor.transpose(tail_ps[0:STREAMS * HIST, m * P:(m + 1) * P], tail[:, m].rearrange("p e b -> p (e b)"), ident[:])
                    ins = nc.tensor.transpose(tailp_ps[0:HIST, m * P:(m + 1) * P], tail1[:, m], ident[:])
                ins.then_inc(tail_tr, 1)
                pe.wait_ge(w_in, 32)
                for m in range(4):
                    pe.wait_ge(pooled_ok, m + 1)
                    for i in range(NB):
                        n = NB * m + i
                        if n >= 3:
                            pe.wait_ge(out_ok, n - 2)
                        nc.tensor.matmul(out_ps[:, n % 3, 0:2 * NC], wp[:, m], pooled[:, m % 2, 2 * i:2 * i + 2].rearrange("p j c -> p (j c)"),
                                         start=True, stop=True).then_inc(out_mm, 1)


def gelu_glu(nc, outer, io, scr):
    sem = lambda n: outer.new("s4_" + n)
    with ExitStack() as ctx:
        room = Room(nc, ctx, "s4")
        sb, ps = room.sb, room.ps
        NB, WB = STEP // 2, 2 * NC
        raw = sb("raw", [P, 4, DP])
        w_hi, w_lo = sb("w_hi", [P, 4, DP], F32R), sb("w_lo", [P, 4, DP], F32R)
        skip, bias = sb("skip", [P, 4]), sb("bias", [P, 4])
        y = sb("y", [P, 2, 4, WB])
        z = sb("z", [P, 2, 4, WB])
        v = sb("v", [P, NB, 4, WB])
        g_hi, g_lo = sb("g_hi", [P, 2, 4, WB], F32R), sb("g_lo", [P, 2, 4, WB], F32R)
        gate = sb("gate", [P, 4, WB])
        out = sb("out", [P, 2, 4, WB])
        outs = sb("outs", [P, 4, STEP, STREAMS])
        acc = ps("acc", [P, 4, 512])

        w_in, c_in = sem("w_in"), sem("c_in")
        yz_in = [sem(f"yz_in{i}") for i in range(2)]
        whi_ok, wlo_ok = sem("whi"), sem("wlo")
        v_ok, gelu_ok, hi_ok, lo_ok, mm, gate_ok, out_ok, outs_ok = (
            sem(n) for n in ("v", "gelu", "hi", "lo", "mm", "gate", "out", "outs"))
        out_st, stored = [sem(f"out_st{i}") for i in range(2)], sem("stored")

        with nc.Block() as block:

            @block.sync
            def _(sp):
                sp.dma_start(skip[:], io["ssm_d"][0].rearrange("(m g) h -> (g h) m", m=4), allow_slow_non_contiguous=True).then_inc(c_in, 16)
                sp.dma_start(bias[:], io["b_glu"][0].rearrange("(m p) -> p m", p=P), allow_slow_non_contiguous=True).then_inc(c_in, 16)

                def load(i):
                    if i >= 2:
                        sp.wait_ge(v_ok, 4 * (i - 1))
                    sp.dma_start(y[:, i % 2].rearrange("p m (j c) -> p m j c", j=2),
                                 scr["y"][:, :, 2 * i:2 * i + 2].rearrange("m p j c -> p m j c")).then_inc(yz_in[i % 2], 16)
                    sp.dma_start(z[:, i % 2].rearrange("p m (j c) -> p m j c", j=2),
                                 scr["z"][4:8, :, 2 * i:2 * i + 2].rearrange("m p j c -> p m j c")).then_inc(yz_in[i % 2], 16)
                load(0)
                load(1)
                sp.dma_start(raw[:], io["w_glu"][0].rearrange("(k p) n -> p k n", p=P)).then_inc(w_in, 16)
                for i in range(2, NB):
                    load(i)
                for i in range(NB):
                    sp.wait_ge(out_ok, 4 * (i + 1))
                    for j in range(2):
                        sp.dma_start(scr["c"][2 * i + j][:, 4:8], out[:, i % 2, :, j * NC:j * NC + CH]).then_inc(out_st[i % 2], 16)
                sp.wait_ge(outs_ok, NB)
                sp.dma_start(scr["c"][STEP][:, 4:8].rearrange("p m (j b) -> p m j b", b=STREAMS), outs[:]).then_inc(stored, 16)
                sp.wait_ge(stored, 16)
                for i in range(2):
                    sp.wait_ge(out_st[i], NB // 2 * 32)

            @block.scalar
            def _(act):
                for i in range(NB):
                    act.wait_ge(v_ok, 4 * (i + 1))
                    flat = v[:, i].rearrange("p m n -> p (m n)")
                    nc.scalar.activation(flat, flat, ACT.Gelu_apprx_tanh).then_inc(gelu_ok, 1)
                act.wait_ge(w_in, 16)
                nc.scalar.activation(w_hi[:], raw[:], ACT.Copy).then_inc(whi_ok, 1)
                act.wait_ge(c_in, 32)

                def upper_half(i):
                    act.wait_ge(gelu_ok, i + 1)
                    if i >= 2:
                        act.wait_ge(mm, 4 * (i - 1))
                    nc.scalar.activation(g_hi[:, i % 2], v[:, i], ACT.Copy).then_inc(hi_ok, 1)
                upper_half(0)
                for i in range(NB):
                    if i + 1 < NB:
                        upper_half(i + 1)
                    for m in range(4):
                        n = 4 * i + m
                        act.wait_ge(mm, n + 1)
                        if i:
                            act.wait_ge(out_ok, n - 3)
                        nc.scalar.activation(gate[:, m], acc[:, m, 0:WB], ACT.Sigmoid, bias=bias[:, m:m + 1]).then_inc(gate_ok, 1)

            @block.vector
            def _(dve):
                dve.wait_ge(c_in, 32)
                for i in range(NB):
                    dve.wait_ge(yz_in[i % 2], 32 * (i // 2 + 1))
                    for m in range(4):
                        nc.vector.scalar_tensor_tensor(v[:, i, m], z[:, i % 2, m], skip[:, m:m + 1], y[:, i % 2, m],
                                                       ALU.mult, ALU.add).then_inc(v_ok, 1)
                dve.wait_ge(whi_ok, 1)
                nc.vector.tensor_tensor(w_lo[:], raw[:], w_hi[:].bitcast(F32), ALU.subtract).then_inc(wlo_ok, 1)

                def lower_half(i):
                    dve.wait_ge(hi_ok, i + 1)
                    nc.vector.tensor_tensor(g_lo[:, i % 2], v[:, i], g_hi[:, i % 2].bitcast(F32), ALU.subtract).then_inc(lo_ok, 1)
                lower_half(0)
                for i in range(NB):
                    if i + 1 < NB:
                        lower_half(i + 1)
                    if i >= 2:
                        dve.wait_ge(out_st[i % 2], 32 * (i // 2))
                    for m in range(4):
                        n = 4 * i + m
                        dve.wait_ge(gate_ok, n + 1)
                        nc.vector.tensor_tensor(out[:, i % 2, m], v[:, i, m], gate[:, m], ALU.mult).then_inc(out_ok, 1)
                    dve.wait_ge(out_ok, 4 * (i + 1))
                    src = out[:, i % 2].rearrange("p m (j c) -> p m j c", j=2)[:, :, :, CH:NC]
                    nc.vector.tensor_copy(outs[:, :, 2 * i:2 * i + 2], src).then_inc(outs_ok, 1)

            @block.tensor
            def _(pe):
                pe.wait_ge(wlo_ok, 1)
                for i in range(NB):
                    pe.wait_ge(lo_ok, i + 1)
                    for m in range(4):
                        n = 4 * i + m
                        if n >= 4:
                            pe.wait_ge(gate_ok, n - 3)
                        for k in range(4):
                            cols = slice(m * P, (m + 1) * P)
                            ins = product3(nc, acc[:, m, 0:WB], w_hi[:, k, cols], w_lo[:, k, cols], g_hi[:, i % 2, k], g_lo[:, i % 2, k],
                                           k == 0, k == 3)
                        ins.then_inc(mm, 1)


def output_projection(nc, outer, io, scr, tag, weight, source, first, target, normed):
    sem = lambda n: outer.new(f"{tag}_{n}")
    with ExitStack() as ctx:
        room = Room(nc, ctx, tag)
        sb, ps = room.sb, room.ps
        ident = sb("ident", [P, P])
        expo = sb("expo", [P, 1])
        raw = sb("raw", [P, 2, D])
        w_hi, w_lo = sb("w_hi", [P, KD, D], F32R), sb("w_lo", [P, KD, D], F32R)
        s = sb("s", [P, 2, KD, P])
        s_hi, s_lo = sb("s_hi", [P, 2, KD, P], F32R), sb("s_lo", [P, 2, KD, P], F32R)
        x = sb("x", [P, 2, D])
        xn = sb("xn", [P, 2, D])
        junk = sb("junk", [P, D])
        stat = sb("stat", [P, 2, 3])
        ht = sb("ht", [P, 2, KD, P])
        acc = ps("acc", [P, 2, 2, 512])
        tr = ps("tr", [P, 2, 2, 512])

        ident0, ident_ok = sem("ident0"), sem("ident")
        raw_in, whi_ok, wlo_ok = [sem(f"raw_in{i}") for i in range(2)], sem("whi"), sem("wlo")
        s_in, x_in = [sem(f"s_in{i}") for i in range(2)], [sem(f"x_in{i}") for i in range(2)]
        shi_ok, slo_ok, mm, x_ok, sumsq, var, rstd, xn_ok, tr_ok, ht_ok = (
            sem(n) for n in ("shi", "slo", "mm", "x", "sumsq", "var", "rstd", "xn", "tr", "ht"))
        x_st, ht_st = [sem(f"x_st{i}") for i in range(2)], [sem(f"ht_st{i}") for i in range(2)]
        LAST = TILES - 1

        with nc.Block() as block:

            @block.sync
            def _(sp):
                w = io[weight][0].rearrange("(k p) n -> k p n", p=P)

                def load_source(t, i):
                    sp.dma_start(s[:, i], source[t]).then_inc(s_in[i], 16)

                def load_x(t, i):
                    sp.dma_start(x[:, i], first(t)).then_inc(x_in[i], 16)

                def store_x(t, i):
                    sp.wait_ge(x_ok, 2 * t + 2)
                    sp.dma_start(target[t], x[:, i]).then_inc(x_st[i], 16)

                def store_normed(t, i):
                    sp.wait_ge(ht_ok, 2 * t + 2)
                    sp.dma_start(normed[t], ht[:, i]).then_inc(ht_st[i], 16)

                def next_loads(t, i, uses):
                    sp.wait_ge(slo_ok, t + 1)
                    load_source(t + 2, i)
                    sp.wait_ge(xn_ok, t + 1)
                    sp.wait_ge(x_st[i], 16 * uses)
                    load_x(t + 2, i)

                load_source(0, 0)
                for k in range(KD):
                    if k >= 2:
                        sp.wait_ge(wlo_ok, k - 1)
                    sp.dma_start(raw[:, k % 2], w[k]).then_inc(raw_in[k % 2], 16)
                    if k == 1:
                        load_source(1, 1)
                        load_x(0, 0)
                        load_x(1, 1)
                store_x(0, 0)
                next_loads(0, 0, 1)
                with sp.Fori(0, 6) as r:
                    for half in range(2):
                        t = 2 * r + 1 + half
                        i = 1 - half
                        store_x(t, i)
                        store_normed(t - 1, 1 - i)
                        next_loads(t, i, r + 1 + half)
                for t in range(13, TILES):
                    store_x(t, t % 2)
                    store_normed(t - 1, (t - 1) % 2)
                    if t + 2 < TILES:
                        next_loads(t, t % 2, t // 2 + 1)
                store_normed(LAST, LAST % 2)
                for i in range(2):
                    sp.wait_ge(x_st[i], 16 * ((TILES + 1 - i) // 2))
                    sp.wait_ge(ht_st[i], 16 * ((TILES + 1 - i) // 2))

            @block.gpsimd
            def _(pool):
                nc.gpsimd.memset(expo[:], -0.5)
                identity_matrix(nc, pool, ident, ident0, ident_ok)
                for t in range(TILES):
                    pool.wait_ge(var, t + 1)
                    nc.gpsimd.tensor_tensor(stat[:, t % 2, 2:3], stat[:, t % 2, 1:2], expo[:], ALU.pow).then_inc(rstd, 1)

            @block.scalar
            def _(act):
                def source_half(t, i, uses):
                    act.wait_ge(s_in[i], 16 * uses)
                    if not isinstance(t, int) or t >= 2:
                        act.wait_ge(mm, t - 1)
                    nc.scalar.activation(s_hi[:, i], s[:, i], ACT.Copy).then_inc(shi_ok, 1)

                def square(t, i):
                    act.wait_ge(x_ok, 2 * t + 2)
                    if not isinstance(t, int) or t >= 1:
                        act.wait_ge(xn_ok, t)
                    nc.scalar.activation(junk[:], x[:, i], ACT.Square, accum_out=stat[:, i, 0:1]).then_inc(sumsq, 1)

                def take_normed(t, i, uses):
                    act.wait_ge(tr_ok, t + 1)
                    if uses is not None:
                        act.wait_ge(ht_st[i], 16 * uses)
                    for a in range(2):
                        nc.scalar.activation(ht[:, i, 4 * a:4 * a + 4].rearrange("p k n -> p (k n)"), tr[:, i, a], ACT.Copy).then_inc(ht_ok, 1)

                source_half(0, 0, 1)
                for k in range(KD):
                    act.wait_ge(raw_in[k % 2], 16 * (k // 2 + 1))
                    nc.scalar.activation(w_hi[:, k], raw[:, k % 2], ACT.Copy).then_inc(whi_ok, 1)
                source_half(1, 1, 1)
                square(0, 0)
                for t in (1, 2):
                    source_half(t + 1, (t + 1) % 2, t // 2 + 1 + t % 2)
                    square(t, t % 2)
                    take_normed(t - 1, (t - 1) % 2, None)
                with act.Fori(0, 6) as r:
                    for half in range(2):
                        t = 2 * r + 3 + half
                        i = 1 - half
                        source_half(t + 1, 1 - i, r + 3)
                        square(t, i)
                        take_normed(t - 1, 1 - i, r + 1)
                source_half(LAST, 0, 9)
                square(LAST - 1, 1)
                take_normed(LAST - 2, 0, 7)
                square(LAST, 0)
                take_normed(LAST - 1, 1, 7)
                take_normed(LAST, 0, 8)

            @block.vector
            def _(dve):
                def source_half(t, i):
                    dve.wait_ge(shi_ok, t + 1)
                    nc.vector.tensor_tensor(s_lo[:, i], s[:, i], s_hi[:, i].bitcast(F32), ALU.subtract).then_inc(slo_ok, 1)

                def residual_and_norm(t, i, uses):
                    dve.wait_ge(mm, t + 1)
                    dve.wait_ge(x_in[i], 16 * uses)
                    for a in range(2):
                        half = x[:, i, a * 512:(a + 1) * 512]
                        nc.vector.tensor_tensor(half, half, acc[:, i, a], ALU.add).then_inc(x_ok, 1)
                    dve.wait_ge(sumsq, t + 1)
                    nc.vector.tensor_scalar(stat[:, i, 1:2], stat[:, i, 0:1], 1.0 / D, EPS, ALU.mult, ALU.add).then_inc(var, 1)
                    dve.wait_ge(rstd, t + 1)
                    if not isinstance(t, int) or t >= 2:
                        dve.wait_ge(tr_ok, t - 1)
                    nc.vector.tensor_scalar(xn[:, i], x[:, i], stat[:, i, 2:3], None, ALU.mult).then_inc(xn_ok, 1)

                source_half(0, 0)
                for k in range(KD):
                    dve.wait_ge(whi_ok, k + 1)
                    nc.vector.tensor_tensor(w_lo[:, k], raw[:, k % 2], w_hi[:, k].bitcast(F32), ALU.subtract).then_inc(wlo_ok, 1)
                source_half(1, 1)
                residual_and_norm(0, 0, 1)
                source_half(2, 0)
                residual_and_norm(1, 1, 1)
                with dve.Fori(0, 7) as r:
                    for half in range(2):
                        t = 2 * r + 2 + half
                        source_half(t + 1, 1 - half)
                        residual_and_norm(t, half, r + 2)
                residual_and_norm(LAST, 0, 9)

            @block.tensor
            def _(pe):
                def multiply(t, i, first_tile=False):
                    pe.wait_ge(slo_ok, t + 1)
                    if not isinstance(t, int) or t >= 2:
                        pe.wait_ge(x_ok, 2 * t - 2)
                    for k in range(KD):
                        if first_tile:
                            pe.wait_ge(wlo_ok, k + 1)
                        for a in range(2):
                            cols = slice(a * 512, (a + 1) * 512)
                            ins = product3(nc, acc[:, i, a], s_hi[:, i, k], s_lo[:, i, k], w_hi[:, k, cols], w_lo[:, k, cols],
                                           k == 0, k == KD - 1)
                    ins.then_inc(mm, 1)

                def turn(t, i):
                    pe.wait_ge(xn_ok, t + 1)
                    if not isinstance(t, int) or t >= 2:
                        pe.wait_ge(ht_ok, 2 * t - 2)
                    for k in range(KD):
                        ins = nc.tensor.transpose(tr[:, i, k // 4, (k % 4) * P:(k % 4 + 1) * P], xn[:, i, k * P:(k + 1) * P], ident[:])
                    ins.then_inc(tr_ok, 1)

                pe.wait_ge(ident_ok, 1)
                multiply(0, 0, True)
                multiply(1, 1)
                turn(0, 0)
                multiply(2, 0)
                turn(1, 1)
                with pe.Fori(0, 7) as r:
                    for half in range(2):
                        t = 2 * r + 3 + half
                        multiply(t, 1 - half)
                        turn(t - 1, half)
                turn(LAST, 0)


def query_projection(nc, outer, io, scr):
    sem = lambda n: outer.new("s6_" + n)
    with ExitStack() as ctx:
        room = Room(nc, ctx, "s6")
        sb, ps = room.sb, room.ps
        g = sb("g", [P, KD])
        raw = sb("raw", [P, 2, D])
        w_hi, w_lo = sb("w_hi", [P, KD, D], F32R), sb("w_lo", [P, KD, D], F32R)
        t_in = sb("t_in", [P, 3, KD, P])
        h = sb("h", [P, 2, 2, BT, KD, P], F32R)
        st = sb("st", [P, 2, BT * P])
        acc = ps("acc", [P, 4, 512])
        g_in, raw_in, whi_ok, wlo_ok = sem("g_in"), [sem(f"raw_in{i}") for i in range(2)], sem("whi"), sem("wlo")
        h_in, hi_ok, lo_ok = [sem(f"h_in{i}") for i in range(3)], sem("hi"), sem("lo")
        mm, q_ok, q_st = sem("mm"), sem("q"), [sem(f"q_st{i}") for i in range(2)]
        BLOCKS = TILES // BT + 1

        def tiles_of(b):
            return range(BT * b, min(BT * b + BT, TILES))

        with nc.Block() as block:

            @block.sync
            def _(sp):
                w = io["w_q"][0].rearrange("(k p) n -> k p n", p=P)

                def load(t):
                    if t >= 3:
                        sp.wait_ge(lo_ok, t - 2)
                    sp.dma_start(t_in[:, t % 3], scr["h"][t]).then_inc(h_in[t % 3], 16)
                sp.dma_start(g[:], io["g_xattn"][0].rearrange("(k p) -> p k", p=P), allow_slow_non_contiguous=True).then_inc(g_in, 16)
                for t in range(3):
                    load(t)
                for k in range(KD):
                    if k >= 2:
                        sp.wait_ge(wlo_ok, k - 1)
                    sp.dma_start(raw[:, k % 2], w[k]).then_inc(raw_in[k % 2], 16)
                for t in range(3, 2 * BT):
                    load(t)
                for b in range(BLOCKS):
                    for m in range(KD):
                        n = b * KD + m
                        sp.wait_ge(q_ok, n + 1)
                        nt = len(tiles_of(b))
                        sp.dma_start(scr["q"][BT * b:BT * b + nt, :, m].rearrange("t p n -> p t n"),
                                     st[:, n % 2, 0:nt * P].rearrange("p (t n) -> p t n", t=nt)).then_inc(q_st[n % 2], 16)
                        if m % 2 and BT * (b + 2) + m // 2 < TILES:
                            load(BT * (b + 2) + m // 2)
                for i in range(2):
                    sp.wait_ge(q_st[i], BLOCKS * KD // 2 * 16)

            @block.scalar
            def _(act):
                def upper_half(t):
                    b, j = divmod(t, BT)
                    act.wait_ge(h_in[t % 3], 16 * (t // 3 + 1))
                    if b >= 2:
                        act.wait_ge(mm, (b - 1) * KD)
                    nc.scalar.activation(h[:, b % 2, 0, j], t_in[:, t % 3], ACT.Copy).then_inc(hi_ok, 1)
                act.wait_ge(g_in, 16)
                for t in range(3):
                    upper_half(t)
                for k in range(KD):
                    act.wait_ge(raw_in[k % 2], 16 * (k // 2 + 1))
                    nc.scalar.activation(w_hi[:, k], raw[:, k % 2], ACT.Copy, scale=g[:, k:k + 1]).then_inc(whi_ok, 1)
                upper_half(3)
                for b in range(BLOCKS):
                    for m in range(KD):
                        n = b * KD + m
                        act.wait_ge(mm, n + 1)
                        if n >= 2:
                            act.wait_ge(q_st[n % 2], 16 * (n // 2))
                        wide = P * len(tiles_of(b))
                        nc.scalar.activation(st[:, n % 2, 0:wide], acc[:, n % 4, 0:wide], ACT.Copy).then_inc(q_ok, 1)
                        if m % 2 and BT * (b + 1) + m // 2 < TILES:
                            upper_half(BT * (b + 1) + m // 2)

            @block.vector
            def _(dve):
                def lower_half(t):
                    b, j = divmod(t, BT)
                    dve.wait_ge(hi_ok, t + 1)
                    nc.vector.tensor_tensor(h[:, b % 2, 1, j], t_in[:, t % 3], h[:, b % 2, 0, j].bitcast(F32), ALU.subtract).then_inc(lo_ok, 1)
                for t in range(3):
                    lower_half(t)
                for k in range(KD):
                    dve.wait_ge(whi_ok, k + 1)
                    nc.vector.scalar_tensor_tensor(w_lo[:, k], raw[:, k % 2], g[:, k:k + 1], w_hi[:, k].bitcast(F32),
                                                   ALU.mult, ALU.subtract).then_inc(wlo_ok, 1)
                for t in range(3, TILES):
                    lower_half(t)

            @block.tensor
            def _(pe):
                for b in range(BLOCKS):
                    nt = len(tiles_of(b))
                    pe.wait_ge(lo_ok, tiles_of(b)[-1] + 1)
                    for m in range(KD):
                        n = b * KD + m
                        if n >= 4:
                            pe.wait_ge(q_ok, n - 3)
                        for k in range(KD):
                            if n == 0:
                                pe.wait_ge(wlo_ok, k + 1)
                            cols = slice(m * P, (m + 1) * P)
                            ins = product3(nc, acc[:, n % 4, 0:nt * P], w_hi[:, k, cols], w_lo[:, k, cols],
                                           h[:, b % 2, 0, 0:nt, k], h[:, b % 2, 1, 0:nt, k], k == 0, k == KD - 1)
                        ins.then_inc(mm, 1)


def attention(nc, outer, io, scr):
    sem = lambda n: outer.new("s7_" + n)
    with ExitStack() as ctx:
        room = Room(nc, ctx, "s7")
        sb, ps = room.sb, room.ps
        SCALE = float(HD) ** -0.5
        RB = 32
        PB = 2
        NS = 4
        ident = sb("ident", [P, P])
        rawkv = sb("rawkv", [P, 2, 2, D])
        k_hi, k_lo = sb("k_hi", [P, KD, MEM], F32R), sb("k_lo", [P, KD, MEM], F32R)
        v_hi, v_lo = sb("v_hi", [P, 2, D], F32R), sb("v_lo", [P, 2, D], F32R)
        q = sb("q", [P, 2, KD, P])
        q_hi, q_lo = sb("q_hi", [P, 2, KD, P], F32R), sb("q_lo", [P, 2, KD, P], F32R)
        prob = sb("prob", [P, 2, D])
        top, ntop, den, rden = (sb(n, [P, 2, HEADS]) for n in ("top", "ntop", "den", "rden"))
        pt = sb("pt", [P, 2, 2, KD, PB * P], F32R)
        ost = sb("ost", [P, 2, PB * P])
        sq = sb("sq", [P, KD, P])
        sqs = sb("sqs", [P, KD, STREAMS, RB])
        skT = sb("skT", [P, NS, KD, MEM])
        sval = sb("sval", [P, NS, 2, D])
        spt = sb("spt", [P, KD, P])
        sot = sb("sot", [P, KD, STEP, STREAMS])
        score = ps("score", [P, 2, 2, 512])
        tr = ps("tr", [P, 2, 512])
        o_ps = ps("o", [P, 2, 512])

        ident0, ident_ok, kv_in, khi_ok, klo_ok = (sem(n) for n in ("ident0", "ident", "kv_in", "khi", "klo"))
        q_in, qhi_ok, qlo_ok = [sem(f"q_in{i}") for i in range(2)], sem("qhi"), sem("qlo")
        sq_in, zero_ok, sqs_ok, sk_in, sv_in = sem("sq_in"), sem("zero"), sem("sqs"), [sem(f"sk_in{i}") for i in range(2)], [sem(f"sv_in{i}") for i in range(2)]
        sc_mm, top_ok, ntop_ok, exp_ok, rden_ok, prob_ok = (sem(n) for n in ("sc_mm", "top", "ntop", "exp", "rden", "prob"))
        turned, hi_ok, taken, o_mm, o_ok = (sem(n) for n in ("turned", "hi", "taken", "o_mm", "o"))
        o_st, stored = [sem(f"o_st{i}") for i in range(2)], sem("stored")

        tiles = [*range(8), ("streams", 0), *range(8, STEP), ("streams", 1)]
        keys_at = {i + i // 8: divmod(i, 2) for i in range(2 * STREAMS)}

        class Step:
            pass

        steps, waiting, streams_next, turns, outs = [], [], None, 0, 0
        for i in range(len(tiles) + 4):
            s = Step()
            s.i = i
            s.tile = tiles[i] if i < len(tiles) else None
            s.keys, s.keys_turn = keys_at.get(i), turns
            turns += 2 if s.keys is not None else 0
            s.outs, waiting, s.out_n = waiting[:4], waiting[4:], outs
            outs += len(s.outs)
            s.streams, s.streams_n = streams_next, outs
            outs += NS if streams_next is not None else 0
            s.turn = tiles[i - 1] if 0 < i <= len(tiles) else None
            s.turn_n = turns
            turns += 2 if s.turn is not None else 0
            streams_next = s.turn[1] if isinstance(s.turn, tuple) else None
            if isinstance(s.turn, int) and s.turn % PB == PB - 1:
                s_pair = s.turn // PB
                waiting = waiting + [(s_pair, m) for m in range(KD)]
            steps.append(s)
        turn_of = {s.turn: s.turn_n for s in steps if s.turn is not None}
        out_of = {key: s.out_n + k for s in steps for k, key in enumerate(s.outs)}
        streams_of = {s.streams: s.streams_n for s in steps if s.streams is not None}
        keys_turn_of = {s.keys: s.keys_turn for s in steps if s.keys is not None}
        place = {t: i for i, t in enumerate(tiles)}

        with nc.Block() as block:

            @block.sync
            def _(sp):
                sp.dma_start(rawkv[:, 0].rearrange("p t n -> p (t n)"), scr["kT"].rearrange("p k n -> p (k n)")).then_inc(kv_in, 16)
                sp.dma_start(rawkv[:, 1], scr["v"]).then_inc(kv_in, 16)

                def load_queries(t):
                    if t >= 2:
                        sp.wait_ge(qlo_ok, t - 1)
                    sp.dma_start(q[:, t % 2], scr["q"][t]).then_inc(q_in[t % 2], 16)

                def load_keys(b):
                    if b >= 2:
                        sp.wait_ge(turned, keys_turn_of[b - 2, 1] + 2)
                    else:
                        sp.wait_ge(klo_ok, 2)
                    sp.dma_start(rawkv[:, b % 2], io["cache_mem_k"][0, b].rearrange("(t p) h e -> p t (h e)", p=P)).then_inc(sk_in[b % 2], 16)

                def load_values(half):
                    if half:
                        sp.wait_ge(o_mm, streams_of[0] + NS)
                    for b in range(NS):
                        sp.dma_start(sval[:, b], io["cache_mem_v"][0, NS * half + b].rearrange("(t p) h e -> p t (h e)", p=P)).then_inc(sv_in[half], 16)

                load_queries(0)
                load_queries(1)
                sp.dma_start(sq[:], scr["q"][STEP]).then_inc(sq_in, 16)
                load_keys(0)
                load_keys(1)
                load_values(0)
                for s in steps:
                    if isinstance(s.tile, int) and s.tile + 2 < STEP:
                        load_queries(s.tile + 2)
                    if s.keys is not None and s.keys[1] and s.keys[0] + 2 < STREAMS:
                        load_keys(s.keys[0] + 2)
                    for pair, m in s.outs:
                        n = pair * KD + m
                        sp.wait_ge(o_ok, out_of[pair, m] + 1)
                        sp.dma_start(scr["o"][PB * pair:PB * pair + PB, :, m].rearrange("t p n -> p t n"),
                                     ost[:, n % 2].rearrange("p (t n) -> p t n", t=PB)).then_inc(o_st[n % 2], 16)
                    if s.streams == 0:
                        load_values(1)
                sp.wait_ge(o_ok, streams_of[1] + NS)
                sp.dma_start(scr["o"][STEP].rearrange("p m n -> p (m n)"), sot[:].rearrange("p m j b -> p (m j b)")).then_inc(stored, 16)
                sp.wait_ge(stored, 16)
                for i in range(2):
                    sp.wait_ge(o_st[i], STEP // PB * KD // 2 * 16)

            @block.gpsimd
            def _(pool):
                identity_matrix(nc, pool, ident, ident0, ident_ok)
                nc.gpsimd.memset(sqs[:, :, :, STEP:RB], 0.0).then_inc(zero_ok, 1)

            @block.scalar
            def _(act):
                def query_half(t):
                    act.wait_ge(q_in[t % 2], 16 * (t // 2 + 1))
                    if t >= 2:
                        act.wait_ge(sc_mm, place[t - 2] + 1)
                    nc.scalar.activation(q_hi[:, t % 2], q[:, t % 2], ACT.Copy).then_inc(qhi_ok, 1)

                def exponentials(u, heads):
                    act.wait_ge(ntop_ok, u + 1)
                    if u >= 2:
                        act.wait_ge(turned, turn_of[tiles[u - 2]] + 2)
                    for hd in heads:
                        cols = slice(hd * MEM, (hd + 1) * MEM)
                        nc.scalar.activation(prob[:, u % 2, cols], score[:, u % 2, hd // 2, (hd % 2) * MEM:(hd % 2 + 1) * MEM], ACT.Exp,
                                             bias=ntop[:, u % 2, hd:hd + 1], scale=SCALE,
                                             accum_out=den[:, u % 2, hd:hd + 1]).then_inc(exp_ok, 1)

                def upper_half(t, turn):
                    pair, j = divmod(t, PB)
                    for a in range(2):
                        act.wait_ge(turned, turn + a + 1)
                        if pair >= 2:
                            act.wait_ge(o_mm, out_of[pair - 2, KD - 1] + 1)
                        nc.scalar.activation(pt[:, pair % 2, 0, 4 * a:4 * a + 4, j * P:(j + 1) * P],
                                             tr[:, (turn + a) % 2].rearrange("p (k n) -> p k n", k=4), ACT.Copy).then_inc(hi_ok, 1)

                def output_copy(pair, m):
                    n, use = pair * KD + m, out_of[pair, m]
                    act.wait_ge(o_mm, use + 1)
                    if n >= 2:
                        act.wait_ge(o_st[n % 2], 16 * (n // 2))
                    nc.scalar.activation(ost[:, n % 2], o_ps[:, use % 2, 0:PB * P], ACT.Copy).then_inc(o_ok, 1)

                act.wait_ge(kv_in, 32)
                nc.scalar.activation(k_hi[:].rearrange("p k n -> p (k n)"), rawkv[:, 0].rearrange("p t n -> p (t n)"), ACT.Copy).then_inc(khi_ok, 1)
                query_half(0)
                nc.scalar.activation(v_hi[:], rawkv[:, 1], ACT.Copy).then_inc(khi_ok, 1)
                query_half(1)
                for s in steps:
                    if s.tile is not None:
                        exponentials(s.i, (0, 1))
                    for pair, m in s.outs[0:2]:
                        output_copy(pair, m)
                    if s.tile is not None:
                        exponentials(s.i, (2, 3))
                    for pair, m in s.outs[2:4]:
                        output_copy(pair, m)
                    if s.streams is not None:
                        for b in range(NS):
                            use = s.streams_n + b
                            act.wait_ge(o_mm, use + 1)
                            nc.scalar.activation(sot[:, :, :, NS * s.streams + b],
                                                 o_ps[:, use % 2, 0:KD * STEP].rearrange("p (m j) -> p m j", m=KD), ACT.Copy).then_inc(o_ok, 1)
                    if isinstance(s.turn, int):
                        upper_half(s.turn, s.turn_n)
                    if isinstance(s.tile, int) and s.tile + 2 < STEP:
                        query_half(s.tile + 2)

            @block.vector
            def _(dve):
                def query_half(t):
                    dve.wait_ge(qhi_ok, t + 1)
                    nc.vector.tensor_tensor(q_lo[:, t % 2], q[:, t % 2], q_hi[:, t % 2].bitcast(F32), ALU.subtract).then_inc(qlo_ok, 1)

                def maxima(u):
                    dve.wait_ge(sc_mm, u + 1)
                    if u >= 2:
                        dve.wait_ge(exp_ok, HEADS * (u - 1))
                    nc.vector.reduce_max(top[:, u % 2], score[:, u % 2].rearrange("p a (b n) -> p (a b) n", b=2), AX_X).then_inc(top_ok, 1)
                    dve.wait_ge(top_ok, u + 1)
                    nc.vector.tensor_scalar(ntop[:, u % 2], top[:, u % 2], -SCALE, None, ALU.mult).then_inc(ntop_ok, 1)

                def normalise(u):
                    dve.wait_ge(exp_ok, HEADS * (u + 1))
                    nc.vector.reciprocal(rden[:, u % 2], den[:, u % 2]).then_inc(rden_ok, 1)
                    dve.wait_ge(rden_ok, u + 1)
                    for hd in range(HEADS):
                        cols = prob[:, u % 2, hd * MEM:(hd + 1) * MEM]
                        nc.vector.tensor_scalar(cols, cols, rden[:, u % 2, hd:hd + 1], None, ALU.mult).then_inc(prob_ok, 1)

                def lower_half(t, turn):
                    pair, j = divmod(t, PB)
                    for a in range(2):
                        dve.wait_ge(hi_ok, 2 * t + a + 1)
                        to = lambda half: pt[:, pair % 2, half, 4 * a:4 * a + 4, j * P:(j + 1) * P]
                        nc.vector.tensor_tensor(to(1), tr[:, (turn + a) % 2].rearrange("p (k n) -> p k n", k=4), to(0).bitcast(F32),
                                                ALU.subtract).then_inc(taken, 1)

                dve.wait_ge(khi_ok, 2)
                nc.vector.tensor_tensor(k_lo[:].rearrange("p k n -> p (k n)"), rawkv[:, 0].rearrange("p t n -> p (t n)"),
                                        k_hi[:].rearrange("p k n -> p (k n)").bitcast(F32), ALU.subtract).then_inc(klo_ok, 1)
                query_half(0)
                nc.vector.tensor_tensor(v_lo[:], rawkv[:, 1], v_hi[:].bitcast(F32), ALU.subtract).then_inc(klo_ok, 1)
                query_half(1)
                query_next = None
                for s in steps:
                    if s.tile is not None:
                        maxima(s.i)
                    if s.i == 1:
                        dve.wait_ge(sq_in, 16)
                        for b in range(STREAMS):
                            nc.vector.tensor_copy(sqs[:, :, b, 0:STEP], sq[:].rearrange("p k (j b) -> p k j b", b=STREAMS)[:, :, :, b]).then_inc(sqs_ok, 1)
                    if s.keys is not None:
                        b, half = s.keys
                        for a in range(2):
                            c = 2 * half + a
                            dve.wait_ge(turned, s.keys_turn + a + 1)
                            if b >= NS:
                                dve.wait_ge(sc_mm, place["streams", 0] + 1)
                            nc.vector.tensor_copy(skT[:, b % NS, 2 * c:2 * c + 2].rearrange("p k n -> p (k n)"),
                                                  tr[:, (s.keys_turn + a) % 2]).then_inc(taken, 1)
                    if query_next is not None:
                        query_half(query_next)
                    query_next = s.tile + 2 if isinstance(s.tile, int) and s.tile + 2 < STEP else None
                    if s.tile is not None:
                        normalise(s.i)
                    if isinstance(s.turn, int):
                        lower_half(s.turn, s.turn_n)
                    elif s.turn is not None:
                        for a in range(2):
                            dve.wait_ge(turned, s.turn_n + a + 1)
                            if s.turn[1]:
                                dve.wait_ge(o_mm, streams_of[0] + NS)
                            nc.vector.tensor_copy(spt[:, 4 * a:4 * a + 4].rearrange("p k n -> p (k n)"), tr[:, (s.turn_n + a) % 2]).then_inc(taken, 1)

            @block.tensor
            def _(pe):
                def bank_free(turn):
                    if turn >= 2:
                        pe.wait_ge(taken, turn - 1)

                def prompt_scores(t, u):
                    pe.wait_ge(qlo_ok, t + 1)
                    for hd in range(HEADS):
                        for k in (2 * hd, 2 * hd + 1):
                            ins = product3(nc, score[:, u % 2, hd // 2, (hd % 2) * MEM:(hd % 2 + 1) * MEM], q_hi[:, t % 2, k],
                                           q_lo[:, t % 2, k], k_hi[:, k], k_lo[:, k], k % 2 == 0, k % 2 == 1)
                    ins.then_inc(sc_mm, 1)

                def stream_scores(half, u):
                    pe.wait_ge(taken, keys_turn_of[NS * half + NS - 1, 1] + 2)
                    pe.wait_ge(sqs_ok, STREAMS)
                    pe.wait_ge(zero_ok, 1)
                    for b in range(NS):
                        rows = slice(RB * b, RB * b + RB)
                        for hd in range(HEADS):
                            for k in (2 * hd, 2 * hd + 1):
                                ins = nc.tensor.matmul(score[rows, u % 2, hd // 2, (hd % 2) * MEM:(hd % 2 + 1) * MEM],
                                                       sqs[:, k, NS * half + b], skT[:, b, k], start=k % 2 == 0, stop=k % 2 == 1)
                    ins.then_inc(sc_mm, 1)

                def turn_keys(b, half, turn):
                    pe.wait_ge(sk_in[b % 2], 16 * (b // 2 + 1))
                    for a in range(2):
                        c = 2 * half + a
                        bank_free(turn + a)
                        for k in (2 * c, 2 * c + 1):
                            for t in range(2):
                                ins = nc.tensor.transpose(tr[:, (turn + a) % 2, (k % 2) * MEM + t * P:(k % 2) * MEM + (t + 1) * P],
                                                          rawkv[:, b % 2, t, k * P:(k + 1) * P], ident[:])
                        ins.then_inc(turned, 1)

                def turn_probabilities(u, turn):
                    pe.wait_ge(prob_ok, HEADS * (u + 1))
                    for a in range(2):
                        bank_free(turn + a)
                        for k in range(4 * a, 4 * a + 4):
                            ins = nc.tensor.transpose(tr[:, (turn + a) % 2, (k % 4) * P:(k % 4 + 1) * P], prob[:, u % 2, k * P:(k + 1) * P], ident[:])
                        ins.then_inc(turned, 1)

                def outputs(pair, m):
                    use = out_of[pair, m]
                    pe.wait_ge(klo_ok, 2)
                    pe.wait_ge(taken, turn_of[PB * pair + PB - 1] + 2)
                    if use >= 2:
                        pe.wait_ge(o_ok, use - 1)
                    for kt in range(2):
                        cols = slice(m * P, (m + 1) * P)
                        row = (m // 2) * 2 + kt
                        ins = product3(nc, o_ps[:, use % 2, 0:PB * P], v_hi[:, kt, cols], v_lo[:, kt, cols], pt[:, pair % 2, 0, row],
                                       pt[:, pair % 2, 1, row], kt == 0, kt == 1)
                    ins.then_inc(o_mm, 1)

                def stream_outputs(half, use0):
                    pe.wait_ge(taken, turn_of["streams", half] + 2)
                    pe.wait_ge(sv_in[half], 16 * NS)
                    for b in range(NS):
                        use = use0 + b
                        if use >= 2:
                            pe.wait_ge(o_ok, use - 1)
                        for m in range(KD):
                            for t in range(2):
                                ins = nc.tensor.matmul(o_ps[:, use % 2, m * STEP:(m + 1) * STEP], sval[:, b, t, m * P:(m + 1) * P],
                                                       spt[:, (m // 2) * 2 + t, RB * b:RB * b + STEP], start=t == 0, stop=t == 1)
                        ins.then_inc(o_mm, 1)

                pe.wait_ge(ident_ok, 1)
                pe.wait_ge(klo_ok, 1)
                for s in steps:
                    if s.tile is not None:
                        if s.i >= 2:
                            pe.wait_ge(exp_ok, HEADS * (s.i - 1))
                        if isinstance(s.tile, int):
                            prompt_scores(s.tile, s.i)
                        else:
                            stream_scores(s.tile[1], s.i)
                    if s.keys is not None:
                        turn_keys(*s.keys, s.keys_turn)
                    for pair, m in s.outs:
                        outputs(pair, m)
                    if s.streams is not None:
                        stream_outputs(s.streams, s.streams_n)
                    if s.turn is not None:
                        turn_probabilities(s.i - 1, s.turn_n)


def mlp(nc, outer, io, scr):
    sem = lambda n: outer.new("s9_" + n)
    FC = 256
    FT = FC // P
    CHUNKS = FF // FC
    BM = 3
    WB = BM * P
    GROUP = 9
    J = GROUP // BM
    with ExitStack() as ctx:
        room = Room(nc, ctx, "s9")
        sb, ps = room.sb, room.ps
        g = sb("g", [P, KD])
        g_last = sb("g_last", [P, D])
        expo = sb("expo", [P, 1])
        stat = sb("stat", [P, 3, GROUP])
        xs = sb("xs", [P, GROUP, D])
        h_hi, h_lo = sb("h_hi", [P, GROUP, KD, P], F32R), sb("h_lo", [P, GROUP, KD, P], F32R)
        up_raw, dn_raw = sb("up_raw", [P, KD, FC]), sb("dn_raw", [P, FT, D])
        up_hi, up_lo = sb("up_hi", [P, 2, KD, FC], F32R), sb("up_lo", [P, 2, KD, FC], F32R)
        dn_hi, dn_lo = sb("dn_hi", [P, 2, FT, D], F32R), sb("dn_lo", [P, 2, FT, D], F32R)
        r = sb("r", [P, FT, WB])
        a_hi, a_lo = sb("a_hi", [P, 2, FT, WB], F32R), sb("a_lo", [P, 2, FT, WB], F32R)
        up_ps = ps("up", [P, 4, 512])
        dn_ps = ps("dn", [P, 2, 2, 512])

        g_in, gl_in = sem("g_in"), sem("gl_in")
        h_in, x_in, y_st = ([sem(f"{n}{t}") for t in range(GROUP)] for n in ("h_in", "x_in", "y_st"))
        hhi_ok, hlo_ok = sem("hhi"), sem("hlo")
        up_in, dn_in, uphi_ok, uplo_ok, dnhi_ok, dnlo_ok = (sem(n) for n in ("up_in", "dn_in", "uphi", "uplo", "dnhi", "dnlo"))
        up_mm, relu_ok, sq_ok, ahi_ok, alo_ok, dn_mm, sum_ok = (
            sem(n) for n in ("up_mm", "relu", "sq", "ahi", "alo", "dn_mm", "sum"))
        expo_ok, sumsq, var, rstd, y_ok = sem("expo"), sem("sumsq"), sem("var"), sem("rstd"), sem("y")

        groups = [(0, GROUP), (GROUP, TILES - GROUP)]
        landing = [up_raw[:, 0:4].rearrange("p k f -> p (k f)"), up_raw[:, 4:8].rearrange("p k f -> p (k f)"), dn_raw[:, 0], dn_raw[:, 1]]
        land_in = [sem(f"land_in{i}") for i in range(4)]
        early_norms = range(0, 2 * BM)
        h_block = lambda j: range(j * BM, min((j + 1) * BM, groups[1][1]))

        class Place:

            def __init__(self, gi, c, odd, j):
                self.t0, self.nt = groups[gi]
                self.sizes = [min(BM, self.nt - BM * i) for i in range(J)]
                self.gi, self.c, self.odd, self.j = gi, c, odd, j
                self.chunk = gi * CHUNKS + c
                self.block = self.chunk * J + j
                self.side = (odd * J + j) % 2
                self.before = sum(self.sizes[:j])
                self.tile = gi * CHUNKS * GROUP + c * self.nt + self.before
                self.size = self.sizes[j]
                self.wide = self.size * P
                self.early = gi == 0 and isinstance(c, int) and c * J + j < 2

            def back(self, n):
                gi, c, odd, j = self.gi, self.c, self.odd, self.j - n
                while j < 0:
                    c, odd, j = c - 1, 1 - odd, j + J
                if isinstance(c, int) and c < 0:
                    gi, c = gi - 1, c + CHUNKS
                return Place(gi, c, odd, j)

            def tiles_two_blocks_ago(self):
                p = self.back(2)
                return p.tile + p.size

        def over_chunks(eng, gi, body):
            for c in (0, 1):
                body(gi, c, c)
            with eng.Fori(1, CHUNKS // 2 - 1) as pair:
                for odd in range(2):
                    body(gi, 2 * pair + odd, odd)
            for c in (CHUNKS - 2, CHUNKS - 1):
                body(gi, c, c % 2)

        with nc.Block() as block:

            @block.sync
            def _(sp):
                up = io["w_up"][0].rearrange("(k p) (c f) -> c p k f", p=P, f=FC)
                down = io["w_down"][0].rearrange("(c t p) n -> c p t n", p=P, t=FT)
                yp = io["y_prompt"][0].rearrange("(c j) d -> j c d", j=STEP)
                ys = io["y_sample"].rearrange("b j d -> j b d")
                sp.dma_start(g[:], io["g_mlp"][0].rearrange("(k p) -> p k", p=P), allow_slow_non_contiguous=True).then_inc(g_in, 16)
                sp.dma_start(up_raw[:], up[0]).then_inc(up_in, 16)
                sp.dma_start(dn_raw[:], down[0]).then_inc(dn_in, 16)
                sp.dma_start(g_last[:], io["g_final"].partition_broadcast(P)).then_inc(gl_in, 16)
                def load_weights(gi, c):
                    n = gi * CHUNKS + c
                    sp.wait_ge(uplo_ok, KD * n)
                    sp.dma_start(up_raw[:], up[c]).then_inc(up_in, 16)
                    sp.wait_ge(dnlo_ok, FT * n)
                    sp.dma_start(dn_raw[:], down[c]).then_inc(dn_in, 16)

                def store_rows(gi, tiles):
                    t0 = groups[gi][0]
                    for t in tiles:
                        sp.wait_ge(y_ok, t0 + t + 1)
                        sp.dma_start(yp[t0 + t] if t0 + t < STEP else ys, xs[:, t]).then_inc(y_st[t], 16)

                def load_rows(gi, tiles):
                    for t in tiles:
                        if gi:
                            sp.wait_ge(y_st[t], 16)
                        else:
                            sp.wait_ge(hlo_ok, t + 1)
                        sp.dma_start(xs[:, t], scr["x2"][groups[gi][0] + t]).then_inc(x_in[t], 16)

                for t in range(GROUP):
                    sp.dma_start(xs[:, t].rearrange("p (k n) -> p k n", k=KD), scr["h2"][t]).then_inc(h_in[t], 16)
                load_rows(0, range(GROUP))
                with sp.Fori(1, CHUNKS) as c:
                    load_weights(0, c)
                load_weights(1, 0)
                for i in range(groups[1][1]):
                    if i < 4:
                        sp.wait_ge(*((uplo_ok, KD * (CHUNKS + 1)) if i < 2 else (dnlo_ok, FT * (CHUNKS + 1))))
                    else:
                        sp.wait_ge(hlo_ok, GROUP + i - 3)
                    sp.dma_start(landing[i % 4], scr["h2"][GROUP + i].rearrange("p k n -> p (k n)")).then_inc(land_in[i % 4], 16)
                store_rows(0, early_norms)
                load_rows(1, early_norms)
                sp.wait_ge(hlo_ok, TILES)
                sp.wait_ge(uplo_ok, KD * (CHUNKS + 1))
                sp.dma_start(up_raw[:], up[1]).then_inc(up_in, 16)
                store_rows(0, range(2 * BM, GROUP))
                load_rows(1, range(2 * BM, groups[1][1]))
                sp.wait_ge(dnlo_ok, FT * (CHUNKS + 1))
                sp.dma_start(dn_raw[:], down[1]).then_inc(dn_in, 16)
                with sp.Fori(2, CHUNKS) as c:
                    load_weights(1, c)
                store_rows(1, range(groups[1][1]))
                for t in range(GROUP):
                    sp.wait_ge(y_st[t], 32 if t < groups[1][1] else 16)

            @block.gpsimd
            def _(pool):
                nc.gpsimd.memset(expo[:], -0.5).then_inc(expo_ok, 1)
                pool.wait_ge(expo_ok, 1)
                for t0, nt in groups:
                    for t in range(nt):
                        pool.wait_ge(var, t0 + t + 1)
                        nc.gpsimd.tensor_tensor(stat[:, 2, t:t + 1], stat[:, 1, t:t + 1], expo[:], ALU.pow).then_inc(rstd, 1)

            @block.scalar
            def _(act):
                def split_up(gi, c, odd):
                    n = gi * CHUNKS + c
                    act.wait_ge(up_in, 16 * (n + 1))
                    if not isinstance(n, int) or n >= 2:
                        act.wait_ge(up_mm, FT * J * (n - 1))
                    for k in range(KD):
                        nc.scalar.activation(up_hi[:, odd, k], up_raw[:, k], ACT.Copy, scale=g[:, k:k + 1]).then_inc(uphi_ok, 1)

                def split_down(gi, c, odd):
                    n = gi * CHUNKS + c
                    act.wait_ge(dn_in, 16 * (n + 1))
                    if not isinstance(n, int) or n >= 2:
                        before = n * GROUP if gi == 0 else CHUNKS * GROUP + c * groups[1][1]
                        act.wait_ge(dn_mm, before - groups[gi][1] if not isinstance(c, int) or c >= 1 else before - GROUP)
                    for k in range(FT):
                        nc.scalar.activation(dn_hi[:, odd, k], dn_raw[:, k], ACT.Copy).then_inc(dnhi_ok, 1)

                def hidden(at):
                    for f in range(FT):
                        act.wait_ge(up_mm, FT * at.block + f + 1)
                        if not isinstance(at.block, int) or at.block >= 1:
                            act.wait_ge(alo_ok, FT * at.block + f - 1)
                        nc.scalar.activation(r[:, f, 0:at.wide], up_ps[:, 2 * at.side + f, 0:at.wide], ACT.Relu).then_inc(relu_ok, 1)
                    if at.gi or not at.early:
                        act.wait_ge(dn_mm, at.tiles_two_blocks_ago())
                    for f in range(FT):
                        act.wait_ge(sq_ok, FT * at.block + f + 1)
                        nc.scalar.activation(a_hi[:, at.side, f, 0:at.wide], r[:, f, 0:at.wide], ACT.Copy).then_inc(ahi_ok, 1)

                def landed_halves(tiles):
                    for i in tiles:
                        act.wait_ge(land_in[i % 4], 16 * (i // 4 + 1))
                        nc.scalar.activation(h_hi[:, i].rearrange("p k n -> p (k n)"), landing[i % 4], ACT.Copy).then_inc(hhi_ok, 1)

                def squares(gi, tiles):
                    t0, nt = groups[gi]
                    for t in tiles:
                        act.wait_ge(sum_ok, gi * CHUNKS * GROUP + (CHUNKS - 1) * nt + t + 1)
                        if t0 + t:
                            act.wait_ge(sumsq, t0 + t)
                        nc.scalar.activation(h_hi[:, GROUP - 1].rearrange("p k n -> p (k n)"), xs[:, t], ACT.Square,
                                             accum_out=stat[:, 0, t:t + 1]).then_inc(sumsq, 1)

                def chunk(gi, c, odd):
                    hidden(Place(gi, c, odd, 0))
                    if gi == 1 and isinstance(c, int) and c == 0:
                        squares(0, range(2 * BM, GROUP))
                    if isinstance(c, int) and c == CHUNKS - 1:
                        if gi == 0:
                            split_up(1, 0, 0)
                            landed_halves((0, 1))
                            split_down(1, 0, 0)
                            landed_halves((2,))
                        hidden(Place(gi, c, odd, 1))
                        if gi == 0:
                            landed_halves(h_block(1))
                        hidden(Place(gi, c, odd, 2))
                        if gi == 0:
                            landed_halves(h_block(2))
                        squares(gi, early_norms)
                    else:
                        split_up(gi, c + 1, 1 - odd)
                        hidden(Place(gi, c, odd, 1))
                        split_down(gi, c + 1, 1 - odd)
                        hidden(Place(gi, c, odd, 2))

                act.wait_ge(g_in, 16)
                split_up(0, 0, 0)
                for t in range(GROUP):
                    act.wait_ge(h_in[t], 16)
                    nc.scalar.activation(h_hi[:, t].rearrange("p k n -> p (k n)"), xs[:, t], ACT.Copy).then_inc(hhi_ok, 1)
                split_down(0, 0, 0)
                over_chunks(act, 0, chunk)
                over_chunks(act, 1, chunk)
                squares(1, range(2 * BM, groups[1][1]))

            @block.vector
            def _(dve):
                def split_up(gi, c, odd):
                    n = gi * CHUNKS + c
                    for k in range(KD):
                        dve.wait_ge(uphi_ok, KD * n + k + 1)
                        nc.vector.scalar_tensor_tensor(up_lo[:, odd, k], up_raw[:, k], g[:, k:k + 1], up_hi[:, odd, k].bitcast(F32),
                                                       ALU.mult, ALU.subtract).then_inc(uplo_ok, 1)

                def split_down(gi, c, odd):
                    n = gi * CHUNKS + c
                    for k in range(FT):
                        dve.wait_ge(dnhi_ok, FT * n + k + 1)
                        nc.vector.tensor_tensor(dn_lo[:, odd, k], dn_raw[:, k], dn_hi[:, odd, k].bitcast(F32), ALU.subtract).then_inc(dnlo_ok, 1)

                def hidden(at):
                    for f in range(FT):
                        dve.wait_ge(relu_ok, FT * at.block + f + 1)
                        rf = r[:, f, 0:at.wide]
                        nc.vector.scalar_tensor_tensor(rf, up_ps[:, 2 * at.side + f, 0:at.wide], 0.0, rf, ALU.max, ALU.mult).then_inc(sq_ok, 1)
                    for f in range(FT):
                        dve.wait_ge(ahi_ok, FT * at.block + f + 1)
                        nc.vector.tensor_tensor(a_lo[:, at.side, f, 0:at.wide], r[:, f, 0:at.wide], a_hi[:, at.side, f, 0:at.wide].bitcast(F32),
                                                ALU.subtract).then_inc(alo_ok, 1)

                def sums(at):
                    for i in range(at.size):
                        t = at.before + i
                        dve.wait_ge(dn_mm, at.tile + i + 1)
                        if isinstance(at.c, int) and at.c == 0:
                            dve.wait_ge(x_in[t], 16 * (at.gi + 1))
                        else:
                            dve.wait_ge(sum_ok, at.tile + i + 1 - at.nt)
                        bank = (at.odd * at.nt + t) % 2
                        nc.vector.tensor_tensor(xs[:, t], xs[:, t], dn_ps[:, bank].rearrange("p a n -> p (a n)"), ALU.add).then_inc(sum_ok, 1)

                def landed_halves(tiles):
                    for i in tiles:
                        dve.wait_ge(hhi_ok, GROUP + i + 1)
                        nc.vector.tensor_tensor(h_lo[:, i].rearrange("p k n -> p (k n)"), landing[i % 4],
                                                h_hi[:, i].rearrange("p k n -> p (k n)").bitcast(F32), ALU.subtract).then_inc(hlo_ok, 1)

                def norms(gi, tiles):
                    t0 = groups[gi][0]
                    for t in tiles:
                        dve.wait_ge(sumsq, t0 + t + 1)
                        nc.vector.tensor_scalar(stat[:, 1, t:t + 1], stat[:, 0, t:t + 1], 1.0 / D, EPS, ALU.mult, ALU.add).then_inc(var, 1)
                        dve.wait_ge(rstd, t0 + t + 1)
                        nc.vector.scalar_tensor_tensor(xs[:, t], xs[:, t], stat[:, 2, t:t + 1], g_last[:], ALU.mult, ALU.mult).then_inc(y_ok, 1)

                def chunk(gi, c, odd):
                    hidden(Place(gi, c, odd, 0))
                    if gi == 1 or not isinstance(c, int) or c > 0:
                        sums(Place(gi, c, odd, 0).back(1))
                    if gi == 1 and isinstance(c, int) and c == 0:
                        norms(0, range(2 * BM, GROUP))
                    if isinstance(c, int) and c == CHUNKS - 1:
                        if gi == 0:
                            split_up(1, 0, 0)
                            landed_halves((0, 1))
                            split_down(1, 0, 0)
                            landed_halves((2,))
                        hidden(Place(gi, c, odd, 1))
                        sums(Place(gi, c, odd, 0))
                        if gi == 0:
                            landed_halves(h_block(1))
                        hidden(Place(gi, c, odd, 2))
                        sums(Place(gi, c, odd, 1))
                        if gi == 0:
                            landed_halves(h_block(2))
                        norms(gi, early_norms)
                    else:
                        split_up(gi, c + 1, 1 - odd)
                        hidden(Place(gi, c, odd, 1))
                        sums(Place(gi, c, odd, 0))
                        split_down(gi, c + 1, 1 - odd)
                        hidden(Place(gi, c, odd, 2))
                        sums(Place(gi, c, odd, 1))

                dve.wait_ge(g_in, 16)
                split_up(0, 0, 0)
                for t in range(GROUP):
                    dve.wait_ge(hhi_ok, t + 1)
                    nc.vector.tensor_tensor(h_lo[:, t].rearrange("p k n -> p (k n)"), xs[:, t],
                                            h_hi[:, t].rearrange("p k n -> p (k n)").bitcast(F32), ALU.subtract).then_inc(hlo_ok, 1)
                split_down(0, 0, 0)
                dve.wait_ge(gl_in, 16)
                over_chunks(dve, 0, chunk)
                over_chunks(dve, 1, chunk)
                sums(Place(1, CHUNKS - 1, 1, J - 1))
                norms(1, range(2 * BM, groups[1][1]))

            @block.tensor
            def _(pe):
                def up(at):
                    if at.j == 0:
                        pe.wait_ge(uplo_ok, KD * (at.chunk + 1))
                    if isinstance(at.c, int) and at.c == 0:
                        pe.wait_ge(hlo_ok, at.t0 + at.before + at.size)
                    if not isinstance(at.block, int) or at.block >= 2:
                        pe.wait_ge(sq_ok, FT * (at.block - 1))
                    tiles = slice(at.before, at.before + at.size)
                    for f in range(FT):
                        for k in range(KD):
                            cols = slice(f * P, (f + 1) * P)
                            ins = product3(nc, up_ps[:, 2 * at.side + f, 0:at.wide], up_hi[:, at.odd, k, cols], up_lo[:, at.odd, k, cols],
                                           h_hi[:, tiles, k], h_lo[:, tiles, k], k == 0, k == KD - 1)
                        ins.then_inc(up_mm, 1)

                def down(at):
                    if at.j == 0:
                        pe.wait_ge(dnlo_ok, FT * (at.chunk + 1))
                    pe.wait_ge(alo_ok, FT * (at.block + 1))
                    for i in range(at.size):
                        bank = (at.odd * at.nt + at.before + i) % 2
                        if not isinstance(at.tile, int) or at.tile + i >= 2:
                            pe.wait_ge(sum_ok, at.tile + i - 1)
                        rows = slice(i * P, (i + 1) * P)
                        for a in range(2):
                            cols = slice(a * 512, (a + 1) * 512)
                            for f in range(FT):
                                ins = product3(nc, dn_ps[:, bank, a], a_hi[:, at.side, f, rows], a_lo[:, at.side, f, rows],
                                               dn_hi[:, at.odd, f, cols], dn_lo[:, at.odd, f, cols], f == 0, f == FT - 1)
                        ins.then_inc(dn_mm, 1)

                def chunk(gi, c, odd):
                    for j in range(J):
                        at = Place(gi, c, odd, j)
                        up(at)
                        if gi == 1 or not isinstance(c, int) or c > 0 or j > 0:
                            down(at.back(1))

                over_chunks(pe, 0, chunk)
                over_chunks(pe, 1, chunk)
                down(Place(1, CHUNKS - 1, 1, J - 1))


def program(nc, io):
    with Semaphores(nc) as outer:
        scr = {
            "kT": nc.dram_tensor("scr_kT", (P, KD, MEM), F32).ap(),
            "v": nc.dram_tensor("scr_v", (P, 2, D), F32).ap(),
            "injT": nc.dram_tensor("scr_injT", (P, PAIRS, 4, P), F32).ap(),
            "turn": nc.dram_tensor("scr_turn", (P, 3, PAIRS), F32).ap(),
            "outm": nc.dram_tensor("scr_outm", (P, 2, PAIRS, STEP + 1, SG), F32).ap(),
            "taps": nc.dram_tensor("scr_taps", (SG, GROUPS, STEP, SG), F32).ap(),
        }
        scr["pow16"] = nc.dram_tensor("scr_pow16", (P, 2, PAIRS), F32).ap()
        scr["z"] = nc.dram_tensor("scr_z", (KD, P, STEP, NC), F32).ap()
        scr["y"] = nc.dram_tensor("scr_y", (4, P, STEP, NC), F32).ap()
        scr["c"] = nc.dram_tensor("scr_c", (TILES, P, KD, P), F32).ap()
        memory_and_tables(nc, outer, io, scr)
        first_input_projection(nc, outer, io, scr)
        mixers(nc, outer, io, scr)
        pooling(nc, outer, io, scr)
        for name in ("h", "q", "o", "h2"):
            scr[name] = nc.dram_tensor("scr_" + name, (TILES, P, KD, P), F32).ap()
        for name in ("x1", "x2"):
            scr[name] = nc.dram_tensor("scr_" + name, (TILES, P, D), F32).ap()
        xp, xs = io["x_prompt"][0].rearrange("(c j) d -> j c d", j=STEP), io["x_sample"].rearrange("b j d -> j b d")
        gelu_glu(nc, outer, io, scr)
        outer.clear()
        output_projection(nc, outer, io, scr, "s5", "w_out", scr["c"], lambda t: xs if isinstance(t, int) and t == STEP else xp[t],
                          scr["x1"], scr["h"])
        query_projection(nc, outer, io, scr)
        attention(nc, outer, io, scr)
        outer.clear()
        output_projection(nc, outer, io, scr, "s8", "w_o", scr["o"], lambda t: scr["x1"][t], scr["x2"], scr["h2"])
        mlp(nc, outer, io, scr)


_INS = ["x_prompt", "x_sample", "cache_mem_k", "cache_mem_v", "state_pool", "state_ssm_re", "state_ssm_im", "mem_prompt",
        "g_mix", "w_in", "w_pool", "pool_scale", "ssm_a_re", "ssm_a_im", "ssm_b_re", "ssm_b_im", "ssm_c_re", "ssm_c_im",
        "ssm_d", "ssm_log_dt", "w_glu", "b_glu", "w_out", "g_xattn", "g_mem", "w_q", "w_k", "w_v", "w_o", "g_mlp",
        "w_up", "w_down", "g_final"]
_OUTS = {
    "y_prompt": (1, SEQ, D), "y_sample": (STREAMS, STEP, D), "new_mem_k": (1, 1, MEM, HEADS, HD), "new_mem_v": (1, 1, MEM, HEADS, HD),
    "new_pool_p": (1, 1, HIST, DP), "new_ssm_re_p": (1, 1, GROUPS, SS), "new_ssm_im_p": (1, 1, GROUPS, SS),
    "new_pool_s": (1, STREAMS, HIST, DP), "new_ssm_re_s": (1, STREAMS, GROUPS, SS), "new_ssm_im_s": (1, STREAMS, GROUPS, SS),
}


def kernel(**inputs):
    import numpy as np
    import concourse.bacc as bacc
    from concourse.bass_utils import run_bass_kernel_spmd

    nc = bacc.Bacc("TRN2", target_bir_lowering=False, num_devices=1)
    arrays, io = {}, {}
    for name in _INS:
        a = np.ascontiguousarray(inputs[name])
        arrays[f"in_{name}_dram"] = a
        io[name] = nc.dram_tensor(f"in_{name}_dram", a.shape, mybir.dt.from_np(a.dtype), kind="ExternalInput").ap()
    for name, shape in _OUTS.items():
        io[name] = nc.dram_tensor(f"out_{name}_dram", shape, F32, kind="ExternalOutput").ap()
    program(nc, io)
    got = run_bass_kernel_spmd(nc, [arrays], core_ids=[0]).results[0]
    return tuple(got[f"out_{name}_dram"] for name in _OUTS)
```

```python
import math
from contextlib import ExitStack

import concourse.bass as bass
from concourse import mybir

F32 = mybir.dt.float32
F32R = mybir.dt.float32r
I32 = mybir.dt.int32
ALU = mybir.AluOpType
ACT = mybir.ActivationFunctionType
AX_X = mybir.AxisListType.X

P = 128
D = 1024
KD = D // P
SEQ = 2048
STREAMS = 8
STEP = 16
CH = SEQ // STEP
NC = CH + STREAMS
TILES = STEP + 1
DP = D // 2
GROUPS = 32
SG = 16
SS = 64
PAIRS = GROUPS // 2
HIST = 15
MEM = 256
HEADS = 4
HD = D // HEADS
FF = 4 * D
EPS = 1e-6
BT = 4
LN2_HI = 0.693359375
LN2_LO = math.log(2.0) - LN2_HI
TWO_PI_A = 6.28125
TWO_PI_B = 0.001934051513671875
TWO_PI_C = 2 * math.pi - TWO_PI_A - TWO_PI_B
MAGIC = 1.5 * 2.0 ** 23


class Room:

    def __init__(self, nc, ctx, tag):
        self.nc, self.ctx, self.tag = nc, ctx, tag

    def sb(self, name, shape, dt=F32):
        return self.ctx.enter_context(self.nc.sbuf_tensor(f"{self.tag}_{name}", shape, dt))

    def ps(self, name, shape, dt=F32):
        return self.ctx.enter_context(self.nc.psum_tensor(f"{self.tag}_ps_{name}", shape, dt))


class Semaphores:

    def __init__(self, nc):
        self.nc, self.held = nc, []

    def __enter__(self):
        return self

    def __exit__(self, *error):
        return False

    def new(self, name):
        self.held.append(self.nc.alloc_semaphore(name=name))
        return self.held[-1]

    def clear(self):
        self.nc.clear_and_free_semaphores(self.held)
        self.nc.all_engine_barrier()
        self.held = []


def product3(nc, out, w_hi, w_lo, x_hi, x_lo, first, last):
    nc.tensor.matmul(out, w_hi, x_hi, start=first, stop=False)
    nc.tensor.matmul(out, w_hi, x_lo, start=False, stop=False)
    return nc.tensor.matmul(out, w_lo, x_hi, start=False, stop=last)


def identity_matrix(nc, pool, ident, filled, done):
    nc.gpsimd.memset(ident[:], 0.0).then_inc(filled, 1)
    pool.wait_ge(filled, 1)
    nc.gpsimd.affine_select(out=ident[:], in_=ident[:], compare_op=ALU.not_equal, fill=1.0, base=0,
                            pattern=[[-1, P]], channel_multiplier=1).then_inc(done, 1)


def memory_and_tables(nc, outer, io, scr, phase):
    sem = lambda n: outer.new("s1_" + n)
    with ExitStack() as ctx:
        room = Room(nc, ctx, "s1")
        sb, ps = room.sb, room.ps
        ident = sb("ident", [P, P])
        memx = sb("memx", [P, 2, D])
        memT = sb("memT", [P, KD, MEM])
        kv = sb("kv", [P, 2, 2, D])
        kT = sb("kT", [P, KD, MEM])
        g_mem = sb("g_mem", [P, KD])
        wring = sb("wring", [P, 4, D])
        pn = sb("pn", [P, P])
        ldt = sb("ldt", [P, 2])
        pt = sb("pt", [P, P])
        braw = sb("braw", [P, 2, PAIRS, SG])
        cnat = sb("cnat", [P, 2, 2, P])
        ct = sb("ct", [P, 2, PAIRS, SG])
        bbar = sb("bbar", [P, 2, PAIRS, SG])
        bwide = sb("bwide", [P, 2, PAIRS, 2, SG])
        powers = sb("powers", [P, 2, PAIRS, STEP + 1])
        small = sb("small", [P, 32, PAIRS])
        turn = sb("turn", [P, 3, PAIRS])
        smalli = sb("smalli", [P, PAIRS], I32)
        stat = sb("stat", [P, 8])
        expo = sb("expo", [P, 1])
        inj = sb("inj", [P, 2, PAIRS, STEP, SG])
        outm = sb("outm", [P, 2, PAIRS, STEP + 1, SG])
        work = sb("work", [P, 2, PAIRS, STEP + 1, SG])
        injT = sb("injT", [P, 4, 4, P])
        tapsT = sb("tapsT", [P, 2, 4, P])
        taps = sb("taps", [P, 4, 2, P])
        acc = ps("acc", [P, 4, 512])
        tr = ps("tr", [P, 4, 512])

        cb_in = sem("cb_in")
        wide0, wide_ok = sem("wide0"), sem("wide")
        ldt_in, ldt_ok = sem("ldt_in"), sem("ldt")
        ident0, ident_ok, mem_in, par_in, gm_in = (sem(n) for n in ("ident0", "ident", "mem_in", "par_in", "gm_in"))
        w_in, w_free = [sem(f"w_in{i}") for i in range(4)], sem("w_free")
        cleared, sumsq, var, rstd, memn_ok = (sem(n) for n in ("cleared", "sumsq", "var", "rstd", "memn"))
        memT_tr, memT_ok, kv_ok, kT_tr, kT_ok = (sem(n) for n in ("memT_tr", "memT", "kv", "kT_tr", "kT"))
        par_tr, ang_ok, sin_ok = (sem(n) for n in ("par_tr", "ang", "sin"))
        c_tr, inj_ok, outm_ok = (sem(n) for n in ("c_tr", "inj", "outm"))
        injT_tr, injT_ok, tap_mm, tapT_ok, tap_tr, tap_ok = (sem(n) for n in ("injT_tr", "injT", "tap_mm", "tapT", "tap_tr", "tap"))
        injT_st = [sem(f"injT_st{i}") for i in range(4)]
        chain, stored = sem("chain"), sem("stored")

        def weight_slice(n):
            w = io["w_k"] if n < KD else io["w_v"]
            return w[0].rearrange("(k p) n -> k p n", p=P)[n % KD]

        with nc.Block() as block:

            @block.sync
            def _(sp):
                sp.wait_ge(cleared, 1)
                sp.dma_start(pn[0:PAIRS, :], io["ssm_a_re"][0].rearrange("(q t) s -> q (t s)", t=2)).then_inc(par_in, 16)
                sp.dma_start(pn[32:32 + PAIRS, :], io["ssm_a_im"][0].rearrange("(q t) s -> q (t s)", t=2)).then_inc(par_in, 16)
                sp.dma_start(ldt[64:64 + PAIRS, :], io["ssm_log_dt"][0].rearrange("(q t) -> q t", t=2)).then_inc(ldt_in, 16)
                for t in range(2):
                    sp.dma_start(memx[:, t], io["mem_prompt"][0, t * P:(t + 1) * P]).then_inc(mem_in, 16)
                sp.dma_start(g_mem[:], io["g_mem"][0].rearrange("(k p) -> p k", p=P), allow_slow_non_contiguous=True).then_inc(gm_in, 16)
                for part, name in enumerate(("ssm_c_re", "ssm_c_im")):
                    c = io[name][0].rearrange("(x q t) h s -> x q h t s", x=2, t=2)
                    for x in range(2):
                        for q in range(8):
                            sp.dma_start(cnat[q * SG:(q + 1) * SG, part, x].rearrange("h (t s) -> h t s", t=2),
                                         c[x, q]).then_inc(cb_in, 16)
                for part, name in enumerate(("ssm_b_re", "ssm_b_im")):
                    sp.dma_start(braw[:, part], io[name][0].rearrange("(q t) s h -> (t s) q h", t=2)).then_inc(cb_in, 16)
                for n in range(2 * KD):
                    if n >= 4:
                        sp.wait_ge(w_free, n - 3)
                    sp.dma_start(wring[:, n % 4], weight_slice(n)).then_inc(w_in[n % 4], 16)
                for m, name in enumerate(("new_mem_k", "new_mem_v")):
                    sp.wait_ge(kv_ok, 4 * (m + 1))
                    sp.dma_start(io[name].rearrange("l b (t p) h e -> p (l b t) (h e)", p=P), kv[:, m]).then_inc(stored, 16)
                sp.dma_start(scr["v"], kv[:, 1]).then_inc(stored, 16)
                sp.wait_ge(kT_ok, KD)
                sp.dma_start(scr["kT"], kT[:]).then_inc(stored, 16)
                for n in range(PAIRS):
                    sp.wait_ge(injT_ok, n + 1)
                    sp.dma_start(scr["injT"][:, n], injT[:, n % 4]).then_inc(injT_st[n % 4], 16)
                sp.wait_ge(outm_ok, 1)
                sp.dma_start(scr["pow16"], powers[:, :, :, STEP], allow_slow_non_contiguous=True).then_inc(stored, 16)
                sp.dma_start(scr["turn"], turn[:]).then_inc(stored, 16)
                sp.dma_start(scr["outm"], outm[:]).then_inc(stored, 16)
                for b in range(4):
                    sp.wait_ge(tap_ok, b // 2 + 1)
                    sp.dma_start(scr["taps"][:, 8 * b:8 * b + 8].rearrange("h g k c -> g h (k c)"), taps[:, b]).then_inc(stored, 16)
                sp.wait_ge(stored, 11 * 16)
                for i in range(4):
                    sp.wait_ge(injT_st[i], PAIRS // 4 * 16)

            @block.gpsimd
            def _(pool):
                nc.gpsimd.memset(expo[:], -0.5)
                identity_matrix(nc, pool, ident, ident0, ident_ok)
                nc.gpsimd.memset(bwide[:], 0.0).then_inc(wide0, 1)
                for t in range(2):
                    pool.wait_ge(var, t + 1)
                    nc.gpsimd.tensor_tensor(stat[:, 4 + t:5 + t], stat[:, 2 + t:3 + t], expo[:], ALU.pow).then_inc(rstd, 1)

            @block.scalar
            def _(act):
                for t in range(2):
                    act.wait_ge(mem_in, 32)
                    nc.scalar.activation(kv[:, 0, t], memx[:, t], ACT.Square, accum_out=stat[:, t:t + 1]).then_inc(sumsq, 1)
                act.wait_ge(gm_in, 16)
                for k in range(KD):
                    act.wait_ge(memT_tr, k // 2 + 1)
                    src = tr[:, k // 2].rearrange("p (a n) -> p a n", a=2)[:, k % 2]
                    nc.scalar.activation(memT[:, k], src, ACT.Copy, scale=g_mem[:, k:k + 1]).then_inc(memT_ok, 1)
                act.wait_ge(ang_ok, 1)
                nc.scalar.activation(small[:, 12], small[:, 10], ACT.Sin).then_inc(sin_ok, 1)
                nc.scalar.activation(small[:, 13], small[:, 11], ACT.Sin).then_inc(sin_ok, 1)
                act.wait_ge(sumsq, 2)
                for m in range(2):
                    act.wait_ge(w_free, (m + 1) * KD)
                    for t in range(2):
                        for h in range(2):
                            nc.scalar.activation(kv[:, m, t, h * 512:(h + 1) * 512], acc[:, 2 * t + h], ACT.Copy).then_inc(kv_ok, 1)
                for k in range(KD):
                    act.wait_ge(kT_tr, k // 2 + 1)
                    src = acc[:, k // 2].rearrange("p (a n) -> p a n", a=2)[:, k % 2]
                    nc.scalar.activation(kT[:, k], src, ACT.Copy).then_inc(kT_ok, 1)
                for n in range(PAIRS):
                    act.wait_ge(injT_tr, n + 1)
                    if n >= 4:
                        act.wait_ge(injT_st[n % 4], 16 * (n // 4))
                    nc.scalar.activation(injT[:, n % 4], tr[:, n % 4].rearrange("p (a n) -> p a n", a=4), ACT.Copy).then_inc(injT_ok, 1)
                for half in range(2):
                    act.wait_ge(tap_mm, half + 1)
                    nc.scalar.activation(tapsT[:, half].rearrange("p b n -> p (b n)"), acc[:, half], ACT.Copy).then_inc(tapT_ok, 1)
                for x in range(2):
                    act.wait_ge(tap_tr, x + 1)
                    nc.scalar.activation(taps[:, 2 * x:2 * x + 2].rearrange("p b k n -> p (b k n)"), tr[:, x], ACT.Copy).then_inc(tap_ok, 1)

            @block.vector
            def _(dve):
                links = [0]

                def then(*instructions):
                    for ins in instructions:
                        ins.then_inc(chain, 1)
                    links[0] += len(instructions)
                    dve.wait_ge(chain, links[0])

                tt, ts, stt = nc.vector.tensor_tensor, nc.vector.tensor_scalar, nc.vector.scalar_tensor_tensor
                nc.vector.memset(pn[:], 0.0).then_inc(cleared, 1)
                dve.wait_ge(ldt_in, 16)
                dve.wait_ge(cleared, 1)
                for t in range(2):
                    ins = nc.vector.tensor_copy(pn[64:64 + PAIRS, t * SS:(t + 1) * SS],
                                                ldt[64:64 + PAIRS, t:t + 1].to_broadcast([PAIRS, SS]))
                ins.then_inc(ldt_ok, 1)
                dve.wait_ge(par_tr, 1)
                then(nc.vector.tensor_copy(pt[:], acc[:, 3, 0:P]))
                a_re, a_im, log_dt = pt[:, 0:PAIRS], pt[:, 32:32 + PAIRS], pt[:, 64:64 + PAIRS]
                S = lambda n: small[:, n]

                def exp_parts(x):
                    then(ts(S(0), x, 88.0, -87.0, ALU.min, ALU.max))
                    then(ts(S(1), S(0), 1.0 / math.log(2.0), MAGIC, ALU.mult, ALU.add))
                    then(ts(S(1), S(1), -MAGIC, None, ALU.add))
                    then(stt(S(0), S(1), -LN2_HI, S(0), ALU.mult, ALU.add))
                    then(stt(S(0), S(1), -LN2_LO, S(0), ALU.mult, ALU.add))
                    then(ts(smalli[:], S(1), 127.0, None, ALU.add))
                    then(ts(small[:, 2].bitcast(I32), smalli[:], 23, None, ALU.logical_shift_left))
                    then(ts(S(3), S(0), 1.0 / math.factorial(8), None, ALU.mult))
                    for n in range(7, 0, -1):
                        then(stt(S(3), S(3), 1.0 / math.factorial(n), S(0), ALU.add, ALU.mult))

                exp_parts(log_dt)
                for t in range(2):
                    dve.wait_ge(sumsq, t + 1)
                    ts(stat[:, 2 + t:3 + t], stat[:, t:t + 1], 1.0 / D, EPS, ALU.mult, ALU.add).then_inc(var, 1)
                for t in range(2):
                    dve.wait_ge(rstd, t + 1)
                    ts(memx[:, t], memx[:, t], stat[:, 4 + t:5 + t], None, ALU.mult).then_inc(memn_ok, 1)
                then(stt(S(4), S(3), 1.0, S(2), ALU.add, ALU.mult))
                then(tt(S(5), a_re, S(4), ALU.mult), tt(S(6), a_im, S(4), ALU.mult))
                then(ts(S(7), S(6), 1.0 / (2 * math.pi), MAGIC, ALU.mult, ALU.add))
                then(ts(S(7), S(7), -MAGIC, None, ALU.add))
                then(stt(S(8), S(7), -TWO_PI_A, S(6), ALU.mult, ALU.add))
                then(stt(S(8), S(7), -TWO_PI_B, S(8), ALU.mult, ALU.add))
                then(stt(S(8), S(7), -TWO_PI_C, S(8), ALU.mult, ALU.add))
                then(ts(S(10), S(8), 0.5, math.pi / 2, ALU.mult, ALU.min))
                then(ts(S(10), S(10), -math.pi / 2, None, ALU.max))
                then(stt(S(9), S(10), -1.0, S(10), ALU.mult, ALU.max))
                then(ts(S(11), S(9), -1.0, math.pi / 2, ALU.mult, ALU.add))
                dve.sem_inc(ang_ok, 1)
                exp_parts(S(5))
                then(tt(S(15), S(2), S(3), ALU.mult), ts(S(16), S(2), -1.0, None, ALU.add))
                then(tt(S(15), S(15), S(16), ALU.add))
                dve.wait_ge(sin_ok, 2)
                then(stt(S(17), S(12), -2.0, S(12), ALU.mult, ALU.mult), stt(S(18), S(12), 2.0, S(13), ALU.mult, ALU.mult))
                then(ts(S(19), S(17), 1.0, None, ALU.add), ts(S(20), S(15), 1.0, None, ALU.add))
                then(tt(S(21), S(15), S(19), ALU.mult), tt(S(22), S(20), S(18), ALU.mult))
                then(tt(S(21), S(21), S(17), ALU.add))
                pw = lambda part, k: powers[:, part, :, k]
                then(nc.vector.memset(pw(0, 0), 1.0), nc.vector.memset(pw(1, 0), 0.0),
                     ts(pw(0, 1), S(21), 1.0, None, ALU.add), ts(pw(1, 1), S(22), 1.0, None, ALU.mult))
                size, cosine, sine = (turn[:, i] for i in range(3))
                then(tt(size, S(20), S(20), ALU.mult), ts(cosine, S(19), 1.0, None, ALU.mult), ts(sine, S(18), 1.0, None, ALU.mult))
                for n in range(4):
                    then(tt(S(23), cosine, cosine, ALU.mult), tt(S(24), sine, sine, ALU.mult), tt(S(25), cosine, sine, ALU.mult))
                    then(tt(cosine, S(23), S(24), ALU.subtract), ts(sine, S(25), 2.0, None, ALU.mult))
                    then(tt(S(23), cosine, cosine, ALU.mult), tt(S(24), sine, sine, ALU.mult))
                    then(tt(S(23), S(23), S(24), ALU.add))
                    then(ts(S(23), S(23), -0.5, 1.5, ALU.mult, ALU.add))
                    then(tt(cosine, cosine, S(23), ALU.mult), tt(sine, sine, S(23), ALU.mult))
                    if n:
                        then(tt(size, size, size, ALU.mult))
                then(tt(S(23), a_re, a_re, ALU.mult), tt(S(24), a_im, a_im, ALU.mult))
                then(tt(S(23), S(23), S(24), ALU.add))
                then(nc.vector.reciprocal(S(23), S(23)))
                then(tt(S(24), S(21), a_re, ALU.mult), tt(S(25), S(22), a_im, ALU.mult),
                     tt(S(26), S(22), a_re, ALU.mult), tt(S(27), S(21), a_im, ALU.mult))
                then(tt(S(24), S(24), S(25), ALU.add), tt(S(26), S(26), S(27), ALU.subtract))
                then(tt(S(28), S(24), S(23), ALU.mult), tt(S(29), S(26), S(23), ALU.mult))

                def times(out, x, y, flip=1.0):
                    shape = x[0].shape
                    size = 1
                    for s in shape[1:]:
                        size *= s

                    def like(flat):
                        if len(shape) == 2:
                            return flat
                        if len(shape) == 3:
                            return flat.rearrange("p (a b) -> p a b", a=shape[1])
                        return flat.rearrange("p (a b c) -> p a b c", a=shape[1], b=shape[2])
                    scratch = work[:].rearrange("p r a b c -> p (r a b c)")
                    t0, t1 = like(scratch[:, 0:size]), like(scratch[:, size:2 * size])
                    then(tt(t0, x[0], y[0], ALU.mult), tt(t1, x[1], y[1], ALU.mult))
                    then(tt(out[0], t0, t1, ALU.subtract))
                    then(tt(t0, x[0], y[1], ALU.mult), tt(t1, x[1], y[0], ALU.mult))
                    if flip == 1.0:
                        then(tt(out[1], t0, t1, ALU.add))
                    else:
                        flat = lambda v: v.rearrange("p a b c -> p (a b c)") if len(shape) == 4 else v
                        then(stt(flat(out[1]), flat(t0), -1.0, flat(t1), ALU.mult, ALU.subtract))

                k = 1
                while k < STEP:
                    y = [powers[:, part, :, k:k + 1].to_broadcast([P, PAIRS, k]) for part in range(2)]
                    times([powers[:, part, :, k + 1:2 * k + 1] for part in range(2)],
                          [powers[:, part, :, 1:k + 1] for part in range(2)], y)
                    k *= 2
                dve.wait_ge(cb_in, 34 * 16)
                f = [S(28 + part).unsqueeze(2).to_broadcast([P, PAIRS, SG]) for part in range(2)]
                times([bbar[:, part] for part in range(2)], [braw[:, part] for part in range(2)], f)
                dve.wait_ge(wide0, 1)
                for part in range(2):
                    for t in range(2):
                        rows = slice(t * SS, (t + 1) * SS)
                        nc.vector.tensor_copy(bwide[rows, part, :, t], bbar[rows, part]).then_inc(wide_ok, 1)
                dve.wait_ge(c_tr, 1)
                then(*(nc.vector.tensor_copy(ct[:, part, 8 * x:8 * x + 8], tr[:, 2 * part + x, 0:P].rearrange("p (q h) -> p q h", h=SG))
                       for part in range(2) for x in range(2)))
                bb = [bbar[:, part].unsqueeze(2).to_broadcast([P, PAIRS, STEP, SG]) for part in range(2)]
                pr = [bass.AP(tensor=powers, offset=part * PAIRS * (STEP + 1) + STEP - 1,
                              ap=[[2 * PAIRS * (STEP + 1), P], [STEP + 1, PAIRS], [-1, STEP], [0, SG]]) for part in range(2)]
                times([inj[:, part] for part in range(2)], pr, bb)
                dve.sem_inc(inj_ok, 1)
                cc = [ct[:, part].unsqueeze(2).to_broadcast([P, PAIRS, STEP + 1, SG]) for part in range(2)]
                pf = [powers[:, part].unsqueeze(3).to_broadcast([P, PAIRS, STEP + 1, SG]) for part in range(2)]
                times([outm[:, part] for part in range(2)], pf, cc, flip=-1.0)
                dve.sem_inc(outm_ok, 1)
                cosine, sine = phase[:, 0], phase[:, 1]
                then(nc.vector.memset(cosine[:, :, 0:1], 1.0), nc.vector.memset(sine[:, :, 0:1], 0.0),
                     nc.vector.tensor_copy(cosine[:, :, 1], turn[:, 1]), nc.vector.tensor_copy(sine[:, :, 1], turn[:, 2]))
                scratch = work[:].rearrange("p r a b c -> p (r a b c)")
                k = 1
                while k < CH - 1:
                    n = min(k, CH - 1 - k)
                    t0, t1 = (scratch[:, i * PAIRS * n:(i + 1) * PAIRS * n].rearrange("p (q c) -> p q c", q=PAIRS) for i in range(2))
                    c0, s0 = cosine[:, :, 1:1 + n], sine[:, :, 1:1 + n]
                    ck, sk = (x[:, :, k:k + 1].to_broadcast([P, PAIRS, n]) for x in (cosine, sine))
                    then(tt(t0, c0, ck, ALU.mult), tt(t1, s0, sk, ALU.mult))
                    then(tt(cosine[:, :, k + 1:k + 1 + n], t0, t1, ALU.subtract))
                    then(tt(t0, c0, sk, ALU.mult), tt(t1, s0, ck, ALU.mult))
                    then(tt(sine[:, :, k + 1:k + 1 + n], t0, t1, ALU.add))
                    k += n
                t0, t1 = scratch[:, 0:PAIRS * CH], scratch[:, PAIRS * CH:2 * PAIRS * CH]
                c, s = (x.rearrange("p q c -> p (q c)") for x in (cosine, sine))
                then(tt(t0, c, c, ALU.mult), tt(t1, s, s, ALU.mult))
                then(tt(t0, t0, t1, ALU.add))
                then(ts(t0, t0, -0.5, 1.5, ALU.mult, ALU.add))
                then(tt(c, c, t0, ALU.mult), tt(s, s, t0, ALU.mult))

            @block.tensor
            def _(pe):
                pe.wait_ge(ident_ok, 1)
                pe.wait_ge(par_in, 32)
                pe.wait_ge(ldt_ok, 1)
                nc.tensor.transpose(acc[:, 3, 0:P], pn[:], ident[:]).then_inc(par_tr, 1)
                for k in range(KD):
                    for t in range(2):
                        pe.wait_ge(memn_ok, t + 1)
                        ins = nc.tensor.transpose(tr[:, k // 2, (k % 2) * MEM + t * P:(k % 2) * MEM + (t + 1) * P],
                                                  memx[:, t, k * P:(k + 1) * P], ident[:])
                    if k % 2:
                        ins.then_inc(memT_tr, 1)
                pe.wait_ge(memT_ok, KD)
                pe.wait_ge(cb_in, 34 * 16)
                for part in range(2):
                    for x in range(2):
                        ins = nc.tensor.transpose(tr[:, 2 * part + x, 0:P], cnat[:, part, x], ident[:])
                ins.then_inc(c_tr, 1)
                pe.wait_ge(ang_ok, 1)
                for m in range(2):
                    if m:
                        pe.wait_ge(kv_ok, 4)
                    for k in range(KD):
                        n = m * KD + k
                        pe.wait_ge(w_in[n % 4], 16 * (n // 4 + 1))
                        for t in range(2):
                            for h in range(2):
                                ins = nc.tensor.matmul(acc[:, 2 * t + h], memT[:, k, t * P:(t + 1) * P],
                                                       wring[:, n % 4, h * 512:(h + 1) * 512], start=k == 0, stop=k == KD - 1)
                        ins.then_inc(w_free, 1)
                pe.wait_ge(kv_ok, 8)
                for k in range(KD):
                    for t in range(2):
                        ins = nc.tensor.transpose(acc[:, k // 2, (k % 2) * MEM + t * P:(k % 2) * MEM + (t + 1) * P],
                                                  kv[:, 0, t, k * P:(k + 1) * P], ident[:])
                    if k % 2:
                        ins.then_inc(kT_tr, 1)
                pe.wait_ge(inj_ok, 1)
                for n in range(PAIRS):
                    if n >= 4:
                        pe.wait_ge(injT_ok, n - 3)
                    for part in range(2):
                        for jh in range(2):
                            ins = nc.tensor.transpose(tr[:, n % 4, (2 * part + jh) * P:(2 * part + jh + 1) * P],
                                                      inj[:, part, n, 8 * jh:8 * jh + 8].rearrange("p j h -> p (j h)"), ident[:])
                    ins.then_inc(injT_tr, 1)
                pe.wait_ge(outm_ok, 1)
                pe.wait_ge(wide_ok, 4)
                pe.wait_ge(kT_ok, KD)
                for half in range(2):
                    for q in range(PAIRS):
                        for part in range(2):
                            ins = nc.tensor.matmul(acc[:, half, q * 2 * SG:(q + 1) * 2 * SG],
                                                   outm[:, part, q, 8 * half:8 * half + 8].rearrange("p k h -> p (k h)"),
                                                   bwide[:, part, q].rearrange("p t h -> p (t h)"), start=part == 0, stop=part == 1)
                    ins.then_inc(tap_mm, 1)
                pe.wait_ge(tapT_ok, 2)
                pe.wait_ge(injT_ok, PAIRS)
                for x in range(2):
                    for b in (2 * x, 2 * x + 1):
                        for half in range(2):
                            ins = nc.tensor.transpose(tr[:, x, ((b % 2) * 2 + half) * P:((b % 2) * 2 + half + 1) * P], tapsT[:, half, b], ident[:])
                    ins.then_inc(tap_tr, 1)


def first_input_projection(nc, outer, io, scr):
    sem = lambda n: outer.new("s2_" + n)
    with ExitStack() as ctx:
        room = Room(nc, ctx, "s2")
        sb, ps = room.sb, room.ps
        ident = sb("ident", [P, P])
        expo = sb("expo", [P, 1])
        g = sb("g", [P, KD])
        raw = sb("raw", [P, 2, D])
        w_hi, w_lo = sb("w_hi", [P, KD, D], F32R), sb("w_lo", [P, KD, D], F32R)
        x = sb("x", [P, 3, D])
        junk = sb("junk", [P, D])
        stat = sb("stat", [P, 3, TILES])
        h = sb("h", [P, 2, 2, BT, KD, P], F32R)
        zst = sb("zst", [P, 2, BT * P])
        acc = ps("acc", [P, 4, 512])
        tr = ps("tr", [P, 2, 2, 512])

        ident0, ident_ok, g_in = sem("ident0"), sem("ident"), sem("g_in")
        raw_in, raw_used, hi_ok = [sem(f"raw_in{i}") for i in range(2)], sem("w_lo"), sem("w_hi")
        x_in = [sem(f"x_in{i}") for i in range(3)]
        sumsq, var, rstd, xn_ok = sem("sumsq"), sem("var"), sem("rstd"), sem("xn")
        tr_ok, th_ok, tl_ok = sem("tr"), sem("th"), sem("tl")
        z_mm, z_ok, z_st = sem("z_mm"), sem("z"), [sem(f"z_st{i}") for i in range(2)]

        BLOCKS = TILES // BT + 1

        def tiles_of(b):
            return range(BT * b, min(BT * b + BT, TILES))

        with nc.Block() as block:

            @block.sync
            def _(sp):
                xp = io["x_prompt"][0].rearrange("(c j) d -> j c d", j=STEP)
                xs = io["x_sample"].rearrange("b j d -> j b d")
                w = io["w_in"][0].rearrange("(k p) n -> k p n", p=P)

                def load_x(t):
                    if t >= 3:
                        sp.wait_ge(tr_ok, t - 2)
                    sp.dma_start(x[:, t % 3], xp[t] if t < STEP else xs).then_inc(x_in[t % 3], 16)

                sp.dma_start(g[:], io["g_mix"][0].rearrange("(k p) -> p k", p=P), allow_slow_non_contiguous=True).then_inc(g_in, 16)
                for t in range(3):
                    load_x(t)
                for k in range(KD):
                    if k == 2:
                        for t in range(3, 7):
                            load_x(t)
                    if k >= 2:
                        sp.wait_ge(raw_used, k - 1)
                    sp.dma_start(raw[:, k % 2], w[k]).then_inc(raw_in[k % 2], 16)
                load_x(7)
                for b in range(BLOCKS):
                    for m in range(KD):
                        n = b * KD + m
                        sp.wait_ge(z_ok, n + 1)
                        if b < BLOCKS - 1:
                            dst = scr["z"][m][:, BT * b:BT * b + BT, 0:CH]
                            src = zst[:, n % 2].rearrange("p (j c) -> p j c", j=BT)
                        else:
                            dst = scr["z"][m][:, :, CH:NC]
                            src = zst[:, n % 2, 0:P].rearrange("p (j b) -> p j b", b=STREAMS)
                        sp.dma_start(dst, src).then_inc(z_st[n % 2], 16)
                        if m % 2 and b < BLOCKS - 2 and BT * (b + 2) + m // 2 < TILES:
                            load_x(BT * (b + 2) + m // 2)
                for i in range(2):
                    sp.wait_ge(z_st[i], BLOCKS * KD // 2 * 16)

            @block.gpsimd
            def _(pool):
                nc.gpsimd.memset(expo[:], -0.5)
                identity_matrix(nc, pool, ident, ident0, ident_ok)
                for t in range(TILES):
                    pool.wait_ge(var, t + 1)
                    nc.gpsimd.tensor_tensor(stat[:, 2, t:t + 1], stat[:, 1, t:t + 1], expo[:], ALU.pow).then_inc(rstd, 1)

            @block.scalar
            def _(act):
                def square(t):
                    act.wait_ge(x_in[t % 3], 16 * (t // 3 + 1))
                    if t:
                        act.wait_ge(sumsq, t)
                    nc.scalar.activation(junk[:], x[:, t % 3], ACT.Square, accum_out=stat[:, 0, t:t + 1]).then_inc(sumsq, 1)

                def upper_half(t):
                    b, j = divmod(t, BT)
                    act.wait_ge(tr_ok, t + 1)
                    if b >= 2:
                        act.wait_ge(z_mm, (b - 1) * KD)
                    for a in range(2):
                        nc.scalar.activation(h[:, b % 2, 0, j, 4 * a:4 * a + 4].rearrange("p k n -> p (k n)"), tr[:, t % 2, a],
                                             ACT.Copy).then_inc(th_ok, 1)

                square(0)
                square(1)
                for t in range(BT):
                    upper_half(t)
                    square(t + 2)
                act.wait_ge(g_in, 16)
                for k in range(KD):
                    act.wait_ge(raw_in[k % 2], 16 * (k // 2 + 1))
                    nc.scalar.activation(w_hi[:, k], raw[:, k % 2], ACT.Copy, scale=g[:, k:k + 1]).then_inc(hi_ok, 1)
                for b in range(BLOCKS):
                    for m in range(KD):
                        n = b * KD + m
                        act.wait_ge(z_mm, n + 1)
                        if n >= 2:
                            act.wait_ge(z_st[n % 2], 16 * (n // 2))
                        wide = P * len(tiles_of(b))
                        nc.scalar.activation(zst[:, n % 2, 0:wide], acc[:, n % 4, 0:wide], ACT.Copy).then_inc(z_ok, 1)
                        t = BT * (b + 1) + m // 2
                        if m % 2 == 0 and t < TILES:
                            upper_half(t)
                            if t + 2 < TILES:
                                square(t + 2)

            @block.vector
            def _(dve):
                def norm(t):
                    dve.wait_ge(sumsq, t + 1)
                    nc.vector.tensor_scalar(stat[:, 1, t:t + 1], stat[:, 0, t:t + 1], 1.0 / D, EPS, ALU.mult, ALU.add).then_inc(var, 1)
                    dve.wait_ge(rstd, t + 1)
                    nc.vector.tensor_scalar(x[:, t % 3], x[:, t % 3], stat[:, 2, t:t + 1], None, ALU.mult).then_inc(xn_ok, 1)

                def lower_half(t):
                    b, j = divmod(t, BT)
                    for a in range(2):
                        dve.wait_ge(th_ok, 2 * t + a + 1)
                        up = h[:, b % 2, 0, j, 4 * a:4 * a + 4].rearrange("p k n -> p (k n)").bitcast(F32)
                        nc.vector.tensor_tensor(h[:, b % 2, 1, j, 4 * a:4 * a + 4].rearrange("p k n -> p (k n)"), tr[:, t % 2, a], up,
                                                ALU.subtract).then_inc(tl_ok, 1)

                norm(0)
                norm(1)
                for t in range(BT):
                    lower_half(t)
                    norm(t + 2)
                for k in range(KD):
                    dve.wait_ge(hi_ok, k + 1)
                    nc.vector.scalar_tensor_tensor(w_lo[:, k], raw[:, k % 2], g[:, k:k + 1], w_hi[:, k].bitcast(F32),
                                                   ALU.mult, ALU.subtract).then_inc(raw_used, 1)
                for t in range(BT, TILES):
                    lower_half(t)
                    if t + 2 < TILES:
                        norm(t + 2)

            @block.tensor
            def _(pe):
                def turn(t):
                    pe.wait_ge(xn_ok, t + 1)
                    if t >= 2:
                        pe.wait_ge(tl_ok, 2 * (t - 1))
                    for k in range(KD):
                        ins = nc.tensor.transpose(tr[:, t % 2, k // 4, (k % 4) * P:(k % 4 + 1) * P],
                                                  x[:, t % 3, k * P:(k + 1) * P], ident[:])
                    ins.then_inc(tr_ok, 1)

                pe.wait_ge(ident_ok, 1)
                for t in range(BT):
                    turn(t)
                for b in range(BLOCKS):
                    nt = len(tiles_of(b))
                    pe.wait_ge(tl_ok, 2 * (tiles_of(b)[-1] + 1))
                    for ms in [range(0, 4)] * (b == 0) + [(m,) for m in range(4 if b == 0 else 0, KD)]:
                        for k in range(KD):
                            for m in ms:
                                n = b * KD + m
                                if k == 0 and n >= 4:
                                    pe.wait_ge(z_ok, n - 3)
                                if n == 0:
                                    pe.wait_ge(raw_used, k + 1)
                                cols = slice(m * P, (m + 1) * P)
                                ins = product3(nc, acc[:, n % 4, 0:nt * P], w_hi[:, k, cols], w_lo[:, k, cols],
                                               h[:, b % 2, 0, 0:nt, k], h[:, b % 2, 1, 0:nt, k], k == 0, k == KD - 1)
                                if k == KD - 1:
                                    ins.then_inc(z_mm, 1)
                        for m in ms:
                            if m % 2 == 0 and BT * (b + 1) + m // 2 < TILES:
                                turn(BT * (b + 1) + m // 2)


def mixers(nc, outer, io, scr, phase):
    sem = lambda n: outer.new("s3_" + n)
    with ExitStack() as ctx:
        room = Room(nc, ctx, "s3")
        sb, ps = room.sb, room.ps
        ident = sb("ident", [P, P])
        u = sb("u", [P, 2, GROUPS, NC])
        injT = sb("injT", [P, PAIRS, 4, P])
        outm = sb("outm", [P, 2, PAIRS, STEP + 1, SG])
        toep = sb("toep", [P, GROUPS, 2 * P])
        ha = sb("ha", [P, 2, PAIRS, NC])
        hb = sb("hb", [P, 2, PAIRS, NC])
        QP = PAIRS // 4
        a16 = sb("a16", [P, 3, PAIRS])
        turn = sb("turn", [P, 3, PAIRS])
        parts = sb("parts", [P, 4, QP * CH])
        h0n = sb("h0n", [P, 2, P])
        h0 = sb("h0", [P, 2, STREAMS, PAIRS])
        ends = sb("ends", [P, 2, STREAMS, PAIRS])
        last = sb("last", [P, 2, P])
        lastp = sb("lastp", [PAIRS, 2, P])
        inj_ps = ps("inj", [P, 2, 512])
        out_ps = ps("out", [P, 3, 512])
        misc = ps("misc", [P, 512])

        ident0, ident_ok, zero_ok = sem("ident0"), sem("ident"), sem("zero")
        inj_in, u_in, outm_in, a16_in, h0_in, toep_in = ([sem(f"{n}{i}") for i in range(4)] if n in ("inj_in", "u_in", "outm_in", "toep_in") else sem(n) for n in ("inj_in", "u_in", "outm_in", "a16_in", "h0_in", "toep_in"))
        inj_mm, inj_ok, h0_tr, h0_ok = sem("inj_mm"), sem("inj_ok"), sem("h0_tr"), sem("h0_ok")
        chain, start_ok, last_tr, last_ok = sem("chain"), sem("start"), sem("last_tr"), sem("last")
        out_mm, out_ok, stored = sem("out_mm"), sem("out_ok"), sem("stored")

        def in_turn(injections, outputs):
            injections(0)
            injections(1)
            outputs(0)
            injections(2)
            injections(3)
            for Q in (1, 2, 3):
                outputs(Q)

        with nc.Block() as block:

            @block.sync
            def _(sp):
                sp.dma_start(a16[:, 0:2], scr["pow16"]).then_inc(a16_in, 16)
                sp.dma_start(turn[:], scr["turn"]).then_inc(a16_in, 16)
                for part, name in enumerate(("state_ssm_re", "state_ssm_im")):
                    sp.dma_start(h0n[:, part], io[name][0].rearrange("b (q t) s -> (b q) (t s)", t=2)).then_inc(h0_in, 16)
                zs = scr["z"].rearrange("m (g h) j c -> m h g j c", h=SG)
                def load_quarter(m):
                    sp.dma_start(injT[:, QP * m:QP * m + QP], scr["injT"][:, QP * m:QP * m + QP]).then_inc(inj_in[m], 16)
                    for j in range(STEP):
                        sp.dma_start(u[SG * (j % 8):SG * (j % 8) + SG, j // 8, 8 * m:8 * m + 8], zs[4 + m][:, :, j]).then_inc(u_in[m], 16)

                def load_outputs(half):
                    pairs, gs = slice(half * 8, half * 8 + 8), slice(half * 16, half * 16 + 16)
                    sp.dma_start(outm[:, :, pairs].rearrange("p r q k h -> p r (q k h)"),
                                 scr["outm"][:, :, pairs].rearrange("p r q k h -> p r (q k h)")).then_inc(outm_in[half], 16)
                    for i in range(8):
                        sp.dma_start(toep[SG * i:SG * i + SG, gs, SG * i:2 * P],
                                     scr["taps"][:, gs, 0:STEP - i].rearrange("h g k c -> h g (k c)")).then_inc(toep_in[half], 16)

                load_quarter(0)
                load_quarter(1)
                sp.wait_ge(zero_ok, 1)
                load_outputs(0)
                load_quarter(2)
                load_quarter(3)
                load_outputs(1)
                for m in range(4):
                    sp.wait_ge(out_ok, 8 * (m + 1))
                    ys = scr["y"].rearrange("m (g h) j c -> m h g j c", h=SG)
                    for j in range(STEP):
                        sp.dma_start(ys[m][:, :, j], u[SG * (j % 8):SG * (j % 8) + SG, j // 8, 8 * m:8 * m + 8]).then_inc(stored, 16)
                sp.wait_ge(last_ok, 4)
                for part, name in enumerate(("new_ssm_re", "new_ssm_im")):
                    sp.dma_start(io[name + "_s"][0].rearrange("b (q t) s -> (b q) (t s)", t=2), last[:, part]).then_inc(stored, 16)
                    sp.dma_start(io[name + "_p"][0, 0].rearrange("(q t) s -> q (t s)", t=2), lastp[:, part]).then_inc(stored, 16)
                sp.wait_ge(stored, (4 + 4 * STEP) * 16)

            @block.gpsimd
            def _(pool):
                identity_matrix(nc, pool, ident, ident0, ident_ok)
                nc.gpsimd.memset(toep[:, :, 0:P], 0.0).then_inc(zero_ok, 1)

            @block.scalar
            def _(act):
                def injections(Q):
                    for q in range(QP * Q, QP * Q + QP):
                        act.wait_ge(inj_mm, q + 1)
                        nc.scalar.activation(ha[:, :, q], inj_ps[:, q % 2, 0:2 * NC].rearrange("p (r c) -> p r c", r=2),
                                             ACT.Copy).then_inc(inj_ok, 1)

                def outputs(Q):
                    for g in range(8 * Q, 8 * Q + 8):
                        act.wait_ge(out_mm, g + 1)
                        nc.scalar.activation(u[:, :, g], out_ps[:, g % 3, 0:2 * NC].rearrange("p (a c) -> p a c", a=2),
                                             ACT.Copy).then_inc(out_ok, 1)

                in_turn(injections, outputs)
                for part in range(2):
                    act.wait_ge(last_tr, 1)
                    nc.scalar.activation(last[:, part], misc[:, part * P:(part + 1) * P], ACT.Copy).then_inc(last_ok, 1)
                    nc.scalar.activation(lastp[:, part], misc[0:PAIRS, (2 + part) * P:(3 + part) * P], ACT.Copy).then_inc(last_ok, 1)

            @block.vector
            def _(dve):
                links = [0]

                def then(*instructions):
                    for ins in instructions:
                        ins.then_inc(chain, 1)
                    links[0] += len(instructions)
                    dve.wait_ge(chain, links[0])

                tt, ts = nc.vector.tensor_tensor, nc.vector.tensor_scalar
                dve.wait_ge(a16_in, 32)
                ts(a16[:, 2], a16[:, 1], -1.0, None, ALU.mult).then_inc(h0_ok, 1)
                cosine, sine = phase[:, 0], phase[:, 1]
                dve.wait_ge(h0_tr, 1)
                nc.vector.tensor_copy(h0[:].rearrange("p r b q -> p (r b q)"), misc[:, 0:2 * P]).then_inc(h0_ok, 1)
                dve.wait_ge(h0_ok, 2)
                for Q in range(4):
                    pairs = slice(Q * QP, Q * QP + QP)
                    dve.wait_ge(inj_ok, QP * (Q + 1))
                    part = [parts[:, i].rearrange("p (q c) -> p q c", q=QP) for i in range(4)]
                    c, s = cosine[:, pairs], sine[:, pairs]
                    x, y = ha[:, 0, pairs, 0:CH], ha[:, 1, pairs, 0:CH]
                    then(tt(part[0], x, c, ALU.mult), tt(part[1], y, s, ALU.mult), tt(part[2], y, c, ALU.mult), tt(part[3], x, s, ALU.mult))
                    then(tt(hb[:, 0, pairs, 0:CH], part[0], part[1], ALU.add), tt(hb[:, 1, pairs, 0:CH], part[2], part[3], ALU.subtract))
                    then(*(nc.vector.tensor_tensor_scan(ha[:, i, q, 0:CH], turn[:, 0, q:q + 1].to_broadcast([P, CH]), hb[:, i, q, 0:CH],
                                                        0.0, ALU.mult, ALU.add) for i in range(2) for q in range(Q * QP, Q * QP + QP)))
                    then(tt(part[0], x, c, ALU.mult), tt(part[1], y, s, ALU.mult), tt(part[2], x, s, ALU.mult), tt(part[3], y, c, ALU.mult))
                    early, final = slice(0, CH - 1), slice(CH - 1, CH)
                    wide = lambda i: a16[:, i, pairs].unsqueeze(2).to_broadcast([P, QP, STREAMS])
                    st = lambda i: h0[:, i].rearrange("p b q -> p q b")[:, pairs]
                    end = lambda i: hb[:, i, pairs, CH:NC]
                    own = lambda i: ha[:, i, pairs, CH:NC]
                    then(tt(ha[:, 0, pairs, 1:CH], part[0][:, :, early], part[1][:, :, early], ALU.subtract),
                         tt(ha[:, 1, pairs, 1:CH], part[2][:, :, early], part[3][:, :, early], ALU.add),
                         tt(hb[:, 0, pairs, final], part[0][:, :, final], part[1][:, :, final], ALU.subtract),
                         tt(hb[:, 1, pairs, final], part[2][:, :, final], part[3][:, :, final], ALU.add),
                         nc.vector.memset(ha[:, 0, pairs, 0:1], 0.0), nc.vector.memset(ha[:, 1, pairs, 0:1], 0.0),
                         tt(end(0), st(0), wide(0), ALU.mult), tt(end(1), st(1), wide(0), ALU.mult))
                    then(tt(own(0), own(0), end(0), ALU.add), tt(own(1), own(1), end(1), ALU.add))
                    then(tt(end(0), st(1), wide(2), ALU.mult), tt(end(1), st(0), wide(1), ALU.mult))
                    then(tt(end(0), own(0), end(0), ALU.add), tt(end(1), own(1), end(1), ALU.add))
                    then(*(nc.vector.tensor_copy(ends[:, i].rearrange("p b q -> p q b")[:, pairs], end(i)) for i in range(2)),
                         *(nc.vector.tensor_copy(own(i), st(i)) for i in range(2)))
                    dve.sem_inc(start_ok, 1)

            @block.tensor
            def _(pe):
                pe.wait_ge(ident_ok, 1)
                pe.wait_ge(h0_in, 32)
                for part in range(2):
                    ins = nc.tensor.transpose(misc[:, part * P:(part + 1) * P], h0n[:, part], ident[:])
                ins.then_inc(h0_tr, 1)

                def injections(Q):
                    pe.wait_ge(inj_in[Q], 16)
                    pe.wait_ge(u_in[Q], STEP * 16)
                    for q in range(QP * Q, QP * Q + QP):
                        if q >= 2:
                            pe.wait_ge(inj_ok, q - 1)
                        for part in range(2):
                            for t in range(2):
                                for jh in range(2):
                                    ins = nc.tensor.matmul(inj_ps[t * SS:(t + 1) * SS, q % 2, part * NC:(part + 1) * NC],
                                                           injT[:, q, 2 * part + jh, t * SS:(t + 1) * SS], u[:, jh, 2 * q + t],
                                                           start=jh == 0, stop=jh == 1)
                        ins.then_inc(inj_mm, 1)

                def outputs(Q):
                    pe.wait_ge(outm_in[Q // 2], 16)
                    pe.wait_ge(toep_in[Q // 2], 8 * 16)
                    pe.wait_ge(start_ok, Q + 1)
                    for g in range(8 * Q, 8 * Q + 8):
                        q, t = divmod(g, 2)
                        rows = slice(t * SS, (t + 1) * SS)
                        if g >= 3:
                            pe.wait_ge(out_ok, g - 2)
                        for jh in range(2):
                            to = out_ps[:, g % 3, jh * NC:(jh + 1) * NC]
                            nc.tensor.matmul(to, toep[:, g, 0:P], u[:, jh, g], start=True, stop=False)
                            if jh:
                                nc.tensor.matmul(to, toep[:, g, P:2 * P], u[:, 0, g], start=False, stop=False)
                            for part in range(2):
                                ins = nc.tensor.matmul(to, outm[rows, part, q, 1 + 8 * jh:9 + 8 * jh].rearrange("p k h -> p (k h)"),
                                                       ha[rows, part, q], start=False, stop=part == 1)
                        ins.then_inc(out_mm, 1)

                in_turn(injections, outputs)
                pe.wait_ge(h0_ok, 2)
                for part in range(2):
                    nc.tensor.transpose(misc[:, part * P:(part + 1) * P], ends[:, part].rearrange("p b q -> p (b q)"), ident[:])
                    ins = nc.tensor.transpose(misc[0:PAIRS, (2 + part) * P:(3 + part) * P], hb[:, part, :, CH - 1], ident[:])
                ins.then_inc(last_tr, 1)


def mixer_outputs(nc, outer, io, scr):
    sem = lambda n: outer.new("s4_" + n)
    with ExitStack() as ctx:
        room = Room(nc, ctx, "s4")
        sb, ps = room.sb, room.ps
        EX = HIST + STEP
        NB, WB = STEP // 2, 2 * NC
        ident = sb("ident", [P, P])
        ext = sb("ext", [P, 2, EX, NC])
        sums = sb("sums", [P, 2, EX, NC])
        pooled = sb("pooled", [P, STEP, NC])
        ost = sb("ost", [P, 2, STEP, NC])
        count = sb("count", [P, 4, STEP])
        wp = sb("wp", [P, 4, P])
        scale = sb("scale", [P, 4])
        hist = sb("hist", [STREAMS * HIST, DP])
        tail = sb("tail", [P, 4, HIST, STREAMS])
        tail1 = sb("tail1", [P, 4, HIST])
        tails = sb("tails", [STREAMS * HIST, DP])
        tailp = sb("tailp", [HIST, DP])
        w_hi, w_lo = sb("w_hi", [P, 4, DP], F32R), sb("w_lo", [P, 4, DP], F32R)
        skip, bias = sb("skip", [P, 4]), sb("bias", [P, 4])
        y = sb("y", [P, 2, 4, WB])
        z = sb("z", [P, 2, 4, WB])
        v = sb("v", [P, NB, 4, WB])
        g_hi, g_lo = sb("g_hi", [P, 2, 4, WB], F32R), sb("g_lo", [P, 2, 4, WB], F32R)
        gate = sb("gate", [P, 2, 4, WB])
        out = sb("out", [P, 2, 4, WB])
        raw = out[:].rearrange("p a m n -> p (a m n)")[:, 0:4 * DP].rearrange("p (k n) -> p k n", k=4)
        outs = sb("outs", [P, 4, STEP, STREAMS])
        hist_ps = ps("hist", [P, 512])
        pool_ps = ps("pool", [P, 3, 512])
        acc = ps("acc", [P, 4, 512])

        ident0, ident_ok, wp_in, hist_in, tail_in, scale_in = (sem(n) for n in ("ident0", "ident", "wp_in", "hist_in", "tail_in", "scale_in"))
        ext_in = [sem(f"ext_in{i}") for i in range(2)]
        hist_tr, tail_tr, tail_ok, cnt_ok = (sem(n) for n in ("hist_tr", "tail_tr", "tail", "cnt"))
        chain, past_ok, pooled_ok, pool_mm, pool_ok = sem("chain"), sem("past"), sem("pooled"), sem("pool_mm"), sem("pool_ok")
        pool_st = [sem(f"pool_st{i}") for i in range(2)]
        w_in, c_in = sem("w_in"), sem("c_in")
        yz_in = [sem(f"yz_in{i}") for i in range(2)]
        whi_ok, wlo_ok = sem("whi"), sem("wlo")
        v_ok, gelu_ok, hi_ok, lo_ok, mm, gate_ok, out_ok, outs_ok = (
            sem(n) for n in ("v", "gelu", "hi", "lo", "mm", "gate", "out", "outs"))
        out_st, stored = [sem(f"out_st{i}") for i in range(2)], sem("stored")

        with nc.Block() as block:

            @block.sync
            def _(sp):
                sp.dma_start(skip[:], io["ssm_d"][0].rearrange("(m g) h -> (g h) m", m=4), allow_slow_non_contiguous=True).then_inc(c_in, 16)

                def load_block(i):
                    if i >= 2:
                        sp.wait_ge(v_ok, 4 * (i - 1))
                    sp.dma_start(y[:, i % 2].rearrange("p m (j c) -> p m j c", j=2),
                                 scr["y"][:, :, 2 * i:2 * i + 2].rearrange("m p j c -> p m j c")).then_inc(yz_in[i % 2], 16)
                    sp.dma_start(z[:, i % 2].rearrange("p m (j c) -> p m j c", j=2),
                                 scr["z"][4:8, :, 2 * i:2 * i + 2].rearrange("m p j c -> p m j c")).then_inc(yz_in[i % 2], 16)

                def load_slab(m):
                    if m >= 2:
                        sp.wait_ge(pooled_ok, m - 1)
                    sp.dma_start(ext[:, m % 2, HIST:EX], scr["z"][m]).then_inc(ext_in[m % 2], 16)
                load_block(0)
                load_block(1)
                sp.dma_start(hist[:], io["state_pool"][0].rearrange("b e c -> (b e) c")).then_inc(hist_in, 16)
                sp.dma_start(bias[:], io["b_glu"][0].rearrange("(m p) -> p m", p=P), allow_slow_non_contiguous=True).then_inc(c_in, 16)
                sp.dma_start(raw, io["w_glu"][0].rearrange("(k p) n -> p k n", p=P)).then_inc(w_in, 16)
                sp.dma_start(wp[:], io["w_pool"][0].rearrange("m c d -> c m d")).then_inc(wp_in, 16)
                sp.dma_start(scale[:], io["pool_scale"][0].rearrange("(m p) -> p m", p=P), allow_slow_non_contiguous=True).then_inc(scale_in, 16)
                for i in range(2, 4):
                    load_block(i)
                load_slab(0)
                for i in range(4, NB):
                    load_block(i)
                load_slab(1)

                def load_tail(m):
                    sp.dma_start(tail[:, m], scr["z"][m][:, 1:STEP, CH:NC]).then_inc(tail_in, 16)
                    sp.dma_start(tail1[:, m], scr["z"][m][:, 1:STEP, CH - 1], allow_slow_non_contiguous=True).then_inc(tail_in, 16)
                def store_block(i):
                    sp.wait_ge(out_ok, 4 * (i + 1))
                    for j in range(2):
                        sp.dma_start(scr["c"][2 * i + j][:, 4:8], out[:, i % 2, :, j * NC:j * NC + CH]).then_inc(out_st[i % 2], 16)

                for m in range(4):
                    if m + 2 < 4:
                        load_slab(m + 2)
                    load_tail(m)
                    store_block(2 * m)
                    sp.wait_ge(pool_ok, NB * (m + 1))
                    sp.dma_start(scr["c"][0:STEP, :, m].rearrange("j p c -> p j c"), ost[:, m % 2, :, 0:CH]).then_inc(pool_st[m % 2], 16)
                    sp.dma_start(scr["c"][STEP, :, m].rearrange("p (j b) -> p j b", b=STREAMS), ost[:, m % 2, :, CH:NC]).then_inc(pool_st[m % 2], 16)
                    store_block(2 * m + 1)
                sp.wait_ge(outs_ok, NB)
                sp.dma_start(scr["c"][STEP][:, 4:8].rearrange("p m (j b) -> p m j b", b=STREAMS), outs[:]).then_inc(stored, 16)
                sp.wait_ge(tail_ok, 2)
                sp.dma_start(io["new_pool_s"][0].rearrange("b e c -> e b c"), tails[:]).then_inc(stored, 16)
                sp.dma_start(io["new_pool_p"][0, 0], tailp[:]).then_inc(stored, 16)
                sp.wait_ge(stored, 3 * 16)
                for i in range(2):
                    sp.wait_ge(out_st[i], NB // 2 * 32)
                    sp.wait_ge(pool_st[i], 64)

            @block.gpsimd
            def _(pool):
                identity_matrix(nc, pool, ident, ident0, ident_ok)
                for m in range(4):
                    w = 2 << m
                    for j in range(STEP):
                        ins = nc.gpsimd.memset(count[:, m, j:j + 1], w / min(j + 1, w))
                ins.then_inc(cnt_ok, 1)

            @block.scalar
            def _(act):
                def past(m):
                    act.wait_ge(ext_in[m % 2], 16 * (m // 2 + 1))
                    nc.scalar.activation(ext[:, m % 2, 0:HIST, 1:CH], ext[:, m % 2, HIST + 1:EX, 0:CH - 1], ACT.Copy).then_inc(past_ok, 1)

                def upper_half(i):
                    act.wait_ge(gelu_ok, i + 1)
                    if i >= 2:
                        act.wait_ge(mm, 4 * (i - 1))
                    nc.scalar.activation(g_hi[:, i % 2], v[:, i], ACT.Copy).then_inc(hi_ok, 1)

                for i in range(NB):
                    act.wait_ge(v_ok, 4 * (i + 1))
                    flat = v[:, i].rearrange("p m n -> p (m n)")
                    nc.scalar.activation(flat, flat, ACT.Gelu_apprx_tanh).then_inc(gelu_ok, 1)
                    if i == 0:
                        act.wait_ge(w_in, 16)
                        nc.scalar.activation(w_hi[:], raw, ACT.Copy).then_inc(whi_ok, 1)
                    elif i == 3:
                        upper_half(0)
                        upper_half(1)
                        past(0)
                act.wait_ge(c_in, 32)

                def gates(i):
                    for m in range(4):
                        n = 4 * i + m
                        act.wait_ge(mm, n + 1)
                        if i >= 2:
                            act.wait_ge(out_ok, n - 7)
                        nc.scalar.activation(gate[:, i % 2, m], acc[:, m, 0:WB], ACT.Sigmoid, bias=bias[:, m:m + 1]).then_inc(gate_ok, 1)
                    if i + 2 < NB:
                        upper_half(i + 2)

                def scaled(m):
                    if m >= 2:
                        act.wait_ge(pool_st[m % 2], 32 * (m // 2))
                    for i in range(NB):
                        n = NB * m + i
                        act.wait_ge(pool_mm, n + 1)
                        nc.scalar.activation(ost[:, m % 2, 2 * i:2 * i + 2].rearrange("p j c -> p (j c)"), pool_ps[:, n % 3, 0:WB],
                                             ACT.Copy, scale=scale[:, m:m + 1]).then_inc(pool_ok, 1)

                act.wait_ge(scale_in, 16)
                for m in range(4):
                    if m + 1 < 4:
                        past(m + 1)
                    gates(2 * m)
                    scaled(m)
                    gates(2 * m + 1)
                act.wait_ge(tail_tr, 1)
                nc.scalar.activation(tails[:], pool_ps[0:STREAMS * HIST, 0], ACT.Copy).then_inc(tail_ok, 1)
                nc.scalar.activation(tailp[:], pool_ps[0:HIST, 1], ACT.Copy).then_inc(tail_ok, 1)

            @block.vector
            def _(dve):
                links = [0]

                def then(*instructions):
                    for ins in instructions:
                        ins.then_inc(chain, 1)
                    links[0] += len(instructions)
                    dve.wait_ge(chain, links[0])

                def windows(m):
                    e, w = ext[:, m % 2], 2 << m
                    dve.wait_ge(past_ok, m + 1)
                    then(nc.vector.memset(e[:, 0:HIST, 0:1], 0.0),
                         nc.vector.tensor_copy(e[:, 0:HIST, CH:NC], hist_ps[:, m * P:m * P + STREAMS * HIST].rearrange("p (b e) -> p e b", b=STREAMS)))
                    flat = lambda buf, a, b: buf[:, a:b].rearrange("p e c -> p (e c)")
                    mean = pooled[:].rearrange("p j c -> p (j c)")
                    src = e
                    for l in range(m):
                        s = 1 << l
                        low = HIST - (w - 2 * s)
                        dst = sums[:, l % 2]
                        then(nc.vector.tensor_tensor(flat(dst, low, EX), flat(src, low, EX), flat(src, low - s, EX - s), ALU.add))
                        src = dst
                    if m:
                        dve.wait_ge(pool_mm, NB * m)
                    then(nc.vector.tensor_tensor(mean, flat(src, HIST, EX), flat(src, HIST - w // 2, EX - w // 2), ALU.add))
                    then(nc.vector.tensor_tensor(pooled[:, :, 0], pooled[:, :, 0], count[:, m], ALU.mult))
                    nc.vector.scalar_tensor_tensor(mean, mean, 1.0 / w, flat(e, HIST, EX), ALU.mult, ALU.subtract).then_inc(pooled_ok, 1)
                    dve.wait_ge(pooled_ok, m + 1)

                def lower_half(i):
                    dve.wait_ge(hi_ok, i + 1)
                    nc.vector.tensor_tensor(g_lo[:, i % 2], v[:, i], g_hi[:, i % 2].bitcast(F32), ALU.subtract).then_inc(lo_ok, 1)

                def gated(i):
                    if i >= 2:
                        dve.wait_ge(out_st[i % 2], 32 * (i // 2))
                    for m in range(4):
                        n = 4 * i + m
                        dve.wait_ge(gate_ok, n + 1)
                        nc.vector.tensor_tensor(out[:, i % 2, m], v[:, i, m], gate[:, i % 2, m], ALU.mult).then_inc(out_ok, 1)
                    dve.wait_ge(out_ok, 4 * (i + 1))
                    src = out[:, i % 2].rearrange("p m (j c) -> p m j c", j=2)[:, :, :, CH:NC]
                    nc.vector.tensor_copy(outs[:, :, 2 * i:2 * i + 2], src).then_inc(outs_ok, 1)

                dve.wait_ge(c_in, 32)
                dve.wait_ge(cnt_ok, 1)
                for i in range(NB):
                    dve.wait_ge(yz_in[i % 2], 32 * (i // 2 + 1))
                    for m in range(4):
                        nc.vector.scalar_tensor_tensor(v[:, i, m], z[:, i % 2, m], skip[:, m:m + 1], y[:, i % 2, m],
                                                       ALU.mult, ALU.add).then_inc(v_ok, 1)
                    if i == 1:
                        dve.wait_ge(whi_ok, 1)
                        nc.vector.tensor_tensor(w_lo[:], raw, w_hi[:].bitcast(F32), ALU.subtract).then_inc(wlo_ok, 1)
                    elif i == 5:
                        lower_half(0)
                        lower_half(1)
                        dve.wait_ge(hist_tr, 1)
                        windows(0)
                for m in range(4):
                    gated(2 * m)
                    if m + 1 < 4:
                        lower_half(2 * m + 2)
                        windows(m + 1)
                    gated(2 * m + 1)
                    if m + 1 < 4:
                        lower_half(2 * m + 3)

            @block.tensor
            def _(pe):
                def gate_products(i):
                    pe.wait_ge(lo_ok, i + 1)
                    for m in range(4):
                        n = 4 * i + m
                        if n >= 4:
                            pe.wait_ge(gate_ok, n - 3)
                        for k in range(4):
                            cols = slice(m * P, (m + 1) * P)
                            ins = product3(nc, acc[:, m, 0:WB], w_hi[:, k, cols], w_lo[:, k, cols], g_hi[:, i % 2, k], g_lo[:, i % 2, k],
                                           k == 0, k == 3)
                        ins.then_inc(mm, 1)

                def pool_products(m):
                    pe.wait_ge(pooled_ok, m + 1)
                    for i in range(NB):
                        n = NB * m + i
                        if n >= 3:
                            pe.wait_ge(pool_ok, n - 2)
                        nc.tensor.matmul(pool_ps[:, n % 3, 0:WB], wp[:, m], pooled[:, 2 * i:2 * i + 2].rearrange("p j c -> p (j c)"),
                                         start=True, stop=True).then_inc(pool_mm, 1)

                pe.wait_ge(ident_ok, 1)
                pe.wait_ge(hist_in, 16)
                for m in range(4):
                    ins = nc.tensor.transpose(hist_ps[:, m * P:m * P + STREAMS * HIST], hist[:, m * P:(m + 1) * P],
                                              ident[0:STREAMS * HIST, 0:STREAMS * HIST])
                ins.then_inc(hist_tr, 1)
                pe.wait_ge(wlo_ok, 1)
                pe.wait_ge(wp_in, 16)
                for m in range(4):
                    gate_products(2 * m)
                    pool_products(m)
                    gate_products(2 * m + 1)
                pe.wait_ge(pool_ok, 4 * NB)
                pe.wait_ge(tail_in, 128)
                for m in range(4):
                    nc.tensor.transpose(pool_ps[0:STREAMS * HIST, 0, m * P:(m + 1) * P], tail[:, m].rearrange("p e b -> p (e b)"), ident[:])
                    ins = nc.tensor.transpose(pool_ps[0:HIST, 1, m * P:(m + 1) * P], tail1[:, m], ident[:])
                ins.then_inc(tail_tr, 1)


def output_projection(nc, outer, io, scr, tag, weight, source, first, target, normed):
    sem = lambda n: outer.new(f"{tag}_{n}")
    with ExitStack() as ctx:
        room = Room(nc, ctx, tag)
        sb, ps = room.sb, room.ps
        ident = sb("ident", [P, P])
        expo = sb("expo", [P, 1])
        raw = sb("raw", [P, 2, D])
        w_hi, w_lo = sb("w_hi", [P, KD, D], F32R), sb("w_lo", [P, KD, D], F32R)
        s = sb("s", [P, 2, KD, P])
        s_hi, s_lo = sb("s_hi", [P, 2, KD, P], F32R), sb("s_lo", [P, 2, KD, P], F32R)
        x = sb("x", [P, 2, D])
        xn = sb("xn", [P, 2, D])
        junk = sb("junk", [P, D])
        stat = sb("stat", [P, 2, 3])
        ht = sb("ht", [P, 2, KD, P])
        acc = ps("acc", [P, 2, 2, 512])
        tr = ps("tr", [P, 2, 2, 512])

        ident0, ident_ok = sem("ident0"), sem("ident")
        raw_in, whi_ok, wlo_ok = [sem(f"raw_in{i}") for i in range(2)], sem("whi"), sem("wlo")
        s_in, x_in = [sem(f"s_in{i}") for i in range(2)], [sem(f"x_in{i}") for i in range(2)]
        shi_ok, slo_ok, mm, x_ok, sumsq, var, rstd, xn_ok, tr_ok, ht_ok = (
            sem(n) for n in ("shi", "slo", "mm", "x", "sumsq", "var", "rstd", "xn", "tr", "ht"))
        x_st, ht_st = [sem(f"x_st{i}") for i in range(2)], [sem(f"ht_st{i}") for i in range(2)]
        LAST = TILES - 1

        with nc.Block() as block:

            @block.sync
            def _(sp):
                w = io[weight][0].rearrange("(k p) n -> k p n", p=P)

                def load_source(t, i):
                    sp.dma_start(s[:, i], source[t]).then_inc(s_in[i], 16)

                def load_x(t, i):
                    sp.dma_start(x[:, i], first(t)).then_inc(x_in[i], 16)

                def store_x(t, i):
                    sp.wait_ge(x_ok, 2 * t + 2)
                    sp.dma_start(target[t], x[:, i]).then_inc(x_st[i], 16)

                def store_normed(t, i):
                    sp.wait_ge(ht_ok, 2 * t + 2)
                    sp.dma_start(normed[t], ht[:, i]).then_inc(ht_st[i], 16)

                def next_loads(t, i, uses):
                    sp.wait_ge(slo_ok, t + 1)
                    load_source(t + 2, i)
                    sp.wait_ge(xn_ok, t + 1)
                    sp.wait_ge(x_st[i], 16 * uses)
                    load_x(t + 2, i)

                load_source(0, 0)
                for k in range(KD):
                    if k >= 2:
                        sp.wait_ge(wlo_ok, k - 1)
                    sp.dma_start(raw[:, k % 2], w[k]).then_inc(raw_in[k % 2], 16)
                    if k == 1:
                        load_source(1, 1)
                        load_x(0, 0)
                        load_x(1, 1)
                store_x(0, 0)
                next_loads(0, 0, 1)
                with sp.Fori(0, 6) as r:
                    for half in range(2):
                        t = 2 * r + 1 + half
                        i = 1 - half
                        store_x(t, i)
                        store_normed(t - 1, 1 - i)
                        next_loads(t, i, r + 1 + half)
                for t in range(13, TILES):
                    store_x(t, t % 2)
                    store_normed(t - 1, (t - 1) % 2)
                    if t + 2 < TILES:
                        next_loads(t, t % 2, t // 2 + 1)
                store_normed(LAST, LAST % 2)
                for i in range(2):
                    sp.wait_ge(x_st[i], 16 * ((TILES + 1 - i) // 2))
                    sp.wait_ge(ht_st[i], 16 * ((TILES + 1 - i) // 2))

            @block.gpsimd
            def _(pool):
                nc.gpsimd.memset(expo[:], -0.5)
                identity_matrix(nc, pool, ident, ident0, ident_ok)
                for t in range(TILES):
                    pool.wait_ge(var, t + 1)
                    nc.gpsimd.tensor_tensor(stat[:, t % 2, 2:3], stat[:, t % 2, 1:2], expo[:], ALU.pow).then_inc(rstd, 1)

            @block.scalar
            def _(act):
                def source_half(t, i, uses):
                    act.wait_ge(s_in[i], 16 * uses)
                    if not isinstance(t, int) or t >= 2:
                        act.wait_ge(mm, t - 1)
                    nc.scalar.activation(s_hi[:, i], s[:, i], ACT.Copy).then_inc(shi_ok, 1)

                def square(t, i):
                    act.wait_ge(x_ok, 2 * t + 2)
                    if not isinstance(t, int) or t >= 1:
                        act.wait_ge(xn_ok, t)
                    nc.scalar.activation(junk[:], x[:, i], ACT.Square, accum_out=stat[:, i, 0:1]).then_inc(sumsq, 1)

                def take_normed(t, i, uses):
                    act.wait_ge(tr_ok, t + 1)
                    if uses is not None:
                        act.wait_ge(ht_st[i], 16 * uses)
                    for a in range(2):
                        nc.scalar.activation(ht[:, i, 4 * a:4 * a + 4].rearrange("p k n -> p (k n)"), tr[:, i, a], ACT.Copy).then_inc(ht_ok, 1)

                source_half(0, 0, 1)
                for k in range(KD):
                    act.wait_ge(raw_in[k % 2], 16 * (k // 2 + 1))
                    nc.scalar.activation(w_hi[:, k], raw[:, k % 2], ACT.Copy).then_inc(whi_ok, 1)
                source_half(1, 1, 1)
                square(0, 0)
                for t in (1, 2):
                    source_half(t + 1, (t + 1) % 2, t // 2 + 1 + t % 2)
                    square(t, t % 2)
                    take_normed(t - 1, (t - 1) % 2, None)
                with act.Fori(0, 6) as r:
                    for half in range(2):
                        t = 2 * r + 3 + half
                        i = 1 - half
                        source_half(t + 1, 1 - i, r + 3)
                        square(t, i)
                        take_normed(t - 1, 1 - i, r + 1)
                source_half(LAST, 0, 9)
                square(LAST - 1, 1)
                take_normed(LAST - 2, 0, 7)
                square(LAST, 0)
                take_normed(LAST - 1, 1, 7)
                take_normed(LAST, 0, 8)

            @block.vector
            def _(dve):
                def source_half(t, i):
                    dve.wait_ge(shi_ok, t + 1)
                    nc.vector.tensor_tensor(s_lo[:, i], s[:, i], s_hi[:, i].bitcast(F32), ALU.subtract).then_inc(slo_ok, 1)

                def residual_and_norm(t, i, uses):
                    dve.wait_ge(mm, t + 1)
                    dve.wait_ge(x_in[i], 16 * uses)
                    for a in range(2):
                        half = x[:, i, a * 512:(a + 1) * 512]
                        nc.vector.tensor_tensor(half, half, acc[:, i, a], ALU.add).then_inc(x_ok, 1)
                    dve.wait_ge(sumsq, t + 1)
                    nc.vector.tensor_scalar(stat[:, i, 1:2], stat[:, i, 0:1], 1.0 / D, EPS, ALU.mult, ALU.add).then_inc(var, 1)
                    dve.wait_ge(rstd, t + 1)
                    if not isinstance(t, int) or t >= 2:
                        dve.wait_ge(tr_ok, t - 1)
                    nc.vector.tensor_scalar(xn[:, i], x[:, i], stat[:, i, 2:3], None, ALU.mult).then_inc(xn_ok, 1)

                source_half(0, 0)
                for k in range(KD):
                    dve.wait_ge(whi_ok, k + 1)
                    nc.vector.tensor_tensor(w_lo[:, k], raw[:, k % 2], w_hi[:, k].bitcast(F32), ALU.subtract).then_inc(wlo_ok, 1)
                source_half(1, 1)
                residual_and_norm(0, 0, 1)
                source_half(2, 0)
                residual_and_norm(1, 1, 1)
                with dve.Fori(0, 7) as r:
                    for half in range(2):
                        t = 2 * r + 2 + half
                        source_half(t + 1, 1 - half)
                        residual_and_norm(t, half, r + 2)
                residual_and_norm(LAST, 0, 9)

            @block.tensor
            def _(pe):
                def multiply(t, i, first_tile=False):
                    pe.wait_ge(slo_ok, t + 1)
                    if not isinstance(t, int) or t >= 2:
                        pe.wait_ge(x_ok, 2 * t - 2)
                    for k in range(KD):
                        if first_tile:
                            pe.wait_ge(wlo_ok, k + 1)
                        for a in range(2):
                            cols = slice(a * 512, (a + 1) * 512)
                            ins = product3(nc, acc[:, i, a], s_hi[:, i, k], s_lo[:, i, k], w_hi[:, k, cols], w_lo[:, k, cols],
                                           k == 0, k == KD - 1)
                    ins.then_inc(mm, 1)

                def turn(t, i):
                    pe.wait_ge(xn_ok, t + 1)
                    if not isinstance(t, int) or t >= 2:
                        pe.wait_ge(ht_ok, 2 * t - 2)
                    for k in range(KD):
                        ins = nc.tensor.transpose(tr[:, i, k // 4, (k % 4) * P:(k % 4 + 1) * P], xn[:, i, k * P:(k + 1) * P], ident[:])
                    ins.then_inc(tr_ok, 1)

                pe.wait_ge(ident_ok, 1)
                multiply(0, 0, True)
                multiply(1, 1)
                turn(0, 0)
                multiply(2, 0)
                turn(1, 1)
                with pe.Fori(0, 7) as r:
                    for half in range(2):
                        t = 2 * r + 3 + half
                        multiply(t, 1 - half)
                        turn(t - 1, half)
                turn(LAST, 0)


def query_projection(nc, outer, io, scr):
    sem = lambda n: outer.new("s6_" + n)
    with ExitStack() as ctx:
        room = Room(nc, ctx, "s6")
        sb, ps = room.sb, room.ps
        g = sb("g", [P, KD])
        raw = sb("raw", [P, 2, D])
        w_hi, w_lo = sb("w_hi", [P, KD, D], F32R), sb("w_lo", [P, KD, D], F32R)
        t_in = sb("t_in", [P, BT, KD, P])
        h = sb("h", [P, 2, 2, BT, KD, P], F32R)
        st = sb("st", [P, 4, BT * P])
        acc = ps("acc", [P, 4, 512])
        g_in, raw_in, whi_ok, wlo_ok = sem("g_in"), [sem(f"raw_in{i}") for i in range(2)], sem("whi"), sem("wlo")
        h_in, hi_ok, lo_ok = [sem(f"h_in{i}") for i in range(BT)], sem("hi"), sem("lo")
        mm, q_ok, q_st = sem("mm"), sem("q"), [sem(f"q_st{i}") for i in range(4)]
        BLOCKS = TILES // BT + 1

        def tiles_of(b):
            return range(BT * b, min(BT * b + BT, TILES))

        with nc.Block() as block:

            @block.sync
            def _(sp):
                w = io["w_q"][0].rearrange("(k p) n -> k p n", p=P)

                def load(t):
                    if t >= BT:
                        sp.wait_ge(lo_ok, t - BT + 1)
                    sp.dma_start(t_in[:, t % BT], scr["h"][t]).then_inc(h_in[t % BT], 16)
                sp.dma_start(g[:], io["g_xattn"][0].rearrange("(k p) -> p k", p=P), allow_slow_non_contiguous=True).then_inc(g_in, 16)
                for t in range(BT):
                    load(t)
                for k in range(KD):
                    if k >= 2:
                        sp.wait_ge(wlo_ok, k - 1)
                    sp.dma_start(raw[:, k % 2], w[k]).then_inc(raw_in[k % 2], 16)
                for t in range(BT, 2 * BT):
                    load(t)
                for b in range(BLOCKS):
                    for m in range(KD):
                        n = b * KD + m
                        sp.wait_ge(q_ok, n + 1)
                        nt = len(tiles_of(b))
                        sp.dma_start(scr["q"][BT * b:BT * b + nt, :, m].rearrange("t p n -> p t n"),
                                     st[:, n % 4, 0:nt * P].rearrange("p (t n) -> p t n", t=nt)).then_inc(q_st[n % 4], 16)
                        if m % 2 and BT * (b + 2) + m // 2 < TILES:
                            load(BT * (b + 2) + m // 2)
                for i in range(4):
                    sp.wait_ge(q_st[i], BLOCKS * KD // 4 * 16)

            @block.scalar
            def _(act):
                def upper_half(t):
                    b, j = divmod(t, BT)
                    act.wait_ge(h_in[t % BT], 16 * (t // BT + 1))
                    if b >= 2:
                        act.wait_ge(mm, (b - 1) * KD)
                    nc.scalar.activation(h[:, b % 2, 0, j], t_in[:, t % BT], ACT.Copy).then_inc(hi_ok, 1)
                act.wait_ge(g_in, 16)
                for t in range(BT):
                    upper_half(t)
                for k in range(KD):
                    act.wait_ge(raw_in[k % 2], 16 * (k // 2 + 1))
                    nc.scalar.activation(w_hi[:, k], raw[:, k % 2], ACT.Copy, scale=g[:, k:k + 1]).then_inc(whi_ok, 1)
                for b in range(BLOCKS):
                    for m in range(KD):
                        n = b * KD + m
                        act.wait_ge(mm, n + 1)
                        if n >= 4:
                            act.wait_ge(q_st[n % 4], 16 * (n // 4))
                        wide = P * len(tiles_of(b))
                        nc.scalar.activation(st[:, n % 4, 0:wide], acc[:, n % 4, 0:wide], ACT.Copy).then_inc(q_ok, 1)
                        if m % 2 == 0 and BT * (b + 1) + m // 2 < TILES:
                            upper_half(BT * (b + 1) + m // 2)

            @block.vector
            def _(dve):
                def lower_half(t):
                    b, j = divmod(t, BT)
                    dve.wait_ge(hi_ok, t + 1)
                    nc.vector.tensor_tensor(h[:, b % 2, 1, j], t_in[:, t % BT], h[:, b % 2, 0, j].bitcast(F32), ALU.subtract).then_inc(lo_ok, 1)
                for t in range(BT):
                    lower_half(t)
                for k in range(KD):
                    dve.wait_ge(whi_ok, k + 1)
                    nc.vector.scalar_tensor_tensor(w_lo[:, k], raw[:, k % 2], g[:, k:k + 1], w_hi[:, k].bitcast(F32),
                                                   ALU.mult, ALU.subtract).then_inc(wlo_ok, 1)
                for t in range(BT, TILES):
                    lower_half(t)

            @block.tensor
            def _(pe):
                for b in range(BLOCKS):
                    nt = len(tiles_of(b))
                    pe.wait_ge(lo_ok, tiles_of(b)[-1] + 1)
                    for ms in [range(0, 4)] * (b == 0) + [(m,) for m in range(4 if b == 0 else 0, KD)]:
                        for k in range(KD):
                            for m in ms:
                                n = b * KD + m
                                if k == 0 and n >= 4:
                                    pe.wait_ge(q_ok, n - 3)
                                if n == 0:
                                    pe.wait_ge(wlo_ok, k + 1)
                                cols = slice(m * P, (m + 1) * P)
                                ins = product3(nc, acc[:, n % 4, 0:nt * P], w_hi[:, k, cols], w_lo[:, k, cols],
                                               h[:, b % 2, 0, 0:nt, k], h[:, b % 2, 1, 0:nt, k], k == 0, k == KD - 1)
                                if k == KD - 1:
                                    ins.then_inc(mm, 1)


def attention(nc, outer, io, scr):
    sem = lambda n: outer.new("s7_" + n)
    with ExitStack() as ctx:
        room = Room(nc, ctx, "s7")
        sb, ps = room.sb, room.ps
        SCALE = float(HD) ** -0.5
        RB = 32
        PB = 2
        NS = 4
        ident = sb("ident", [P, P])
        rawkv = sb("rawkv", [P, 2, 2, D])
        k_hi, k_lo = sb("k_hi", [P, KD, MEM], F32R), sb("k_lo", [P, KD, MEM], F32R)
        v_hi, v_lo = sb("v_hi", [P, 2, D], F32R), sb("v_lo", [P, 2, D], F32R)
        q = sb("q", [P, 2, KD, P])
        q_hi, q_lo = sb("q_hi", [P, 2, KD, P], F32R), sb("q_lo", [P, 2, KD, P], F32R)
        prob = sb("prob", [P, 2, D])
        top, ntop, den, rden = (sb(n, [P, 2, HEADS]) for n in ("top", "ntop", "den", "rden"))
        pt = sb("pt", [P, 2, 2, KD, PB * P], F32R)
        ost = sb("ost", [P, 2, PB * P])
        sq = sb("sq", [P, KD, P])
        sqs = sb("sqs", [P, KD, STREAMS, RB])
        skT = sb("skT", [P, NS, KD, MEM])
        sval = sb("sval", [P, NS, 2, D])
        spt = sb("spt", [P, KD, P])
        sot = sb("sot", [P, KD, STEP, STREAMS])
        srow = sb("srow", [P, 2, 512])
        score = ps("score", [P, 2, 2, 512])
        tr = ps("tr", [P, 2, 512])
        o_ps = ps("o", [P, 2, 512])

        ident0, ident_ok, k_in, v_in, khi_ok, klo_ok = (sem(n) for n in ("ident0", "ident", "k_in", "v_in", "khi", "klo"))
        q_in, qhi_ok, qlo_ok = [sem(f"q_in{i}") for i in range(2)], sem("qhi"), sem("qlo")
        sq_in, zero_ok, sqs_ok, sk_in, sv_in = sem("sq_in"), sem("zero"), sem("sqs"), [sem(f"sk_in{i}") for i in range(2)], [sem(f"sv_in{i}") for i in range(2)]
        sc_mm, top_ok, ntop_ok, exp_ok, rden_ok, prob_ok = (sem(n) for n in ("sc_mm", "top", "ntop", "exp", "rden", "prob"))
        turned, hi_ok, taken, o_mm, o_ok = (sem(n) for n in ("turned", "hi", "taken", "o_mm", "o"))
        o_st, stored = [sem(f"o_st{i}") for i in range(2)], sem("stored")

        tiles = [*range(8), ("streams", 0), *range(8, STEP), ("streams", 1)]
        keys_at = {i + i // 8: divmod(i, 2) for i in range(2 * STREAMS)}

        class Step:
            pass

        steps, waiting, streams_next, turns, outs = [], [], None, 0, 0
        for i in range(len(tiles) + 4):
            s = Step()
            s.i = i
            s.tile = tiles[i] if i < len(tiles) else None
            s.keys, s.keys_turn = keys_at.get(i), turns
            turns += 2 if s.keys is not None else 0
            s.outs, waiting, s.out_n = waiting[:4], waiting[4:], outs
            outs += len(s.outs)
            s.streams, s.streams_n = streams_next, outs
            outs += NS if streams_next is not None else 0
            s.turn = tiles[i - 1] if 0 < i <= len(tiles) else None
            s.turn_n = turns
            turns += 2 if s.turn is not None else 0
            streams_next = s.turn[1] if isinstance(s.turn, tuple) else None
            if isinstance(s.turn, int) and s.turn % PB == PB - 1:
                s_pair = s.turn // PB
                waiting = waiting + [(s_pair, m) for m in range(KD)]
            steps.append(s)
        turn_of = {s.turn: s.turn_n for s in steps if s.turn is not None}
        out_of = {key: s.out_n + k for s in steps for k, key in enumerate(s.outs)}
        streams_of = {s.streams: s.streams_n for s in steps if s.streams is not None}
        keys_turn_of = {s.keys: s.keys_turn for s in steps if s.keys is not None}
        place = {t: i for i, t in enumerate(tiles)}

        with nc.Block() as block:

            @block.sync
            def _(sp):
                sp.dma_start(rawkv[:, 0].rearrange("p t n -> p (t n)"), scr["kT"].rearrange("p k n -> p (k n)")).then_inc(k_in, 16)
                def load_queries(t):
                    if t >= 2:
                        sp.wait_ge(qlo_ok, t - 1)
                    sp.dma_start(q[:, t % 2], scr["q"][t]).then_inc(q_in[t % 2], 16)

                def load_keys(b):
                    if b >= 2:
                        sp.wait_ge(turned, keys_turn_of[b - 2, 1] + 2)
                    else:
                        sp.wait_ge(klo_ok, 2)
                    sp.dma_start(rawkv[:, b % 2], io["cache_mem_k"][0, b].rearrange("(t p) h e -> p t (h e)", p=P)).then_inc(sk_in[b % 2], 16)

                def load_values(half):
                    if half:
                        sp.wait_ge(o_mm, streams_of[0] + NS)
                    for b in range(NS):
                        sp.dma_start(sval[:, b], io["cache_mem_v"][0, NS * half + b].rearrange("(t p) h e -> p t (h e)", p=P)).then_inc(sv_in[half], 16)

                load_queries(0)
                sp.dma_start(rawkv[:, 1], scr["v"]).then_inc(v_in, 16)
                load_queries(1)
                sp.dma_start(sq[:], scr["q"][STEP]).then_inc(sq_in, 16)
                load_keys(0)
                load_keys(1)
                load_values(0)
                for s in steps:
                    if isinstance(s.tile, int) and s.tile + 2 < STEP:
                        load_queries(s.tile + 2)
                    if s.keys is not None and s.keys[1] and s.keys[0] + 2 < STREAMS:
                        load_keys(s.keys[0] + 2)
                    for pair, m in s.outs:
                        n = pair * KD + m
                        sp.wait_ge(o_ok, out_of[pair, m] + 1)
                        sp.dma_start(scr["o"][PB * pair:PB * pair + PB, :, m].rearrange("t p n -> p t n"),
                                     ost[:, n % 2].rearrange("p (t n) -> p t n", t=PB)).then_inc(o_st[n % 2], 16)
                    if s.streams == 0:
                        load_values(1)
                sp.wait_ge(o_ok, streams_of[1] + NS)
                sp.dma_start(scr["o"][STEP].rearrange("p m n -> p (m n)"), sot[:].rearrange("p m j b -> p (m j b)")).then_inc(stored, 16)
                sp.wait_ge(stored, 16)
                for i in range(2):
                    sp.wait_ge(o_st[i], STEP // PB * KD // 2 * 16)

            @block.gpsimd
            def _(pool):
                identity_matrix(nc, pool, ident, ident0, ident_ok)
                nc.gpsimd.memset(sqs[:, :, :, STEP:RB], 0.0).then_inc(zero_ok, 1)

            @block.scalar
            def _(act):
                def query_half(t):
                    act.wait_ge(q_in[t % 2], 16 * (t // 2 + 1))
                    if t >= 2:
                        act.wait_ge(sc_mm, place[t - 2] + 1)
                    nc.scalar.activation(q_hi[:, t % 2], q[:, t % 2], ACT.Copy).then_inc(qhi_ok, 1)

                def exponentials(u, heads):
                    act.wait_ge(ntop_ok, u + 1)
                    if u >= 2:
                        act.wait_ge(turned, turn_of[tiles[u - 2]] + 2)
                    for hd in heads:
                        cols = slice(hd * MEM, (hd + 1) * MEM)
                        nc.scalar.activation(prob[:, u % 2, cols], score[:, u % 2, hd // 2, (hd % 2) * MEM:(hd % 2 + 1) * MEM], ACT.Exp,
                                             bias=ntop[:, u % 2, hd:hd + 1], scale=SCALE,
                                             accum_out=den[:, u % 2, hd:hd + 1]).then_inc(exp_ok, 1)

                def upper_half(t, turn):
                    pair, j = divmod(t, PB)
                    for a in range(2):
                        act.wait_ge(turned, turn + a + 1)
                        if pair >= 2:
                            act.wait_ge(o_mm, out_of[pair - 2, KD - 1] + 1)
                        nc.scalar.activation(pt[:, pair % 2, 0, 4 * a:4 * a + 4, j * P:(j + 1) * P],
                                             tr[:, (turn + a) % 2].rearrange("p (k n) -> p k n", k=4), ACT.Copy).then_inc(hi_ok, 1)

                def output_copy(pair, m):
                    n, use = pair * KD + m, out_of[pair, m]
                    act.wait_ge(o_mm, use + 1)
                    if n >= 2:
                        act.wait_ge(o_st[n % 2], 16 * (n // 2))
                    nc.scalar.activation(ost[:, n % 2], o_ps[:, use % 2, 0:PB * P], ACT.Copy).then_inc(o_ok, 1)

                act.wait_ge(k_in, 16)
                nc.scalar.activation(k_hi[:].rearrange("p k n -> p (k n)"), rawkv[:, 0].rearrange("p t n -> p (t n)"), ACT.Copy).then_inc(khi_ok, 1)
                query_half(0)
                act.wait_ge(v_in, 16)
                nc.scalar.activation(v_hi[:], rawkv[:, 1], ACT.Copy).then_inc(khi_ok, 1)
                query_half(1)
                for s in steps:
                    if s.tile is not None:
                        exponentials(s.i, (0, 1))
                    for pair, m in s.outs[0:2]:
                        output_copy(pair, m)
                    if s.tile is not None:
                        exponentials(s.i, (2, 3))
                    if isinstance(s.turn, int):
                        upper_half(s.turn, s.turn_n)
                    for pair, m in s.outs[2:4]:
                        output_copy(pair, m)
                    if s.streams is not None:
                        for a in range(2):
                            use = s.streams_n + a
                            act.wait_ge(o_mm, use + 1)
                            if s.streams:
                                act.wait_ge(o_mm, streams_of[0] + NS)
                            nc.scalar.activation(srow[:, a], o_ps[:, use % 2], ACT.Copy).then_inc(o_ok, 1)
                        for a in range(2):
                            use = s.streams_n + 2 + a
                            act.wait_ge(o_mm, use + 1)
                            nc.scalar.activation(sot[:, 4 * a:4 * a + 4, :, NS * s.streams:NS * s.streams + NS],
                                                 o_ps[:, use % 2].rearrange("p (m b r) -> p m r b", m=4, r=RB)[:, :, 0:STEP],
                                                 ACT.Copy).then_inc(o_ok, 1)
                    if isinstance(s.tile, int) and s.tile + 2 < STEP:
                        query_half(s.tile + 2)

            @block.vector
            def _(dve):
                def query_half(t):
                    dve.wait_ge(qhi_ok, t + 1)
                    nc.vector.tensor_tensor(q_lo[:, t % 2], q[:, t % 2], q_hi[:, t % 2].bitcast(F32), ALU.subtract).then_inc(qlo_ok, 1)

                def maxima(u):
                    dve.wait_ge(sc_mm, u + 1)
                    if u >= 2:
                        dve.wait_ge(exp_ok, HEADS * (u - 1))
                    nc.vector.reduce_max(top[:, u % 2], score[:, u % 2].rearrange("p a (b n) -> p (a b) n", b=2), AX_X).then_inc(top_ok, 1)
                    dve.wait_ge(top_ok, u + 1)
                    nc.vector.tensor_scalar(ntop[:, u % 2], top[:, u % 2], -SCALE, None, ALU.mult).then_inc(ntop_ok, 1)

                def normalise(u):
                    dve.wait_ge(exp_ok, HEADS * (u + 1))
                    nc.vector.reciprocal(rden[:, u % 2], den[:, u % 2]).then_inc(rden_ok, 1)
                    dve.wait_ge(rden_ok, u + 1)
                    for hd in range(HEADS):
                        cols = prob[:, u % 2, hd * MEM:(hd + 1) * MEM]
                        nc.vector.tensor_scalar(cols, cols, rden[:, u % 2, hd:hd + 1], None, ALU.mult).then_inc(prob_ok, 1)

                def lower_half(t, turn):
                    pair, j = divmod(t, PB)
                    for a in range(2):
                        dve.wait_ge(hi_ok, 2 * t + a + 1)
                        to = lambda half: pt[:, pair % 2, half, 4 * a:4 * a + 4, j * P:(j + 1) * P]
                        nc.vector.tensor_tensor(to(1), tr[:, (turn + a) % 2].rearrange("p (k n) -> p k n", k=4), to(0).bitcast(F32),
                                                ALU.subtract).then_inc(taken, 1)

                dve.wait_ge(khi_ok, 1)
                nc.vector.tensor_tensor(k_lo[:].rearrange("p k n -> p (k n)"), rawkv[:, 0].rearrange("p t n -> p (t n)"),
                                        k_hi[:].rearrange("p k n -> p (k n)").bitcast(F32), ALU.subtract).then_inc(klo_ok, 1)
                query_half(0)
                dve.wait_ge(khi_ok, 2)
                nc.vector.tensor_tensor(v_lo[:], rawkv[:, 1], v_hi[:].bitcast(F32), ALU.subtract).then_inc(klo_ok, 1)
                query_half(1)
                query_next = None
                for s in steps:
                    if s.tile is not None:
                        maxima(s.i)
                    if s.i == 1:
                        dve.wait_ge(sq_in, 16)
                        for b in range(STREAMS):
                            nc.vector.tensor_copy(sqs[:, :, b, 0:STEP], sq[:].rearrange("p k (j b) -> p k j b", b=STREAMS)[:, :, :, b]).then_inc(sqs_ok, 1)
                    if s.keys is not None:
                        b, half = s.keys
                        for a in range(2):
                            c = 2 * half + a
                            dve.wait_ge(turned, s.keys_turn + a + 1)
                            if b >= NS:
                                dve.wait_ge(sc_mm, place["streams", 0] + 1)
                            nc.vector.tensor_copy(skT[:, b % NS, 2 * c:2 * c + 2].rearrange("p k n -> p (k n)"),
                                                  tr[:, (s.keys_turn + a) % 2]).then_inc(taken, 1)
                    if query_next is not None:
                        query_half(query_next)
                    query_next = s.tile + 2 if isinstance(s.tile, int) and s.tile + 2 < STEP else None
                    if s.tile is not None:
                        normalise(s.i)
                    if isinstance(s.turn, int):
                        lower_half(s.turn, s.turn_n)
                    elif s.turn is not None:
                        for a in range(2):
                            dve.wait_ge(turned, s.turn_n + a + 1)
                            if s.turn[1]:
                                dve.wait_ge(o_mm, streams_of[0] + NS)
                            nc.vector.tensor_copy(spt[:, 4 * a:4 * a + 4].rearrange("p k n -> p (k n)"), tr[:, (s.turn_n + a) % 2]).then_inc(taken, 1)

            @block.tensor
            def _(pe):
                def bank_free(turn):
                    if turn >= 2:
                        pe.wait_ge(taken, turn - 1)

                def prompt_scores(t, u):
                    pe.wait_ge(qlo_ok, t + 1)
                    for hd in range(HEADS):
                        for k in (2 * hd, 2 * hd + 1):
                            ins = product3(nc, score[:, u % 2, hd // 2, (hd % 2) * MEM:(hd % 2 + 1) * MEM], q_hi[:, t % 2, k],
                                           q_lo[:, t % 2, k], k_hi[:, k], k_lo[:, k], k % 2 == 0, k % 2 == 1)
                    ins.then_inc(sc_mm, 1)

                def stream_scores(half, u):
                    pe.wait_ge(taken, keys_turn_of[NS * half + NS - 1, 1] + 2)
                    pe.wait_ge(sqs_ok, STREAMS)
                    pe.wait_ge(zero_ok, 1)
                    for b in range(NS):
                        rows = slice(RB * b, RB * b + RB)
                        for hd in range(HEADS):
                            for k in (2 * hd, 2 * hd + 1):
                                ins = nc.tensor.matmul(score[rows, u % 2, hd // 2, (hd % 2) * MEM:(hd % 2 + 1) * MEM],
                                                       sqs[:, k, NS * half + b], skT[:, b, k], start=k % 2 == 0, stop=k % 2 == 1)
                    ins.then_inc(sc_mm, 1)

                def turn_keys(b, half, turn):
                    pe.wait_ge(sk_in[b % 2], 16 * (b // 2 + 1))
                    for a in range(2):
                        c = 2 * half + a
                        bank_free(turn + a)
                        for k in (2 * c, 2 * c + 1):
                            for t in range(2):
                                ins = nc.tensor.transpose(tr[:, (turn + a) % 2, (k % 2) * MEM + t * P:(k % 2) * MEM + (t + 1) * P],
                                                          rawkv[:, b % 2, t, k * P:(k + 1) * P], ident[:])
                        ins.then_inc(turned, 1)

                def turn_probabilities(u, turn):
                    pe.wait_ge(prob_ok, HEADS * (u + 1))
                    for a in range(2):
                        bank_free(turn + a)
                        for k in range(4 * a, 4 * a + 4):
                            ins = nc.tensor.transpose(tr[:, (turn + a) % 2, (k % 4) * P:(k % 4 + 1) * P], prob[:, u % 2, k * P:(k + 1) * P], ident[:])
                        ins.then_inc(turned, 1)

                def outputs(pair, m):
                    use = out_of[pair, m]
                    pe.wait_ge(klo_ok, 2)
                    pe.wait_ge(taken, turn_of[PB * pair + PB - 1] + 2)
                    if use >= 2:
                        pe.wait_ge(o_ok, use - 1)
                    for kt in range(2):
                        cols = slice(m * P, (m + 1) * P)
                        row = (m // 2) * 2 + kt
                        ins = product3(nc, o_ps[:, use % 2, 0:PB * P], v_hi[:, kt, cols], v_lo[:, kt, cols], pt[:, pair % 2, 0, row],
                                       pt[:, pair % 2, 1, row], kt == 0, kt == 1)
                    ins.then_inc(o_mm, 1)

                def stream_outputs(half, use0):
                    pe.wait_ge(taken, turn_of["streams", half] + 2)
                    pe.wait_ge(sv_in[half], 16 * NS)
                    for a in range(2):
                        use = use0 + a
                        pe.wait_ge(o_ok, use - 1)
                        for b in range(NS):
                            for hd in (2 * a, 2 * a + 1):
                                for t in range(2):
                                    ins = nc.tensor.matmul(o_ps[RB * b:RB * b + RB, use % 2, (hd % 2) * HD:(hd % 2 + 1) * HD],
                                                           spt[:, hd * 2 + t, RB * b:RB * b + RB], sval[:, b, t, hd * HD:(hd + 1) * HD],
                                                           start=t == 0, stop=t == 1)
                        ins.then_inc(o_mm, 1)
                    for a in range(2):
                        pe.wait_ge(o_ok, use0 + a + 1)
                        for m in range(4):
                            ins = nc.tensor.transpose(o_ps[:, (use0 + 2 + a) % 2, m * P:(m + 1) * P], srow[:, a, m * P:(m + 1) * P], ident[:])
                        ins.then_inc(o_mm, 1)

                pe.wait_ge(ident_ok, 1)
                pe.wait_ge(klo_ok, 1)
                for s in steps:
                    if s.tile is not None:
                        if s.i >= 2:
                            pe.wait_ge(exp_ok, HEADS * (s.i - 1))
                        if isinstance(s.tile, int):
                            prompt_scores(s.tile, s.i)
                        else:
                            stream_scores(s.tile[1], s.i)
                    if s.keys is not None:
                        turn_keys(*s.keys, s.keys_turn)
                    for pair, m in s.outs[0:2]:
                        outputs(pair, m)
                    if s.turn is not None:
                        turn_probabilities(s.i - 1, s.turn_n)
                    for pair, m in s.outs[2:4]:
                        outputs(pair, m)
                    if s.streams is not None:
                        stream_outputs(s.streams, s.streams_n)


def mlp(nc, outer, io, scr):
    sem = lambda n: outer.new("s9_" + n)
    FC = 256
    FT = FC // P
    CHUNKS = FF // FC
    BM = 3
    WB = BM * P
    GROUP = 9
    J = GROUP // BM
    with ExitStack() as ctx:
        room = Room(nc, ctx, "s9")
        sb, ps = room.sb, room.ps
        g = sb("g", [P, KD])
        g_last = sb("g_last", [P, D])
        expo = sb("expo", [P, 1])
        stat = sb("stat", [P, 3, GROUP])
        xs = sb("xs", [P, GROUP, D])
        h_hi, h_lo = sb("h_hi", [P, GROUP, KD, P], F32R), sb("h_lo", [P, GROUP, KD, P], F32R)
        up_raw, dn_raw = sb("up_raw", [P, KD, FC]), sb("dn_raw", [P, FT, D])
        up_hi, up_lo = sb("up_hi", [P, 2, KD, FC], F32R), sb("up_lo", [P, 2, KD, FC], F32R)
        dn_hi, dn_lo = sb("dn_hi", [P, 2, FT, D], F32R), sb("dn_lo", [P, 2, FT, D], F32R)
        r = sb("r", [P, FT, WB])
        a_hi, a_lo = sb("a_hi", [P, 2, FT, WB], F32R), sb("a_lo", [P, 2, FT, WB], F32R)
        up_ps = ps("up", [P, 4, 512])
        dn_ps = ps("dn", [P, 2, 2, 512])

        g_in, gl_in = sem("g_in"), sem("gl_in")
        h_in, x_in, y_st = ([sem(f"{n}{t}") for t in range(GROUP)] for n in ("h_in", "x_in", "y_st"))
        hhi_ok, hlo_ok = sem("hhi"), sem("hlo")
        up_in, dn_in, uphi_ok, uplo_ok, dnhi_ok, dnlo_ok = (sem(n) for n in ("up_in", "dn_in", "uphi", "uplo", "dnhi", "dnlo"))
        up_mm, relu_ok, sq_ok, ahi_ok, alo_ok, dn_mm, sum_ok = (
            sem(n) for n in ("up_mm", "relu", "sq", "ahi", "alo", "dn_mm", "sum"))
        expo_ok, sumsq, var, rstd, y_ok = sem("expo"), sem("sumsq"), sem("var"), sem("rstd"), sem("y")

        groups = [(0, GROUP), (GROUP, TILES - GROUP)]
        landing = [up_raw[:, 0:4].rearrange("p k f -> p (k f)"), up_raw[:, 4:8].rearrange("p k f -> p (k f)"), dn_raw[:, 0], dn_raw[:, 1]]
        land_in = [sem(f"land_in{i}") for i in range(4)]
        tiles_of = [range(j * BM, (j + 1) * BM) for j in range(J)]
        early_norms = (tiles_of[0], range(0, 2 * BM))
        h_block = lambda j: range(j * BM, min((j + 1) * BM, groups[1][1]))

        class Place:

            def __init__(self, gi, c, odd, j):
                self.t0, self.nt = groups[gi]
                self.sizes = [min(BM, self.nt - BM * i) for i in range(J)]
                self.gi, self.c, self.odd, self.j = gi, c, odd, j
                self.chunk = gi * CHUNKS + c
                self.block = self.chunk * J + j
                self.side = (odd * J + j) % 2
                self.before = sum(self.sizes[:j])
                self.tile = gi * CHUNKS * GROUP + c * self.nt + self.before
                self.size = self.sizes[j]
                self.wide = self.size * P
                self.early = gi == 0 and isinstance(c, int) and c * J + j < 2

            def back(self, n):
                gi, c, odd, j = self.gi, self.c, self.odd, self.j - n
                while j < 0:
                    c, odd, j = c - 1, 1 - odd, j + J
                if isinstance(c, int) and c < 0:
                    gi, c = gi - 1, c + CHUNKS
                return Place(gi, c, odd, j)

            def tiles_two_blocks_ago(self):
                p = self.back(2)
                return p.tile + p.size

        def over_chunks(eng, gi, body):
            for c in (0, 1):
                body(gi, c, c)
            with eng.Fori(1, CHUNKS // 2 - 1) as pair:
                for odd in range(2):
                    body(gi, 2 * pair + odd, odd)
            for c in (CHUNKS - 2, CHUNKS - 1):
                body(gi, c, c % 2)

        with nc.Block() as block:

            @block.sync
            def _(sp):
                up = io["w_up"][0].rearrange("(k p) (c f) -> c p k f", p=P, f=FC)
                down = io["w_down"][0].rearrange("(c t p) n -> c p t n", p=P, t=FT)
                yp = io["y_prompt"][0].rearrange("(c j) d -> j c d", j=STEP)
                ys = io["y_sample"].rearrange("b j d -> j b d")
                sp.dma_start(g[:], io["g_mlp"][0].rearrange("(k p) -> p k", p=P), allow_slow_non_contiguous=True).then_inc(g_in, 16)
                sp.dma_start(up_raw[:], up[0]).then_inc(up_in, 16)
                sp.dma_start(dn_raw[:], down[0]).then_inc(dn_in, 16)
                sp.dma_start(g_last[:], io["g_final"].partition_broadcast(P)).then_inc(gl_in, 16)
                def load_weights(gi, c):
                    n = gi * CHUNKS + c
                    sp.wait_ge(uplo_ok, KD * n)
                    sp.dma_start(up_raw[:], up[c]).then_inc(up_in, 16)
                    sp.wait_ge(dnlo_ok, FT * n)
                    sp.dma_start(dn_raw[:], down[c]).then_inc(dn_in, 16)

                def store_rows(gi, tiles):
                    t0 = groups[gi][0]
                    for t in tiles:
                        sp.wait_ge(y_ok, t0 + t + 1)
                        sp.dma_start(yp[t0 + t] if t0 + t < STEP else ys, xs[:, t]).then_inc(y_st[t], 16)

                def load_rows(gi, tiles):
                    for t in tiles:
                        if gi:
                            sp.wait_ge(y_st[t], 16)
                        else:
                            sp.wait_ge(hlo_ok, t + 1)
                        sp.dma_start(xs[:, t], scr["x2"][groups[gi][0] + t]).then_inc(x_in[t], 16)

                for t in range(GROUP):
                    sp.dma_start(xs[:, t].rearrange("p (k n) -> p k n", k=KD), scr["h2"][t]).then_inc(h_in[t], 16)
                load_rows(0, range(GROUP))
                with sp.Fori(1, CHUNKS) as c:
                    load_weights(0, c)
                load_weights(1, 0)
                for i in range(groups[1][1]):
                    if i < 4:
                        sp.wait_ge(*((uplo_ok, KD * (CHUNKS + 1)) if i < 2 else (dnlo_ok, FT * (CHUNKS + 1))))
                    else:
                        sp.wait_ge(hlo_ok, GROUP + i - 3)
                    sp.dma_start(landing[i % 4], scr["h2"][GROUP + i].rearrange("p k n -> p (k n)")).then_inc(land_in[i % 4], 16)
                store_rows(0, tiles_of[0])
                load_rows(1, tiles_of[0])
                sp.wait_ge(hlo_ok, TILES)
                sp.wait_ge(uplo_ok, KD * (CHUNKS + 1))
                sp.dma_start(up_raw[:], up[1]).then_inc(up_in, 16)
                store_rows(0, tiles_of[1])
                load_rows(1, tiles_of[1])
                sp.wait_ge(dnlo_ok, FT * (CHUNKS + 1))
                sp.dma_start(dn_raw[:], down[1]).then_inc(dn_in, 16)
                store_rows(0, tiles_of[2])
                load_rows(1, h_block(2))
                with sp.Fori(2, CHUNKS) as c:
                    load_weights(1, c)
                store_rows(1, range(groups[1][1]))
                for t in range(GROUP):
                    sp.wait_ge(y_st[t], 32 if t < groups[1][1] else 16)

            @block.gpsimd
            def _(pool):
                nc.gpsimd.memset(expo[:], -0.5).then_inc(expo_ok, 1)
                pool.wait_ge(expo_ok, 1)
                for t0, nt in groups:
                    for t in range(nt):
                        pool.wait_ge(var, t0 + t + 1)
                        nc.gpsimd.tensor_tensor(stat[:, 2, t:t + 1], stat[:, 1, t:t + 1], expo[:], ALU.pow).then_inc(rstd, 1)

            @block.scalar
            def _(act):
                def split_up(gi, c, odd):
                    n = gi * CHUNKS + c
                    act.wait_ge(up_in, 16 * (n + 1))
                    if not isinstance(n, int) or n >= 2:
                        act.wait_ge(up_mm, FT * J * (n - 1))
                    for k in range(KD):
                        nc.scalar.activation(up_hi[:, odd, k], up_raw[:, k], ACT.Copy, scale=g[:, k:k + 1]).then_inc(uphi_ok, 1)

                def split_down(gi, c, odd):
                    n = gi * CHUNKS + c
                    act.wait_ge(dn_in, 16 * (n + 1))
                    if not isinstance(n, int) or n >= 2:
                        before = n * GROUP if gi == 0 else CHUNKS * GROUP + c * groups[1][1]
                        act.wait_ge(dn_mm, before - groups[gi][1] if not isinstance(c, int) or c >= 1 else before - GROUP)
                    for k in range(FT):
                        nc.scalar.activation(dn_hi[:, odd, k], dn_raw[:, k], ACT.Copy).then_inc(dnhi_ok, 1)

                def hidden(at):
                    for f in range(FT):
                        act.wait_ge(up_mm, FT * at.block + f + 1)
                        if not isinstance(at.block, int) or at.block >= 1:
                            act.wait_ge(alo_ok, FT * at.block + f - 1)
                        nc.scalar.activation(r[:, f, 0:at.wide], up_ps[:, 2 * at.side + f, 0:at.wide], ACT.Relu).then_inc(relu_ok, 1)
                    if at.gi or not at.early:
                        act.wait_ge(dn_mm, at.tiles_two_blocks_ago())
                    for f in range(FT):
                        act.wait_ge(sq_ok, FT * at.block + f + 1)
                        nc.scalar.activation(a_hi[:, at.side, f, 0:at.wide], r[:, f, 0:at.wide], ACT.Copy).then_inc(ahi_ok, 1)

                def landed_halves(tiles):
                    for i in tiles:
                        act.wait_ge(land_in[i % 4], 16 * (i // 4 + 1))
                        nc.scalar.activation(h_hi[:, i].rearrange("p k n -> p (k n)"), landing[i % 4], ACT.Copy).then_inc(hhi_ok, 1)

                def squares(gi, tiles):
                    t0, nt = groups[gi]
                    for t in tiles:
                        act.wait_ge(sum_ok, gi * CHUNKS * GROUP + (CHUNKS - 1) * nt + t + 1)
                        if t0 + t:
                            act.wait_ge(sumsq, t0 + t)
                        nc.scalar.activation(h_hi[:, GROUP - 1].rearrange("p k n -> p (k n)"), xs[:, t], ACT.Square,
                                             accum_out=stat[:, 0, t:t + 1]).then_inc(sumsq, 1)

                def chunk(gi, c, odd):
                    hidden(Place(gi, c, odd, 0))
                    switch = gi == 1 and isinstance(c, int) and c == 0
                    if switch:
                        squares(0, tiles_of[1])
                    if isinstance(c, int) and c == CHUNKS - 1:
                        if gi == 0:
                            split_up(1, 0, 0)
                            split_down(1, 0, 0)
                        hidden(Place(gi, c, odd, 1))
                        if gi == 0:
                            landed_halves(h_block(0))
                        hidden(Place(gi, c, odd, 2))
                        if gi == 0:
                            landed_halves((*h_block(1), *h_block(2)))
                        squares(gi, early_norms[gi])
                    else:
                        split_up(gi, c + 1, 1 - odd)
                        hidden(Place(gi, c, odd, 1))
                        if switch:
                            squares(0, tiles_of[2])
                        split_down(gi, c + 1, 1 - odd)
                        hidden(Place(gi, c, odd, 2))

                act.wait_ge(g_in, 16)
                split_up(0, 0, 0)
                for t in range(GROUP):
                    act.wait_ge(h_in[t], 16)
                    nc.scalar.activation(h_hi[:, t].rearrange("p k n -> p (k n)"), xs[:, t], ACT.Copy).then_inc(hhi_ok, 1)
                split_down(0, 0, 0)
                over_chunks(act, 0, chunk)
                over_chunks(act, 1, chunk)
                squares(1, range(2 * BM, groups[1][1]))

            @block.vector
            def _(dve):
                def split_up(gi, c, odd):
                    n = gi * CHUNKS + c
                    for k in range(KD):
                        dve.wait_ge(uphi_ok, KD * n + k + 1)
                        nc.vector.scalar_tensor_tensor(up_lo[:, odd, k], up_raw[:, k], g[:, k:k + 1], up_hi[:, odd, k].bitcast(F32),
                                                       ALU.mult, ALU.subtract).then_inc(uplo_ok, 1)

                def split_down(gi, c, odd):
                    n = gi * CHUNKS + c
                    for k in range(FT):
                        dve.wait_ge(dnhi_ok, FT * n + k + 1)
                        nc.vector.tensor_tensor(dn_lo[:, odd, k], dn_raw[:, k], dn_hi[:, odd, k].bitcast(F32), ALU.subtract).then_inc(dnlo_ok, 1)

                def hidden(at):
                    for f in range(FT):
                        dve.wait_ge(relu_ok, FT * at.block + f + 1)
                        rf = r[:, f, 0:at.wide]
                        nc.vector.scalar_tensor_tensor(rf, up_ps[:, 2 * at.side + f, 0:at.wide], 0.0, rf, ALU.max, ALU.mult).then_inc(sq_ok, 1)
                    for f in range(FT):
                        dve.wait_ge(ahi_ok, FT * at.block + f + 1)
                        nc.vector.tensor_tensor(a_lo[:, at.side, f, 0:at.wide], r[:, f, 0:at.wide], a_hi[:, at.side, f, 0:at.wide].bitcast(F32),
                                                ALU.subtract).then_inc(alo_ok, 1)

                def sums(at):
                    for i in range(at.size):
                        t = at.before + i
                        dve.wait_ge(dn_mm, at.tile + i + 1)
                        if isinstance(at.c, int) and at.c == 0:
                            dve.wait_ge(x_in[t], 16 * (at.gi + 1))
                        else:
                            dve.wait_ge(sum_ok, at.tile + i + 1 - at.nt)
                        bank = (at.odd * at.nt + t) % 2
                        nc.vector.tensor_tensor(xs[:, t], xs[:, t], dn_ps[:, bank].rearrange("p a n -> p (a n)"), ALU.add).then_inc(sum_ok, 1)

                def landed_halves(tiles):
                    for i in tiles:
                        dve.wait_ge(hhi_ok, GROUP + i + 1)
                        nc.vector.tensor_tensor(h_lo[:, i].rearrange("p k n -> p (k n)"), landing[i % 4],
                                                h_hi[:, i].rearrange("p k n -> p (k n)").bitcast(F32), ALU.subtract).then_inc(hlo_ok, 1)

                def norms(gi, tiles):
                    t0 = groups[gi][0]
                    for t in tiles:
                        dve.wait_ge(sumsq, t0 + t + 1)
                        nc.vector.tensor_scalar(stat[:, 1, t:t + 1], stat[:, 0, t:t + 1], 1.0 / D, EPS, ALU.mult, ALU.add).then_inc(var, 1)
                        dve.wait_ge(rstd, t0 + t + 1)
                        nc.vector.scalar_tensor_tensor(xs[:, t], xs[:, t], stat[:, 2, t:t + 1], g_last[:], ALU.mult, ALU.mult).then_inc(y_ok, 1)

                def chunk(gi, c, odd):
                    hidden(Place(gi, c, odd, 0))
                    if gi == 1 or not isinstance(c, int) or c > 0:
                        sums(Place(gi, c, odd, 0).back(1))
                    switch = gi == 1 and isinstance(c, int) and c == 0
                    if switch:
                        norms(0, tiles_of[1])
                    if isinstance(c, int) and c == CHUNKS - 1:
                        if gi == 0:
                            split_up(1, 0, 0)
                            split_down(1, 0, 0)
                        hidden(Place(gi, c, odd, 1))
                        sums(Place(gi, c, odd, 0))
                        if gi == 0:
                            landed_halves(h_block(0))
                        hidden(Place(gi, c, odd, 2))
                        sums(Place(gi, c, odd, 1))
                        if gi == 0:
                            landed_halves((*h_block(1), *h_block(2)))
                        norms(gi, early_norms[gi])
                    else:
                        split_up(gi, c + 1, 1 - odd)
                        hidden(Place(gi, c, odd, 1))
                        sums(Place(gi, c, odd, 0))
                        if switch:
                            norms(0, tiles_of[2])
                        split_down(gi, c + 1, 1 - odd)
                        hidden(Place(gi, c, odd, 2))
                        sums(Place(gi, c, odd, 1))

                dve.wait_ge(g_in, 16)
                split_up(0, 0, 0)
                for t in range(GROUP):
                    dve.wait_ge(hhi_ok, t + 1)
                    nc.vector.tensor_tensor(h_lo[:, t].rearrange("p k n -> p (k n)"), xs[:, t],
                                            h_hi[:, t].rearrange("p k n -> p (k n)").bitcast(F32), ALU.subtract).then_inc(hlo_ok, 1)
                split_down(0, 0, 0)
                dve.wait_ge(gl_in, 16)
                over_chunks(dve, 0, chunk)
                over_chunks(dve, 1, chunk)
                sums(Place(1, CHUNKS - 1, 1, J - 1))
                norms(1, range(2 * BM, groups[1][1]))

            @block.tensor
            def _(pe):
                def up(at):
                    if at.j == 0:
                        pe.wait_ge(uplo_ok, KD * (at.chunk + 1))
                    if isinstance(at.c, int) and at.c == 0:
                        pe.wait_ge(hlo_ok, at.t0 + at.before + at.size)
                    if not isinstance(at.block, int) or at.block >= 2:
                        pe.wait_ge(sq_ok, FT * (at.block - 1))
                    tiles = slice(at.before, at.before + at.size)
                    for f in range(FT):
                        for k in range(KD):
                            cols = slice(f * P, (f + 1) * P)
                            ins = product3(nc, up_ps[:, 2 * at.side + f, 0:at.wide], up_hi[:, at.odd, k, cols], up_lo[:, at.odd, k, cols],
                                           h_hi[:, tiles, k], h_lo[:, tiles, k], k == 0, k == KD - 1)
                        ins.then_inc(up_mm, 1)

                def down(at):
                    if at.j == 0:
                        pe.wait_ge(dnlo_ok, FT * (at.chunk + 1))
                    pe.wait_ge(alo_ok, FT * (at.block + 1))
                    for i in range(at.size):
                        bank = (at.odd * at.nt + at.before + i) % 2
                        if not isinstance(at.tile, int) or at.tile + i >= 2:
                            pe.wait_ge(sum_ok, at.tile + i - 1)
                        rows = slice(i * P, (i + 1) * P)
                        for a in range(2):
                            cols = slice(a * 512, (a + 1) * 512)
                            for f in range(FT):
                                ins = product3(nc, dn_ps[:, bank, a], a_hi[:, at.side, f, rows], a_lo[:, at.side, f, rows],
                                               dn_hi[:, at.odd, f, cols], dn_lo[:, at.odd, f, cols], f == 0, f == FT - 1)
                        ins.then_inc(dn_mm, 1)

                def chunk(gi, c, odd):
                    for j in range(J):
                        at = Place(gi, c, odd, j)
                        up(at)
                        if gi == 1 or not isinstance(c, int) or c > 0 or j > 0:
                            down(at.back(1))

                over_chunks(pe, 0, chunk)
                over_chunks(pe, 1, chunk)
                down(Place(1, CHUNKS - 1, 1, J - 1))


def program(nc, io):
    with Semaphores(nc) as outer:
        scr = {
            "kT": nc.dram_tensor("scr_kT", (P, KD, MEM), F32).ap(),
            "v": nc.dram_tensor("scr_v", (P, 2, D), F32).ap(),
            "injT": nc.dram_tensor("scr_injT", (P, PAIRS, 4, P), F32).ap(),
            "turn": nc.dram_tensor("scr_turn", (P, 3, PAIRS), F32).ap(),
            "outm": nc.dram_tensor("scr_outm", (P, 2, PAIRS, STEP + 1, SG), F32).ap(),
            "taps": nc.dram_tensor("scr_taps", (SG, GROUPS, STEP, SG), F32).ap(),
        }
        scr["pow16"] = nc.dram_tensor("scr_pow16", (P, 2, PAIRS), F32).ap()
        scr["z"] = nc.dram_tensor("scr_z", (KD, P, STEP, NC), F32).ap()
        scr["y"] = nc.dram_tensor("scr_y", (4, P, STEP, NC), F32).ap()
        scr["c"] = nc.dram_tensor("scr_c", (TILES, P, KD, P), F32).ap()
        with nc.sbuf_tensor("phase", [P, 2, PAIRS, CH], F32) as phase:
            memory_and_tables(nc, outer, io, scr, phase)
            first_input_projection(nc, outer, io, scr)
            mixers(nc, outer, io, scr, phase)
        for name in ("h", "q", "o", "h2"):
            scr[name] = nc.dram_tensor("scr_" + name, (TILES, P, KD, P), F32).ap()
        for name in ("x1", "x2"):
            scr[name] = nc.dram_tensor("scr_" + name, (TILES, P, D), F32).ap()
        xp, xs = io["x_prompt"][0].rearrange("(c j) d -> j c d", j=STEP), io["x_sample"].rearrange("b j d -> j b d")
        mixer_outputs(nc, outer, io, scr)
        outer.clear()
        output_projection(nc, outer, io, scr, "s5", "w_out", scr["c"], lambda t: xs if isinstance(t, int) and t == STEP else xp[t],
                          scr["x1"], scr["h"])
        query_projection(nc, outer, io, scr)
        attention(nc, outer, io, scr)
        outer.clear()
        output_projection(nc, outer, io, scr, "s8", "w_o", scr["o"], lambda t: scr["x1"][t], scr["x2"], scr["h2"])
        mlp(nc, outer, io, scr)


_INS = ["x_prompt", "x_sample", "cache_mem_k", "cache_mem_v", "state_pool", "state_ssm_re", "state_ssm_im", "mem_prompt",
        "g_mix", "w_in", "w_pool", "pool_scale", "ssm_a_re", "ssm_a_im", "ssm_b_re", "ssm_b_im", "ssm_c_re", "ssm_c_im",
        "ssm_d", "ssm_log_dt", "w_glu", "b_glu", "w_out", "g_xattn", "g_mem", "w_q", "w_k", "w_v", "w_o", "g_mlp",
        "w_up", "w_down", "g_final"]
_OUTS = {
    "y_prompt": (1, SEQ, D), "y_sample": (STREAMS, STEP, D), "new_mem_k": (1, 1, MEM, HEADS, HD), "new_mem_v": (1, 1, MEM, HEADS, HD),
    "new_pool_p": (1, 1, HIST, DP), "new_ssm_re_p": (1, 1, GROUPS, SS), "new_ssm_im_p": (1, 1, GROUPS, SS),
    "new_pool_s": (1, STREAMS, HIST, DP), "new_ssm_re_s": (1, STREAMS, GROUPS, SS), "new_ssm_im_s": (1, STREAMS, GROUPS, SS),
}


def kernel(**inputs):
    import numpy as np
    import concourse.bacc as bacc
    from concourse.bass_utils import run_bass_kernel_spmd

    nc = bacc.Bacc("TRN2", target_bir_lowering=False, num_devices=1)
    arrays, io = {}, {}
    for name in _INS:
        a = np.ascontiguousarray(inputs[name])
        arrays[f"in_{name}_dram"] = a
        io[name] = nc.dram_tensor(f"in_{name}_dram", a.shape, mybir.dt.from_np(a.dtype), kind="ExternalInput").ap()
    for name, shape in _OUTS.items():
        io[name] = nc.dram_tensor(f"out_{name}_dram", shape, F32, kind="ExternalOutput").ap()
    program(nc, io)
    got = run_bass_kernel_spmd(nc, [arrays], core_ids=[0]).results[0]
    return tuple(got[f"out_{name}_dram"] for name in _OUTS)
```
